# Optimizing a Trainium2 kernel written in Bass

```python
import math, functools
import jax, jax.numpy as jnp
from jax import lax
import numpy as np

D_MODEL = 1024
BATCH = 1
SEQ = 128
DEPTH = 2
DEC_BATCH = 1
DEC_SEQ = 512
PAST_LEN = 128

GRID_W = 64
N_EVEN = (DEPTH + 1) // 2
N_ODD = DEPTH // 2
D_MIX = D_MODEL
D_A = D_MIX // 2
H_A = 4
DH_A = D_A // H_A
CHUNK = 128
D_RG = D_MIX // 2
H_RG = 8
BLK_RG = D_RG // H_RG
CONV_W = 4
RG_C = 8.0
HEAD_DIM = 64
N_HEADS = D_MIX // HEAD_DIM
N_KV = 4
GQA = N_HEADS // N_KV
WINDOW = 128
QBLK = 128
ROPE_BASE = 10000.0
D_FF = 4 * D_MODEL
N_MOD = 6
EPS = 1e-6
NEG_INF = -1e30

kernel_name = 'hybrid_dit_gmlp_rglru_swa_step'

def rmsnorm(x, g):
    xf = x.astype(jnp.float32)
    y = xf * lax.rsqrt(jnp.mean(xf * xf, axis=-1, keepdims=True) + EPS)
    return (y * g.astype(jnp.float32)).astype(x.dtype)

def modulate(x, shift, scale):
    return x * (1 + scale) + shift

def ada_params(cvec, w_mod, b_mod):
    m = jax.nn.silu(cvec) @ w_mod + b_mod
    return jnp.split(m[:, None, :], N_MOD, axis=-1)

def chunk_gmlp(u, v, g, ws, bs):
    B, T, _ = u.shape
    u = jax.nn.gelu(u)
    v = rmsnorm(jax.nn.gelu(v), g)
    vr = v.reshape(B, T // CHUNK, CHUNK, H_A, DH_A)
    mixed = jnp.einsum('hpq,bnqhd->bnphd', ws, vr) + bs.T[None, None, :, :, None]
    return u * mixed.reshape(B, T, D_A)

def dwconv(x, w, b, reverse):
    T = x.shape[1]
    pad = (0, CONV_W - 1) if reverse else (CONV_W - 1, 0)
    xp = jnp.pad(x, ((0, 0), pad, (0, 0)))
    out = b
    for k in range(CONV_W):
        out = out + xp[:, k:k + T] * w[k]
    return out

def _linear_combine(e1, e2):
    a1, b1 = e1
    a2, b2 = e2
    return a1 * a2, a2 * b1 + b2

def rglru_direction(xc, wa, ba, wi, bi, lam, h0, reverse):
    B, T, _ = xc.shape
    xf = xc.astype(jnp.float32)
    xb = xf.reshape(B, T, H_RG, BLK_RG)
    r = jax.nn.sigmoid(jnp.einsum('bthi,hij->bthj', xb, wa.astype(jnp.float32)).reshape(B, T, D_RG) + ba.astype(jnp.float32))
    ig = jax.nn.sigmoid(jnp.einsum('bthi,hij->bthj', xb, wi.astype(jnp.float32)).reshape(B, T, D_RG) + bi.astype(jnp.float32))
    log_a = RG_C * r * jax.nn.log_sigmoid(lam.astype(jnp.float32))
    a = jnp.exp(log_a)
    bterm = jnp.sqrt(-jnp.expm1(2.0 * log_a)) * (ig * xf)
    h0 = h0.astype(jnp.float32)
    if reverse:
        bterm = bterm.at[:, -1].add(a[:, -1] * h0)
    else:
        bterm = bterm.at[:, 0].add(a[:, 0] * h0)
    _, h = lax.associative_scan(_linear_combine, (a, bterm), reverse=reverse, axis=1)
    final = h[:, 0] if reverse else h[:, -1]
    return h, final

def rglru_mixer(xr, gate, h0, conv_w, conv_b, wa, ba, wi, bi, lam):
    hs, finals = [], []
    for d in range(2):
        xc = dwconv(xr, conv_w[d], conv_b[d], reverse=(d == 1))
        h, fin = rglru_direction(xc, wa[d], ba[d], wi[d], bi[d], lam[d], h0[:, d], reverse=(d == 1))
        hs.append(h)
        finals.append(fin)
    y = (hs[0] + hs[1]).astype(xr.dtype) * jax.nn.gelu(gate)
    return y, jnp.stack(finals, axis=1).astype(xr.dtype)

def even_mixer(h, h0, w_in, w_out, gm_g, gm_ws, gm_bs, conv_w, conv_b, wa, ba, wi, bi, lam):
    u, v, gate, xr = jnp.split(h @ w_in, [D_A, 2 * D_A, 2 * D_A + D_RG], axis=-1)
    ya = chunk_gmlp(u, v, gm_g, gm_ws, gm_bs)
    yb, fin = rglru_mixer(xr, gate, h0, conv_w, conv_b, wa, ba, wi, bi, lam)
    return jnp.concatenate([ya, yb], axis=-1) @ w_out, fin

def split_qkv(h, w_qkv):
    B, T, _ = h.shape
    qkv = h @ w_qkv
    kv_w = N_KV * HEAD_DIM
    q = qkv[..., :D_MIX].reshape(B, T, N_HEADS, HEAD_DIM)
    k = qkv[..., D_MIX:D_MIX + kv_w].reshape(B, T, N_KV, HEAD_DIM)
    v = qkv[..., D_MIX + kv_w:].reshape(B, T, N_KV, HEAD_DIM)
    return q, k, v

def rope_2d(x):
    T = x.shape[1]
    rows = T // GRID_W
    row = jnp.repeat(jnp.arange(rows), GRID_W, total_repeat_length=T)
    col = jnp.tile(jnp.arange(GRID_W), rows)
    nf = HEAD_DIM // 4
    inv = ROPE_BASE ** (-jnp.arange(nf, dtype=jnp.float32) / nf)

    def rot(xh, pos):
        ang = pos.astype(jnp.float32)[:, None] * inv[None, :]
        cos = jnp.cos(ang)[None, :, None, :]
        sin = jnp.sin(ang)[None, :, None, :]
        x1 = xh[..., :nf].astype(jnp.float32)
        x2 = xh[..., nf:].astype(jnp.float32)
        return jnp.concatenate([x1 * cos - x2 * sin, x2 * cos + x1 * sin], axis=-1)

    half = HEAD_DIM // 2
    out = jnp.concatenate([rot(x[..., :half], row), rot(x[..., half:], col)], axis=-1)
    return out.astype(x.dtype)

def context_attention(q, k, v, sink):
    B, T = q.shape[:2]
    qg = q.reshape(B, T, N_KV, GQA, HEAD_DIM)
    s = jnp.einsum('btkgd,bskd->bkgts', qg, k).astype(jnp.float32) * (HEAD_DIM ** -0.5)
    sk = jnp.broadcast_to(sink.astype(jnp.float32).reshape(1, N_KV, GQA, 1, 1), s.shape[:-1] + (1,))
    p = jax.nn.softmax(jnp.concatenate([s, sk], axis=-1), axis=-1)[..., :-1]
    o = jnp.einsum('bkgts,bskd->btkgd', p.astype(v.dtype), v)
    return o.reshape(B, T, D_MIX)

def latent_attention(q, k, v, kc, vc, sink):
    B, T = q.shape[:2]
    nb = T // QBLK
    P = kc.shape[1]
    L = 3 * QBLK
    qb = q.reshape(B, nb, QBLK, N_KV, GQA, HEAD_DIM)

    def band(t):
        tp = jnp.pad(t, ((0, 0), (QBLK, QBLK), (0, 0), (0, 0))).reshape(B, nb + 2, QBLK, N_KV, HEAD_DIM)
        return jnp.concatenate([tp[:, :-2], tp[:, 1:-1], tp[:, 2:]], axis=2)

    kw, vw = band(k), band(v)
    blk = jnp.arange(nb)[:, None, None]
    qpos = blk * QBLK + jnp.arange(QBLK)[None, :, None]
    kpos = (blk - 1) * QBLK + jnp.arange(L)[None, None, :]
    valid = (jnp.abs(kpos - qpos) <= WINDOW) & (kpos >= 0) & (kpos < T)
    scale = HEAD_DIM ** -0.5
    s_loc = jnp.einsum('bnqkgd,bnmkd->bnkgqm', qb, kw).astype(jnp.float32) * scale
    s_loc = jnp.where(valid[None, :, None, None], s_loc, NEG_INF)
    s_ctx = jnp.einsum('bnqkgd,bskd->bnkgqs', qb, kc).astype(jnp.float32) * scale
    sk = jnp.broadcast_to(sink.astype(jnp.float32).reshape(1, 1, N_KV, GQA, 1, 1), s_loc.shape[:-1] + (1,))
    p = jax.nn.softmax(jnp.concatenate([s_loc, s_ctx, sk], axis=-1), axis=-1)
    p_loc = p[..., :L].astype(v.dtype)
    p_ctx = p[..., L:L + P].astype(vc.dtype)
    o = jnp.einsum('bnkgqm,bnmkd->bnqkgd', p_loc, vw) + jnp.einsum('bnkgqs,bskd->bnqkgd', p_ctx, vc)
    return o.reshape(B, T, D_MIX)

def odd_mixer_context(h, w_qkv, w_out, sink):
    q, k, v = split_qkv(h, w_qkv)
    return context_attention(q, k, v, sink) @ w_out, k, v

def odd_mixer_latent(h, kc, vc, w_qkv, w_out, sink):
    q, k, v = split_qkv(h, w_qkv)
    q = rope_2d(q)
    k = rope_2d(k)
    return latent_attention(q, k, v, kc, vc, sink) @ w_out

def sq_relu_mlp(h, w1, w2):
    return jnp.square(jax.nn.relu(h @ w1)) @ w2

def setup_inputs(seed: int = 0) -> dict:
    key = jax.random.key(seed)
    ks = jax.random.split(key, 40)

    def nrm(k, shape, scale=1.0):
        return jax.random.normal(k, shape, jnp.float32) * scale

    def gain(k, shape):
        return 1.0 + 0.05 * jax.random.normal(k, shape, jnp.float32)

    a8 = jax.random.uniform(ks[26], (N_EVEN, 2, D_RG), jnp.float32, 0.9, 0.999)
    a = a8 ** (1.0 / RG_C)
    rg_lambda = jnp.log(a) - jnp.log1p(-a)
    return {
        'x_prompt': nrm(ks[0], (BATCH, SEQ, D_MODEL)),
        'x_sample': nrm(ks[1], (DEC_BATCH, DEC_SEQ, D_MODEL)),
        'c': nrm(ks[2], (DEC_BATCH, D_MODEL)),
        'state_rglru': nrm(ks[3], (DEC_BATCH, N_EVEN, 2, D_RG), 0.5),
        'cache_k': nrm(ks[4], (DEC_BATCH, N_ODD, PAST_LEN, N_KV, HEAD_DIM)),
        'cache_v': nrm(ks[5], (DEC_BATCH, N_ODD, PAST_LEN, N_KV, HEAD_DIM)),
        'c_ctx': nrm(ks[6], (D_MODEL,)),
        'w_mod': nrm(ks[7], (DEPTH, D_MODEL, N_MOD * D_MODEL), 0.5 * D_MODEL ** -0.5),
        'b_mod': nrm(ks[8], (DEPTH, N_MOD * D_MODEL), 0.02),
        'norm_mix_pre': gain(ks[9], (DEPTH, D_MODEL)),
        'norm_mix_post': gain(ks[10], (DEPTH, D_MODEL)),
        'norm_ffn_pre': gain(ks[11], (DEPTH, D_MODEL)),
        'norm_ffn_post': gain(ks[12], (DEPTH, D_MODEL)),
        'w_ffn_in': nrm(ks[13], (DEPTH, D_MODEL, D_FF), D_MODEL ** -0.5),
        'w_ffn_out': nrm(ks[14], (DEPTH, D_FF, D_MODEL), D_FF ** -0.5),
        'w_in_even': nrm(ks[15], (N_EVEN, D_MODEL, 2 * D_A + 2 * D_RG), D_MODEL ** -0.5),
        'w_out_even': nrm(ks[16], (N_EVEN, D_A + D_RG, D_MODEL), (D_A + D_RG) ** -0.5),
        'gmlp_norm': gain(ks[17], (N_EVEN, D_A)),
        'gmlp_ws': nrm(ks[18], (N_EVEN, H_A, CHUNK, CHUNK), CHUNK ** -0.5),
        'gmlp_bs': 1.0 + nrm(ks[19], (N_EVEN, H_A, CHUNK), 0.02),
        'rg_conv_w': nrm(ks[20], (N_EVEN, 2, CONV_W, D_RG), CONV_W ** -0.5),
        'rg_conv_b': nrm(ks[21], (N_EVEN, 2, D_RG), 0.02),
        'rg_wa': nrm(ks[22], (N_EVEN, 2, H_RG, BLK_RG, BLK_RG), BLK_RG ** -0.5),
        'rg_ba': nrm(ks[23], (N_EVEN, 2, D_RG), 0.02),
        'rg_wi': nrm(ks[24], (N_EVEN, 2, H_RG, BLK_RG, BLK_RG), BLK_RG ** -0.5),
        'rg_bi': nrm(ks[25], (N_EVEN, 2, D_RG), 0.02),
        'rg_lambda': rg_lambda,
        'w_qkv': nrm(ks[27], (N_ODD, D_MODEL, D_MIX + 2 * N_KV * HEAD_DIM), D_MODEL ** -0.5),
        'w_out_odd': nrm(ks[28], (N_ODD, D_MIX, D_MODEL), D_MIX ** -0.5),
        'attn_sink': nrm(ks[29], (N_ODD, N_HEADS), 0.5),
    }

def reference(x_prompt, x_sample, c, state_rglru, cache_k, cache_v, c_ctx, w_mod, b_mod,
              norm_mix_pre, norm_mix_post, norm_ffn_pre, norm_ffn_post, w_ffn_in, w_ffn_out,
              w_in_even, w_out_even, gmlp_norm, gmlp_ws, gmlp_bs, rg_conv_w, rg_conv_b,
              rg_wa, rg_ba, rg_wi, rg_bi, rg_lambda, w_qkv, w_out_odd, attn_sink):
    xp, xs = x_prompt, x_sample
    n_ctx = xp.shape[0]
    rg_states, ctx_keys, ctx_vals = [], [], []
    for layer in range(DEPTH):
        mod_p = ada_params(c_ctx[None, :], w_mod[layer], b_mod[layer])
        mod_s = ada_params(c, w_mod[layer], b_mod[layer])
        hp = modulate(rmsnorm(xp, norm_mix_pre[layer]), mod_p[0], mod_p[1])
        hs = modulate(rmsnorm(xs, norm_mix_pre[layer]), mod_s[0], mod_s[1])
        if layer % 2 == 0:
            e = layer // 2
            prm = (w_in_even[e], w_out_even[e], gmlp_norm[e], gmlp_ws[e], gmlp_bs[e],
                   rg_conv_w[e], rg_conv_b[e], rg_wa[e], rg_ba[e], rg_wi[e], rg_bi[e], rg_lambda[e])
            h0 = jnp.zeros((n_ctx, 2, D_RG), dtype=xp.dtype)
            yp, fin = even_mixer(hp, h0, *prm)
            ys, _ = even_mixer(hs, state_rglru[:, e], *prm)
            rg_states.append(fin)
        else:
            o = layer // 2
            yp, kc, vc = odd_mixer_context(hp, w_qkv[o], w_out_odd[o], attn_sink[o])
            ys = odd_mixer_latent(hs, cache_k[:, o], cache_v[:, o], w_qkv[o], w_out_odd[o], attn_sink[o])
            ctx_keys.append(kc)
            ctx_vals.append(vc)
        xp = xp + mod_p[2] * rmsnorm(yp, norm_mix_post[layer])
        xs = xs + mod_s[2] * rmsnorm(ys, norm_mix_post[layer])
        hp = modulate(rmsnorm(xp, norm_ffn_pre[layer]), mod_p[3], mod_p[4])
        hs = modulate(rmsnorm(xs, norm_ffn_pre[layer]), mod_s[3], mod_s[4])
        xp = xp + mod_p[5] * rmsnorm(sq_relu_mlp(hp, w_ffn_in[layer], w_ffn_out[layer]), norm_ffn_post[layer])
        xs = xs + mod_s[5] * rmsnorm(sq_relu_mlp(hs, w_ffn_in[layer], w_ffn_out[layer]), norm_ffn_post[layer])
    new_state_rglru = jnp.stack(rg_states, axis=1)
    new_cache_k = jnp.stack(ctx_keys, axis=1)
    new_cache_v = jnp.stack(ctx_vals, axis=1)
    return (xp, xs, new_state_rglru, new_cache_k, new_cache_v)


_drawn_inputs = setup_inputs


def setup_inputs(seed=0):
    import zlib

    import numpy as np

    out = dict(_drawn_inputs(seed))
    spreads = {}
    factors = {'norm_mix_post': 2.737,
     'norm_ffn_post': 2.807,
     'gmlp_norm': 8.0,
     'gmlp_bs': 8.0,
     'rg_ba': 8.0,
     'rg_bi': 7.614,
     'attn_sink': 8.0}
    for name, (base, spread) in spreads.items():
        noise = np.random.default_rng([zlib.crc32(name.encode()), seed]).standard_normal(out[name].shape)
        drawn = base * np.exp(spread * noise) if base else spread * noise
        out[name] = __import__('jax').numpy.asarray(drawn.astype(out[name].dtype))
    for name, factor in factors.items():
        out[name] = (out[name] * factor).astype(out[name].dtype)
    return out
```

```python
from contextlib import ExitStack

import numpy as np

import concourse.bass as bass
from concourse import mybir

P = 128
D = 1024
KD = D // P
TT = 5
TOK = TT * P
LAT = 4
FF = 4 * D
FC = FF // 512
HD = 64
NKV = 4
RAWN = 2
RING = 6
AS = 6
EPS = 1e-6
G_MIX, G_FFN, CW, CB, BA, BI, LAM, ST, BS, NCOL = 0, 16, 32, 64, 72, 80, 88, 96, 104, 108


def schedule():
    loads, steps = [], []
    n = dict(block=0, a=0, b=0, m=0)

    def load(kind, **spec):
        blocks = 0 if kind == "mod" else 2
        loads.append(dict(kind=kind, first=n["block"], blocks=blocks, m=n["m"], **spec))
        n["block"] += blocks
        return len(loads) - 1

    def step(kind, uses_a=0, uses_b=0, uses_m=0, frees=0, **spec):
        s = dict(kind=kind, a=n["a"], b=n["b"], m=n["m"], split=[], **spec)
        n["a"] += uses_a
        n["b"] += uses_b
        n["m"] += uses_m
        if frees:
            done = n.setdefault("freed", 0)
            s["split"] = list(range(done + RING, done + RING + frees))
            n["freed"] = done + frees
        s["frees"] = frees
        steps.append(s)
        return s

    pend = []

    def flush():
        if pend:
            layer, c, half, k = pend.pop()
            step("modfin", uses_m=1 if c not in (2, 5) else 2, layer=layer, c=c, half=half, n=k)

    cb = [0]

    def mod(layer, c, half):
        flush()
        ld = load("mod", layer=layer, c=c, half=half, kh=0, n=cb[0])
        load("mod", layer=layer, c=c, half=half, kh=1, n=cb[0])
        step("mod", uses_m=1, layer=layer, c=c, half=half, ld=ld, n=cb[0])
        pend.append((layer, c, half, cb[0]))
        cb[0] += 1

    def apair(what, tile, src, col, part=None, ld=None, norm=0):
        if ld is None:
            ld = load("acols", src=src, col=col)
        j = loads[ld]["first"]
        if part == 0:
            return step("A", uses_a=0, what=what, tile=tile, j=j, parts=(0,), fin=False, norm=norm), ld
        return step("A", uses_a=2, frees=2, what=what, tile=tile, j=j, parts=(1,) if part == 1 else (0, 1), fin=True, norm=norm), ld

    def bgroup(what, nb, t, j, ph=None):
        step("B", uses_b=1, frees=4 if t == TT - 1 else 0, what=what, nb=nb, t=t, j=j, ph=ph)

    def bload(src, nb):
        ld = load("bcols", src=src, col=512 * nb, kh=0)
        load("bcols", src=src, col=512 * nb, kh=1)
        return loads[ld]["first"]

    tcount = [0]

    def P_(ph, t):
        step("P", ph=ph, t=t, yb=n["b"] - 1)

    def T_(ph, t):
        step("T", uses_m=2, ph=ph, t=t, n=tcount[0])
        tcount[0] += 1

    def ffn(layer, fillers):
        fill = list(fillers)
        ph = 1 if layer == 0 else 3

        def tiles(nt, part=None, ld=None):
            return apair("ffn", nt + 32 * layer, ("w1", layer), nt * P, part, ld, ph)[1]

        ld = tiles(0, 0)
        T_(ph, TT - 1)
        tiles(0, 1, ld)
        tiles(2)
        for c in range(FC):
            if c + 1 < FC:
                tiles(4 * c + 4)
            l0 = load("w2", layer=layer, c=c, kh=0)
            load("w2", layer=layer, c=c, kh=1)
            j = loads[l0]["first"]
            last = c == FC - 1
            for t in range(TT):
                step("G2", uses_b=2, frees=4 if t == TT - 1 else 0, layer=layer, c=c, t=t, j=j, ph=ph + 1)
                if t in (0, 2) and fill and not last:
                    mod(*fill.pop(0))
                if last:
                    if t:
                        if ph + 1 < 4:
                            T_(ph + 1, t - 1)
                    else:
                        flush()
                    P_(ph + 1, t)
            if c + 1 < FC:
                tiles(4 * c + 6)
        assert not fill and not pend

    step("sheet", uses_m=1)
    for t in range(TT):
        P_(0, t)
    for c in (1, 0):
        for half in (0, 1):
            mod(0, c, half)
    flush()
    for t in range(TT):
        T_(0, t)
        if t in (1, 3, 4):
            j = {1: 0, 3: 2, 4: 4}[t]
            steps[-1]["split"] = [j, j + 1]
    apair("xr", 0, ("w_in",), 1536)
    apair("xr", 2, ("w_in",), 1536 + 256)
    apair("gate", 0, ("w_in",), 1024)
    step("rg", uses_a=4, tile=0)
    apair("gate", 2, ("w_in",), 1024 + 256)
    step("rg", uses_a=4, tile=1)
    j = bload(("w_in",), 1)
    for t in range(TT):
        bgroup("v", 1, t, j)
        if t in (0, 2):
            mod(0, 3, t // 2)
        if t == 2:
            step("rg", uses_a=4, tile=2)
    j = bload(("w_in",), 0)
    for t in range(TT):
        bgroup("u", 0, t, j)
        if t == 0:
            mod(0, 4, 0)
            step("rg", uses_a=4, tile=3)
        if t == 3:
            mod(0, 4, 1)
            step("wsin")
    flush()
    step("gmlp", uses_a=4, uses_m=1)
    step("ya", uses_m=TT)
    for nb in (0, 1):
        j = bload(("w_out_even",), nb)
        for t in range(TT):
            bgroup("wout", nb, t, j, ph=1)
            if nb == 0 and t in (0, 2):
                mod(0, 2, t // 2)
            if nb == 0 and t == 4:
                flush()
            if nb:
                if t:
                    T_(1, t - 1)
                P_(1, t)
    ffn(0, [(0, 5, 0), (0, 5, 1)] + [(1, c, h) for c in (0, 1, 3, 4) for h in (0, 1)])
    step("l1in")
    pu = None
    for nb in range(3):
        j = bload(("w_qkv",), nb)
        b0 = n["b"]
        for t in range(TT):
            bgroup("qkv", nb, t, j)
            if nb == 0 and t == 1:
                T_(2, TT - 1)
            if t:
                pu = n["m"]
                step("qkvT", uses_m=1, nb=nb, t=t - 1, group=b0 + t - 1)
            step("rope", nb=nb, t=t, group=b0 + t, pu=pu)
        pu = n["m"]
        step("qkvT", uses_m=1, nb=nb, t=TT - 1, group=b0 + TT - 1)
        if nb == 1:
            pu = n["m"]
            step("kcache", uses_m=1)
    step("kvout", group=b0)
    units = [(g, t) for t in range(TT) for g in range(NKV)]
    for i, (g, t) in enumerate(units):
        step("S", n=i, g=g, t=t)
        if i > 1:
            step("PV", uses_m=1, n=i - 2, g=units[i - 2][0], t=units[i - 2][1])
        step("softmax", n=i, g=g, t=t)
    for i in (len(units) - 2, len(units) - 1):
        step("PV", uses_m=1, n=i, g=units[i][0], t=units[i][1])
    for nb in (0, 1):
        j = bload(("w_out_odd",), nb)
        for t in range(TT):
            bgroup("wout", nb, t, j, ph=3)
            if nb == 0 and t in (0, 2):
                mod(1, 2, t // 2)
            if nb == 0 and t == 4:
                flush()
            if nb:
                if t:
                    T_(3, t - 1)
                P_(3, t)
    ffn(1, [(1, 5, 0), (1, 5, 1)])
    mod_step = {ld: i for i, s in enumerate(steps) if s["kind"] == "mod" for ld in (s["ld"], s["ld"] + 1)}
    owner = [i for i, ld in enumerate(loads) for _ in range(ld["blocks"])]
    pending = [(i, j) for i, s in enumerate(steps) for j in s["split"] if j < n["block"]]
    for s in steps:
        s["split"] = []
    at = 0
    for i, j in pending:
        at = max([at, i] + [mod_step[ld] for ld in range(max(0, owner[j] - 9), owner[j] - 1) if ld in mod_step])
        steps[at]["split"].append((j, steps[i]))
    return loads, steps


def key_tiles(t):
    if t == 0:
        return [0]
    return list(range(max(1, t - 1), min(LAT, t + 1) + 1)) + [5]


def mask_start(t):
    return {0: P, 1: P, LAT: 4 * P}.get(t, 0)


def pv_steps(n):
    return sum(len(key_tiles(t)) for t in range(TT) for _ in range(NKV) if t * NKV + _ < n)


def hybrid_step(nc, A):
    f32, f32r, bf16 = mybir.dt.float32, mybir.dt.float32r, mybir.dt.bfloat16
    ALU, ACT, AX = mybir.AluOpType, mybir.ActivationFunctionType, mybir.AxisListType
    LOADS, STEPS = schedule()

    ctx = ExitStack()
    with ctx:
        def sb(name, shape, dt=f32):
            return ctx.enter_context(nc.sbuf_tensor(name, shape, dt))

        def alias(name, shape, dt=f32):
            with nc.sbuf_tensor(name, shape, dt) as t:
                return t

        def sem(name):
            return ctx.enter_context(nc.semaphore(name))

        X = sb("X", [P, TT, D])
        HH = sb("HH", [P, KD, TOK], f32r)
        HL = sb("HL", [P, KD, TOK], f32r)
        WH = sb("WH", [P, RING, 1024], f32r)
        WL = sb("WL", [P, RING, 1024], f32r)
        RAW = sb("RAW", [P, RAWN, 2048])
        MX = alias("MX", [P, 2 * AS * TOK])
        AH = sb("AH", [P, AS, TOK], f32r)
        AL = sb("AL", [P, AS, TOK], f32r)
        ACC = sb("ACC", [P, TT, D])
        GG = sb("GG", [P, 4, D])
        HF = sb("HF", [P, KD, P])
        PART = sb("PART", [P, 512])
        BMR = sb("BMR", [2, 512])
        IDN = sb("IDN", [P, P])
        SEL = sb("SEL", [P, 2, P])
        CC = sb("CC", [P, 2, KD])
        CSG = sb("CSG", [P, 2, KD])
        CL = sb("CL", [P, KD, 32])
        MODC = sb("MODC", [P, 2, 4, KD, 2])
        SHEET = sb("SHEET", [NCOL, P])
        PC = sb("PC", [P, NCOL])
        STAT = sb("STAT", [P, TT, 6])
        EPSC = sb("EPSC", [P, 1])
        LG = sb("LG", [P, 4, 8])
        NCL = sb("NCL", [P, 8])
        NS = sb("NS", [P, 8])
        SV = sb("SV", [P, TT, 3])
        AST = sb("AST", [P, 2, 6, 4])
        SINK = sb("SINK", [P, 16])

        PS = ctx.enter_context(nc.psum_tensor("PS", [P, 8, 512], f32))
        PSF = PS[:, :, :].rearrange("p b n -> p (b n)")

        U = ACC[:, :, 0:512]
        V = ACC[:, :, 512:1024]
        XR = MX[:, 0:2560].rearrange("p (j n) -> p j n", j=4)
        GT = MX[:, 2560:5120].rearrange("p (j n) -> p j n", j=4)
        BD = MX[:, 5120:7168].rearrange("p (w d j n) -> p w d j n", w=2, d=2, j=4)
        GMN = MX[:, 7168:7680]
        GGF = GG[:, :, :].rearrange("p v n -> p (v n)")
        RG = [GGF[:, i * TOK:(i + 1) * TOK] for i in range(6)] + [HF[:, :, :].rearrange("p k n -> p (k n)")[:, 0:TOK]]
        RR, II, TH, DD = RG[0:2], RG[2:4], RG[4:6], RG[6]
        WST = GG[:, 2, 0:512].rearrange("p (h n) -> p h n", h=4)
        WSR = GG[:, 2, 512:1024].rearrange("p (h n) -> p h n", h=4)
        KT = MX[:, 0:3072].rearrange("p (g n) -> p g n", g=NKV)
        VV = MX[:, 3072:4608].rearrange("p (t n) -> p t n", t=6)
        MASK = MX[:, 4608:5504]
        ROPE = MX[:, 5504:6016].rearrange("p (w t n) -> p w t n", w=2, t=LAT)
        QK1 = MX[:, 6016:6528]
        QK2 = MX[:, 6528:7040]
        KDUP = MX[:, 7040:7552].rearrange("p (g s d) -> p g s d", g=NKV, s=2)
        ACF = ACC[:, :, :].rearrange("p t n -> p (t n)")
        QT = ACF.rearrange("p (k n) -> p k n", k=KD)
        Z = GGF.rearrange("p (u h n) -> p u h n", u=2, h=4)
        XCB = sb("XCB", [P, 2 * TOK])
        XC = [XCB[:, i * TOK:(i + 1) * TOK] for i in range(2)]
        JUNK = XCB[:, 0:D]
        PT = [HF[:, 0:4, :].rearrange("p k n -> p (k n)"), HF[:, 4:8, :].rearrange("p k n -> p (k n)"),
              XC[0][:, 0:512], XC[1][:, 0:512]]

        raw_in = [sem(f"raw_in{i}") for i in range(RAWN)]
        const_in = [sem(f"const_in{i}") for i in range(14)]
        w_hi, w_lo, mod_read = sem("w_hi"), sem("w_lo"), sem("mod_read")
        a_ready = [sem(f"a_ready{i}") for i in range(2)]
        a_free = [sem(f"a_free{i}") for i in range(2)]
        b_ready = [sem(f"b_ready{i}") for i in range(2)]
        b_free = [sem(f"b_free{i}") for i in range(2)]
        m_ready = [sem(f"m_ready{i}") for i in range(2)]
        m_free = [sem(f"m_free{i}") for i in range(2)]
        bmr_in, bmr_free = sem("bmr_in"), sem("bmr_free")
        gg_in = [sem(f"gg_in{i}") for i in range(2)]
        dve_done, act_done = sem("dve_done"), sem("act_done")
        cl_ready, lam_e, lam_ready, csg = sem("cl_ready"), sem("lam_e"), sem("lam_ready"), sem("csg")
        consts_made = sem("consts_made")
        ysum, xsum, x_new, xn_ready = sem("ysum"), sem("xsum"), sem("x_new"), sem("xn_ready")
        h_hi, h_lo = sem("h_hi"), sem("h_lo")
        sq_ready, a_hi, a_lo = sem("sq_ready"), sem("a_hi"), sem("a_lo")
        xc_ready, ea_ready, q_ready, root_ready, rg_done = (sem("xc_ready"), sem("ea_ready"), sem("q_ready"), sem("root_ready"),
                                                            sem("rg_done"))
        vs_ready, vn_ready, wst_in = sem("vs_ready"), sem("vn_ready"), sem("wst_in")
        mix_hi, mix_lo = sem("mix_hi"), sem("mix_lo")
        l1_in = [sem(f"l1_in{i}") for i in range(5)]
        qk_ready, v_done = sem("qk_ready"), sem("v_done")
        s_done, z_ready, e_ready, p_ready, nm_ready, es_ready = (sem("s_done"), sem("z_ready"), sem("e_ready"),
                                                                 sem("p_ready"), sem("nm_ready"), sem("es_ready"))
        pt_mm = [sem(f"pt_mm{i}") for i in range(2)]
        pt_ready = sem("pt_ready")
        stored = sem("stored")

        def upto(eng, pair, n):
            eng.wait_ge(pair[n % 2], n // 2 + 1)

        CHUNK_B = [s["b"] + 1 for s in STEPS if s["kind"] == "G2" and s["t"] == TT - 1]
        PV_M = [s["m"] for s in STEPS if s["kind"] == "PV"]
        QKV_M = [s["m"] for s in STEPS if s["kind"] == "qkvT"][-1]

        def step_done(eng, s):
            if s["kind"] == "A":
                upto(eng, a_ready, s["a"] + 1)
            elif s["kind"] == "B":
                upto(eng, b_ready, s["b"])
            elif s["kind"] == "G2":
                upto(eng, b_ready, s["b"] + 1)

        def w_view(ld, b):
            raw = RAW[:, ld % RAWN, :]
            k = LOADS[ld]["kind"]
            if k == "acols":
                return raw.rearrange("p (k n) -> p k n", k=KD)[:, :, P * b:P * b + P]
            return raw[:, 1024 * b:1024 * b + 1024]

        def ring_view(buf, ld, j):
            k = LOADS[ld]["kind"]
            if k == "acols":
                return buf[:, j % RING, :].rearrange("p (k n) -> p k n", k=KD)
            return buf[:, j % RING, :]

        BLOCK_LOAD = {}
        for i, ld in enumerate(LOADS):
            for b in range(ld["blocks"]):
                BLOCK_LOAD[ld["first"] + b] = (i, b)

        def raw_arrived(eng, ld):
            eng.wait_ge(raw_in[ld % RAWN], 16 * (ld // RAWN + 1))

        def dram_view(ld):
            k = ld["kind"]
            if k == "mod":
                w = A["w_mod"][ld["layer"]].rearrange("(p k) n -> p k n", k=KD)
                c0 = ld["c"] * D + ld["half"] * 512
                return w[:, 4 * ld["kh"]:4 * ld["kh"] + 4, c0:c0 + 512]
            if k == "w2":
                w = A["w_ffn_out"][ld["layer"]].rearrange("(k p) n -> p k n", p=P)
                k0 = 4 * ld["c"] + 2 * ld["kh"]
                return w[:, k0:k0 + 2, :]
            src = ld["src"]
            w = A["w_ffn_in"][src[1]] if src[0] == "w1" else {
                "w_in": A["w_in_even"], "w_out_even": A["w_out_even"], "w_qkv": A["w_qkv"],
                "w_out_odd": A["w_out_odd"]}[src[0]][0]
            w = w.rearrange("(k p) n -> p k n", p=P)
            if k == "acols":
                return w[:, :, ld["col"]:ld["col"] + 256]
            return w[:, 4 * ld["kh"]:4 * ld["kh"] + 4, ld["col"]:ld["col"] + 512]

        def raw_dst(i, ld):
            k = {"mod": 4, "w2": 2, "acols": KD, "bcols": 4}[ld["kind"]]
            return RAW[:, i % RAWN, :].rearrange("p (k n) -> p k n", k=k)

        def a_bank(a):
            base = 1024 * (a % 2) + 256
            return PSF[:, base:base + TOK]

        def m_bank(u):
            return PS[:, 6 + u % 2, :]

        def modc(layer, c):
            return MODC[:, layer, {0: 0, 1: 1, 3: 2, 4: 3}[c], :, :]

        block = ctx.enter_context(nc.Block())

        @block.sync
        def _(sp):
            sp.dma_start(X[:, 0, :], A["x_prompt"][0]).then_inc(const_in[0], 16)
            for i, ld in enumerate(LOADS):
                if i >= RAWN:
                    old = LOADS[i - RAWN]
                    if old["kind"] == "mod" and old["kh"] == 0:
                        sp.wait_ge(mod_read, old["n"] + 1)
                    elif old["kind"] == "mod":
                        upto(sp, m_ready, old["m"])
                    else:
                        sp.wait_ge(w_lo, old["first"] + 2)
                sp.dma_start(raw_dst(i, ld), dram_view(ld)).then_inc(raw_in[i % RAWN], 16)
            for t in range(TT):
                sp.wait_ge(x_new, 3 * TT + t + 1)
                dst = A["y_prompt"][0] if t == 0 else A["y_sample"][0, (t - 1) * P:t * P, :]
                sp.dma_start(dst, X[:, t, :]).then_inc(stored, 16)
            sp.wait_ge(stored, 16 * (3 + TT))

        @block.scalar
        def _(act):
            own = [0]

            def link(ins):
                own[0] += 1
                ins.then_inc(act_done, 1)
                act.wait_ge(act_done, own[0])

            xs = A["x_sample"][0].rearrange("(t p) n -> p t n", p=P)
            act.dma_start(SHEET[:, :], A["sheet"]).then_inc(const_in[2], 16)
            act.dma_start(IDN[:, :], A["ident"]).then_inc(const_in[5], 16)
            act.dma_start(CC[:, 0, :], A["c_ctx"].rearrange("(p k) -> p k", k=KD)).then_inc(const_in[3], 16)
            act.dma_start(CC[:, 1, :], A["c"][0].rearrange("(p k) -> p k", k=KD)).then_inc(const_in[4], 16)
            act.dma_start(X[:, 1:TT, :], xs).then_inc(const_in[1], 16)
            act.dma_start(SEL[:, :, :], A["sel"]).then_inc(const_in[6], 16)
            act.dma_start(GMN, A["gmlp_norm"].broadcast_to([P, 512])).then_inc(const_in[8], 16)
            act.dma_start(SINK[:, :], A["attn_sink"].broadcast_to([P, 16])).then_inc(const_in[9], 16)
            act.wait_ge(consts_made, 3)
            for w, name in enumerate(("rg_wa", "rg_wi")):
                for d in (0, 1):
                    for odd in (0, 1):
                        act.dma_start(BD[64 * odd:64 * odd + 64, w, d, :, 64 * odd:64 * odd + 64],
                                      A[name][0, d].rearrange("(j o) i n -> o i j n", o=2)[odd]).then_inc(const_in[7], 16)
            act.wait_ge(const_in[3], 16)
            act.wait_ge(const_in[4], 16)
            nc.scalar.activation(CSG[:, :, :], CC[:, :, :], ACT.Sigmoid).then_inc(csg, 1)
            act.wait_ge(lam_e, 1)
            nc.scalar.activation(LG[:, 1, :], LG[:, 0, :], ACT.Exp).then_inc(lam_e, 1)

            def split(s):
                for j, freed_by in s["split"]:
                    ld, b = BLOCK_LOAD[j]
                    raw_arrived(act, ld)
                    step_done(act, freed_by)
                    nc.scalar.copy(ring_view(WH, ld, j), w_view(ld, b)).then_inc(w_hi, 1)

            cnt = dict(nx=0)
            for s in STEPS:
                k = s["kind"]
                if k == "mod":
                    if s["n"]:
                        act.wait_ge(bmr_free, s["n"])
                    c0 = s["c"] * D + 512 * s["half"]
                    act.dma_start(BMR[:, :], A["b_mod"][s["layer"]:s["layer"] + 1, c0:c0 + 512].broadcast_to([2, 512]))\
                        .then_inc(bmr_in, 16)
                    if s["c"] in (2, 5):
                        half, kind = s["half"], 0 if s["c"] == 2 else 2
                        if s["layer"] == 1:
                            for i in (18, 19):
                                upto(act, m_ready, PV_M[i])
                        elif kind:
                            act.wait_ge(x_new, TT)
                        else:
                            act.wait_ge(rg_done, 4)
                        g = A["norm_mix_post" if kind == 0 else "norm_ffn_post"][s["layer"]:s["layer"] + 1, 512 * half:512 * half + 512]
                        for v in (0, 1):
                            act.dma_start(GG[:, kind + v, 512 * half:512 * half + 512], g.broadcast_to([P, 512])).then_inc(gg_in[half], 16)
                if k == "P":
                    ph, t = s["ph"], s["t"]
                    if ph:
                        b = s["yb"]
                        act.wait_ge(b_free[b % 2], b // 2 + 1)
                        if ph % 2 == 0:
                            act.wait_ge(a_lo, 16 * ph)
                        link(nc.scalar.activation(JUNK, ACC[:, t, :], ACT.Square, accum_out=STAT[:, t, 0:1]))
                        nc.scalar.activation(STAT[:, t, 1:2], STAT[:, t, 0:1], ACT.Sqrt, scale=1.0 / D, bias=EPSC[:, :])\
                            .then_inc(ysum, 1)
                        act.wait_ge(x_new, cnt["nx"] + 1)
                        cnt["nx"] += 1
                    else:
                        act.wait_ge(const_in[0] if t == 0 else const_in[1], 16)
                        act.wait_ge(consts_made, 3)
                    if ph < 4:
                        link(nc.scalar.activation(JUNK, X[:, t, :], ACT.Square, accum_out=STAT[:, t, 3:4]))
                        nc.scalar.activation(STAT[:, t, 4:5], STAT[:, t, 3:4], ACT.Sqrt, scale=1.0 / D, bias=EPSC[:, :])\
                            .then_inc(xsum, 1)
                elif k == "T":
                    t = s["t"]
                    u = s["m"] + 1
                    act.wait_ge(m_free[u % 2], u // 2 + 1)
                    nc.scalar.copy(HH[:, :, t * P:t * P + P], HF[:, :, :]).then_inc(h_hi, 1)
                elif k == "A" and s["fin"]:
                    for i in (0, 1):
                        a, tile = s["a"] + i, s["tile"] + i
                        act.wait_ge(a_ready[a % 2], a // 2 + 1)
                        if s["what"] == "xr":
                            nc.scalar.copy(XR[:, tile, :], a_bank(a)).then_inc(a_free[a % 2], 1)
                        elif s["what"] == "gate":
                            nc.scalar.activation(GT[:, tile, :], a_bank(a), ACT.Gelu_apprx_tanh).then_inc(a_free[a % 2], 1)
                        else:
                            if tile:
                                act.wait_ge(sq_ready, tile)
                            nc.scalar.activation(XC[0], a_bank(a), ACT.Relu).then_inc(a_free[a % 2], 1)
                            slot, c = tile % AS, (tile - AS) // 4
                            act.wait_ge(sq_ready, tile + 1)
                            if tile >= AS:
                                upto(act, b_ready, CHUNK_B[c])
                            nc.scalar.copy(AH[:, slot, :], XC[1]).then_inc(a_hi, 1)
                elif k == "rg":
                    j = s["tile"]
                    if j:
                        act.wait_ge(rg_done, j)
                    for d in (0, 1):
                        for w, dst, col in ((0, RR[d], BA), (1, II[d], BI)):
                            a = s["a"] + 2 * d + w
                            act.wait_ge(a_ready[a % 2], a // 2 + 1)
                            nc.scalar.activation(dst, a_bank(a), ACT.Sigmoid, bias=PC[:, col + 4 * d + j:col + 4 * d + j + 1])\
                                .then_inc(a_free[a % 2], 1)
                    act.wait_ge(a_free[0], (s["a"] + 3) // 2 + 1)
                    act.wait_ge(a_free[1], (s["a"] + 3) // 2 + 1)
                    act.wait_ge(lam_ready, 1)
                    for d in (0, 1):
                        c = 4 * d + j
                        link(nc.scalar.activation(TH[d], RR[d], ACT.Tanh, scale=NCL[:, c:c + 1]))
                        nc.scalar.activation(RR[d], RR[d], ACT.Exp, scale=LG[:, 3, c:c + 1]).then_inc(ea_ready, 1)
                    for d in (0, 1):
                        act.wait_ge(q_ready, 2 * j + d + 1)
                        nc.scalar.activation(TH[d], TH[d], ACT.Sqrt, scale=2.0).then_inc(root_ready, 1)
                elif k == "B":
                    b = s["b"]
                    bank = PS[:, 4 + b % 2, :]
                    if s["what"] == "v":
                        act.wait_ge(b_ready[b % 2], b // 2 + 1)
                        nc.scalar.activation(V[:, s["t"], :], bank, ACT.Gelu_apprx_tanh).then_inc(b_free[b % 2], 1)
                        act.wait_ge(b_free[b % 2], b // 2 + 1)
                        link(nc.scalar.activation(U[:, s["t"], :], V[:, s["t"], :], ACT.Square, accum_out=SV[:, s["t"], 0:1]))
                    elif s["what"] == "u":
                        act.wait_ge(b_ready[b % 2], b // 2 + 1)
                        nc.scalar.activation(U[:, s["t"], :], bank, ACT.Gelu_apprx_tanh).then_inc(b_free[b % 2], 1)
                    elif s["what"] == "qkv" and s["nb"] == 2:
                        act.wait_ge(b_ready[b % 2], b // 2 + 1)
                        nc.scalar.copy(VV[:, s["t"], :], PS[:, 4 + b % 2, 256:512]).then_inc(v_done, 1)
                elif k == "wsin":
                    act.wait_ge(rg_done, 4)
                    act.dma_start(WSR, A["gmlp_ws"][0].rearrange("h p q -> p h q")).then_inc(wst_in, 16)
                    with nc.allow_non_contiguous_dma(reason="1024 state values, features on the partitions"):
                        act.dma_start(A["new_state"], NS[:, :]).then_inc(stored, 16)
                elif k == "l1in":
                    upto(act, b_ready, CHUNK_B[FC - 1])
                    act.dma_start(MASK, A["mask"]).then_inc(l1_in[0], 16)
                    act.dma_start(ROPE, A["rope"].rearrange("p (w t n) -> p w t n", w=2, t=LAT)).then_inc(l1_in[1], 16)
                    for dup in (0, 1):
                        act.dma_start(KDUP[:, :, dup, :], A["cache_k"][0, 0]).then_inc(l1_in[2 + dup], 16)
                    act.dma_start(VV[:, 5, :].rearrange("p (g d) -> p g d", g=NKV), A["cache_v"][0, 0]).then_inc(l1_in[4], 16)
                elif k == "gmlp":
                    act.wait_ge(act_done, own[0])
                    nc.scalar.activation(SV[:, :, 1:2], SV[:, :, 0:1], ACT.Sqrt, scale=1.0 / 512, bias=EPSC[:, :]).then_inc(vs_ready, 1)
                elif k == "ya":
                    for t in range(TT):
                        u = s["m"] + t
                        act.wait_ge(m_ready[u % 2], u // 2 + 1)
                        nc.scalar.copy(HH[:, 0:4, t * P:t * P + P], m_bank(u).rearrange("p (k n) -> p k n", k=4)).then_inc(mix_hi, 1)
                    act.wait_ge(rg_done, 4)
                    for j in range(4):
                        nc.scalar.copy(HH[:, 4 + j, :], GT[:, j, :]).then_inc(mix_hi, 1)
                elif k == "kcache":
                    u = s["m"]
                    act.wait_ge(m_ready[u % 2], u // 2 + 1)
                    nc.scalar.copy(KT[:, :, 5 * P:6 * P], m_bank(u).rearrange("p (g n) -> p g n", g=NKV)).then_inc(m_free[u % 2], 1)
                elif k == "qkvT":
                    u, nb, t = s["m"], s["nb"], s["t"]
                    act.wait_ge(m_ready[u % 2], u // 2 + 1)
                    src = m_bank(u).rearrange("p (k n) -> p k n", k=4)
                    dst = QT[:, 4 * nb:4 * nb + 4, t * P:t * P + P] if nb < 2 else KT[:, :, t * P:t * P + P]
                    nc.scalar.copy(dst, src).then_inc(m_free[u % 2], 1)
                elif k == "kvout":
                    upto(act, b_free, s["group"])
                    act.dma_start(A["new_k"], QK2[:, 256:512].rearrange("p (g d) -> p g d", g=NKV)).then_inc(stored, 16)
                    act.wait_ge(v_done, 1)
                    act.dma_start(A["new_v"], VV[:, 0, :].rearrange("p (g d) -> p g d", g=NKV)).then_inc(stored, 16)
                elif k == "softmax":
                    i, g, z = s["n"], s["g"], s["n"] % 2
                    nk = P * len(key_tiles(s["t"]))
                    act.wait_ge(nm_ready, i + 1)
                    for h in range(4):
                        nc.scalar.activation(Z[:, z, h, 0:nk], Z[:, z, h, 0:nk], ACT.Exp, scale=0.125,
                                             bias=AST[:, z, 1, h:h + 1], accum_out=AST[:, z, 2, h:h + 1]).then_inc(e_ready, 1)
                    nc.scalar.activation(AST[:, z, 3, :], AST[:, z, 4, :], ACT.Exp).then_inc(es_ready, 1)
                elif k == "PV":
                    i, g, t = s["n"], s["g"], s["t"]
                    nk = len(key_tiles(t))
                    base = pv_steps(i)
                    for kt in range(nk):
                        q = base + kt
                        act.wait_ge(pt_mm[q % 2], q // 2 + 1)
                        if i:
                            upto(act, m_ready, PV_M[i - 1])
                        nc.scalar.copy(PT[kt], PS[:, 4 + q % 2, :]).then_inc(pt_ready, 1)
                    u = s["m"]
                    act.wait_ge(m_ready[u % 2], u // 2 + 1)
                    nc.scalar.copy(HH[:, 2 * g:2 * g + 2, t * P:t * P + P], m_bank(u)[:, 0:256].rearrange("p (k n) -> p k n", k=2))\
                        .then_inc(mix_hi, 1)
                split(s)

        @block.gpsimd
        def _(pool):
            for s in STEPS:
                if s["kind"] == "T":
                    t = s["t"]
                    pool.wait_ge(h_hi, s["n"] + 1)
                    cols = slice(t * P, t * P + P)
                    nc.gpsimd.tensor_tensor(HL[:, :, cols], HF[:, :, :], HH[:, :, cols].bitcast(f32), ALU.subtract).then_inc(h_lo, 1)
                for j, _ in s["split"]:
                    ld, b = BLOCK_LOAD[j]
                    pool.wait_ge(w_hi, j + 1)
                    nc.gpsimd.tensor_tensor(ring_view(WL, ld, j), w_view(ld, b), ring_view(WH, ld, j).bitcast(f32),
                                            ALU.subtract).then_inc(w_lo, 1)

        @block.vector
        def _(dve):
            own = [0]
            V_ = nc.vector

            def link(ins):
                own[0] += 1
                ins.then_inc(dve_done, 1)
                dve.wait_ge(dve_done, own[0])

            V_.memset(EPSC[:, :], EPS).then_inc(consts_made, 1)
            V_.memset(BD, 0.0).then_inc(consts_made, 1)
            V_.memset(CL[:, :, :], 0.0).then_inc(consts_made, 1)
            dve.wait_ge(csg, 1)
            dve.wait_ge(consts_made, 3)
            V_.tensor_tensor(CL[:, :, 0:2].rearrange("p k v -> p v k"), CC[:, :, :], CSG[:, :, :], ALU.mult).then_inc(cl_ready, 1)

            def conv(j):
                if j == 0:
                    upto(dve, a_free, 2)
                    upto(dve, a_free, 3)
                for d in (0, 1):
                    w = lambda k: PC[:, CW + 16 * d + 4 * k + j:CW + 16 * d + 4 * k + j + 1]
                    link(V_.tensor_scalar(XC[d], XR[:, j, :], w(3 if d == 0 else 0),
                                          PC[:, CB + 4 * d + j:CB + 4 * d + j + 1], ALU.mult, ALU.add))
                    for sh in (1, 2, 3):
                        for lo, hi in ((0, P), (P, TOK)):
                            dst, src = (slice(lo + sh, hi), slice(lo, hi - sh)) if d == 0 else (slice(lo, hi - sh), slice(lo + sh, hi))
                            ins = V_.scalar_tensor_tensor(XC[d][:, dst], XR[:, j, src], w(3 - sh if d == 0 else sh),
                                                          XC[d][:, dst], ALU.mult, ALU.add)
                            if sh == 3 and lo:
                                ins.then_inc(xc_ready, 1)
                            else:
                                link(ins)

            def scans(d, j):
                seg = lambda lo, hi: slice(lo, hi) if d == 0 else slice(hi - 1, lo - 1 if lo else None, -1)
                link(V_.tensor_tensor_scan(TH[d][:, seg(0, P)], RR[d][:, seg(0, P)], II[d][:, seg(0, P)], 0.0, ALU.mult, ALU.add))
                link(V_.tensor_tensor_scan(TH[d][:, seg(P, TOK)], RR[d][:, seg(P, TOK)], II[d][:, seg(P, TOK)],
                                           PC[:, ST + 4 * d + j:ST + 4 * d + j + 1], ALU.mult, ALU.add))
                end = P - 1 if d == 0 else 0
                V_.tensor_copy(NS[:, 4 * d + j:4 * d + j + 1], TH[d][:, end:end + 1]).then_inc(dve_done, 1)
                own[0] += 1

            def normalise(i, t):
                z = i % 2
                nk = P * len(key_tiles(t))
                dve.wait_ge(e_ready, 4 * (i + 1))
                dve.wait_ge(es_ready, i + 1)
                link(V_.tensor_tensor(AST[:, z, 2, :], AST[:, z, 2, :], AST[:, z, 3, :], ALU.add))
                link(V_.reciprocal(AST[:, z, 5, :], AST[:, z, 2, :]))
                for h in range(4):
                    V_.tensor_scalar(Z[:, z, h, 0:nk], Z[:, z, h, 0:nk], AST[:, z, 5, h:h + 1], None, ALU.mult).then_inc(p_ready, 1)

            nmod = nchain = 0
            fin_g = 0
            prev_t = None
            for s in STEPS:
                k = s["kind"]
                if k == "sheet":
                    u = s["m"]
                    dve.wait_ge(m_ready[u % 2], u // 2 + 1)
                    V_.tensor_copy(PC[:, :], m_bank(u)[:, 0:NCOL]).then_inc(m_free[u % 2], 1)
                    dve.wait_ge(m_free[u % 2], u // 2 + 1)
                    lam = PC[:, LAM:LAM + 8]
                    link(V_.tensor_scalar(LG[:, 1, :], lam, -1.0, None, ALU.mult))
                    V_.tensor_tensor(LG[:, 0, :], lam, LG[:, 1, :], ALU.min).then_inc(lam_e, 1)
                    dve.wait_ge(lam_e, 2)
                    e, v, w, acc = LG[:, 1, :], LG[:, 0, :], LG[:, 2, :], LG[:, 3, :]
                    link(V_.tensor_scalar(w, e, 2.0, None, ALU.add))
                    link(V_.reciprocal(w, w))
                    link(V_.tensor_tensor(v, e, w, ALU.mult))
                    link(V_.tensor_tensor(w, v, v, ALU.mult))
                    link(V_.memset(acc, 1.0 / 17))
                    for q in (15, 13, 11, 9, 7, 5, 3, 1):
                        link(V_.tensor_tensor(acc, acc, w, ALU.mult))
                        link(V_.tensor_scalar(acc, acc, 1.0 / q, None, ALU.add))
                    link(V_.tensor_tensor(acc, acc, v, ALU.mult))
                    link(V_.tensor_scalar(v, lam, 0.0, 8.0, ALU.min, ALU.mult))
                    link(V_.scalar_tensor_tensor(acc, acc, -16.0, v, ALU.mult, ALU.add))
                    V_.tensor_scalar(NCL[:, :], acc, -1.0, None, ALU.mult).then_inc(lam_ready, 1)
                elif k == "mod":
                    u = s["m"]
                    nmod += 1
                    dve.wait_ge(bmr_in, 16 * nmod)
                    dve.wait_ge(m_ready[u % 2], u // 2 + 1)
                    V_.tensor_copy(PART[:, :], m_bank(u)).then_inc(m_free[u % 2], 1)
                    dve.wait_ge(m_free[u % 2], u // 2 + 1)
                    V_.tensor_tensor(PART[0:2, :], PART[0:2, :], BMR[:, :], ALU.add).then_inc(bmr_free, 1)
                elif k == "modfin":
                    layer, c, half = s["layer"], s["c"], s["half"]
                    if c in (2, 5):
                        fin_g += half == 0
                        for v in (0, 1):
                            u = s["m"] + v
                            dve.wait_ge(m_ready[u % 2], u // 2 + 1)
                            dve.wait_ge(gg_in[half], 32 * fin_g)
                            g = GG[:, (0 if c == 2 else 2) + v, 512 * half:512 * half + 512]
                            V_.tensor_tensor(g, m_bank(u), g, ALU.mult).then_inc(m_free[u % 2], 1)
                    else:
                        u = s["m"]
                        dve.wait_ge(m_ready[u % 2], u // 2 + 1)
                        src = m_bank(u).rearrange("p (i g w) -> p i w g", i=4, g=4)[:, :, 0:2, :]
                        dst = modc(layer, c)[:, 4 * half:4 * half + 4, :]
                        V_.tensor_reduce(dst, src, AX.X, ALU.add).then_inc(m_free[u % 2], 1)
                        if c in (1, 4):
                            dve.wait_ge(m_free[u % 2], u // 2 + 1)
                            g0 = (G_MIX if c == 1 else G_FFN) + 8 * layer + 4 * half
                            for v in (0, 1):
                                link(V_.scalar_tensor_tensor(dst[:, :, v], dst[:, :, v], 1.0, PC[:, g0:g0 + 4], ALU.add, ALU.mult))
                elif k == "P":
                    ph, t = s["ph"], s["t"]
                    if ph:
                        nchain += 1
                        dve.wait_ge(ysum, nchain)
                        link(V_.reciprocal(STAT[:, t, 2:3], STAT[:, t, 1:2]))
                        gain = GG[:, (0 if ph in (1, 3) else 2) + (t > 0), :]
                        link(V_.scalar_tensor_tensor(ACC[:, t, :], ACC[:, t, :], STAT[:, t, 2:3], gain, ALU.mult, ALU.mult))
                        V_.tensor_tensor(X[:, t, :], X[:, t, :], ACC[:, t, :], ALU.add).then_inc(x_new, 1)
                    if ph < 4:
                        dve.wait_ge(xsum, ph * TT + t + 1)
                        link(V_.reciprocal(STAT[:, t, 5:6], STAT[:, t, 4:5]))
                        V_.tensor_scalar(ACC[:, t, :], X[:, t, :], STAT[:, t, 5:6], None, ALU.mult).then_inc(xn_ready, 1)
                elif k == "T":
                    ph, t, u0 = s["ph"], s["t"], s["m"]
                    layer, off = ph // 2, 0 if ph % 2 == 0 else 2
                    v = 0 if t == 0 else 1
                    if s["n"]:
                        dve.wait_ge(h_lo, s["n"])
                    for q in (0, 1):
                        u = u0 + q
                        dve.wait_ge(m_ready[u % 2], u // 2 + 1)
                        for i in range(4):
                            f = 4 * q + i
                            ins = V_.tensor_scalar(HF[:, f, :], m_bank(u)[:, P * i:P * i + P], MODC[:, layer, off + 1, f, v:v + 1],
                                                   MODC[:, layer, off, f, v:v + 1], ALU.mult, ALU.add)
                        ins.then_inc(m_free[u % 2], 1)
                elif k == "A":
                    if s["what"] == "xr" and s["fin"] and s["tile"] == 2:
                        conv(0)
                    if s["what"] == "ffn" and s["fin"]:
                        for tile in (s["tile"], s["tile"] + 1):
                            slot = tile % AS
                            a = s["a"] + tile - s["tile"]
                            dve.wait_ge(a_free[a % 2], a // 2 + 1)
                            if tile:
                                dve.wait_ge(a_hi, tile)
                                dve.wait_ge(a_lo, tile)
                            V_.tensor_tensor(XC[1], XC[0], XC[0], ALU.mult).then_inc(sq_ready, 1)
                            dve.wait_ge(a_hi, tile + 1)
                            V_.tensor_tensor(AL[:, slot, :], XC[1], AH[:, slot, :].bitcast(f32), ALU.subtract).then_inc(a_lo, 1)
                elif k == "rg":
                    j = s["tile"]
                    if j == 0:
                        dve.wait_ge(h_lo, TT)
                    for d in (0, 1):
                        dve.wait_ge(ea_ready, 2 * j + d + 1)
                        link(V_.tensor_scalar(DD, TH[d], 1.0, None, ALU.add))
                        link(V_.reciprocal(DD, DD))
                        V_.tensor_tensor(TH[d], TH[d], DD, ALU.mult).then_inc(q_ready, 1)
                        dve.wait_ge(q_ready, 2 * j + d + 1)
                        link(V_.tensor_tensor(II[d], II[d], XC[d], ALU.mult))
                    for d in (0, 1):
                        dve.wait_ge(root_ready, 2 * j + d + 1)
                        link(V_.tensor_tensor(II[d], II[d], TH[d], ALU.mult))
                        scans(d, j)
                    link(V_.tensor_tensor(TH[0], TH[0], TH[1], ALU.add))
                    V_.tensor_tensor(GT[:, j, :], GT[:, j, :], TH[0], ALU.mult).then_inc(rg_done, 1)
                    if j < 3:
                        conv(j + 1)
                elif k == "B":
                    b, t, nb, what = s["b"], s["t"], s["nb"], s["what"]
                    bank = PS[:, 4 + b % 2, :]
                    if what == "wout":
                        dve.wait_ge(b_ready[b % 2], b // 2 + 1)
                        V_.tensor_copy(ACC[:, t, 512 * nb:512 * nb + 512], bank).then_inc(b_free[b % 2], 1)
                elif k == "rope":
                    t, nb, b = s["t"], s["nb"], s["group"]
                    bank = PS[:, 4 + b % 2, :]
                    heads = 8 if nb < 2 else NKV
                    n = heads * HD
                    if nb == 2:
                        dve.wait_ge(v_done, t + 1)
                    upto(dve, b_ready, b)
                    if s["pu"] is not None:
                        upto(dve, m_ready, s["pu"])
                    if t == 0 and nb < 2:
                        V_.tensor_copy(QK1, bank).then_inc(b_free[b % 2], 1)
                    elif t == 0:
                        kv = bank[:, 0:n].rearrange("p (g d) -> p g d", g=NKV)
                        V_.tensor_copy(KDUP[:, :, 0, :], kv)
                        V_.tensor_copy(KDUP[:, :, 1, :], kv)
                        V_.tensor_copy(QK2[:, 256:512], bank[:, 0:n]).then_inc(b_free[b % 2], 1)
                    else:
                        if nb == 0 and t == 1:
                            dve.wait_ge(l1_in[1], 16)
                        hv = lambda x: x[:, 0:n].rearrange("p (h d) -> p h d", h=heads)
                        parts = lambda x, o: x.rearrange("p (h b o f) -> p h b o f", b=2, o=2, f=16)[:, :, :, o, :]
                        link(V_.tensor_tensor(hv(QK1), hv(bank), ROPE[:, 0, t - 1, :].unsqueeze(1).broadcast_to([P, heads, HD]), ALU.mult))
                        for o in (0, 1):
                            sn = parts(ROPE[:, 1, t - 1, :], o).broadcast_to([P, heads, 2, 16])
                            ins = V_.tensor_tensor(parts(QK2[:, 0:n], o), parts(bank[:, 0:n], 1 - o), sn, ALU.mult)
                        ins.then_inc(b_free[b % 2], 1)
                        upto(dve, b_free, b)
                        if nb < 2:
                            V_.tensor_tensor(QK1, QK1, QK2, ALU.add).then_inc(qk_ready, 1)
                        else:
                            V_.tensor_tensor(KDUP[:, :, 0, :], hv(QK1), hv(QK2), ALU.add)
                            V_.tensor_tensor(KDUP[:, :, 1, :], hv(QK1), hv(QK2), ALU.add).then_inc(qk_ready, 1)
                elif k == "G2":
                    t, c = s["t"], s["c"]
                    for nh in (0, 1):
                        b = s["b"] + nh
                        bank = PS[:, 4 + b % 2, :]
                        acc = ACC[:, t, 512 * nh:512 * nh + 512]
                        dve.wait_ge(b_ready[b % 2], b // 2 + 1)
                        if c:
                            V_.tensor_tensor(acc, acc, bank, ALU.add).then_inc(b_free[b % 2], 1)
                        else:
                            V_.tensor_copy(acc, bank).then_inc(b_free[b % 2], 1)
                elif k == "gmlp":
                    u = s["m"]
                    dve.wait_ge(m_ready[u % 2], u // 2 + 1)
                    V_.tensor_copy(WST, m_bank(u).rearrange("p (h n) -> p h n", h=4)).then_inc(m_free[u % 2], 1)
                    dve.wait_ge(vs_ready, 1)
                    dve.wait_ge(const_in[8], 16)
                    link(V_.reciprocal(SV[:, :, 2:3], SV[:, :, 1:2]))
                    for t in range(TT):
                        V_.scalar_tensor_tensor(V[:, t, :], V[:, t, :], SV[:, t, 2:3], GMN, ALU.mult, ALU.mult).then_inc(vn_ready, 1)
                    for h in range(4):
                        a = s["a"] + h
                        dve.wait_ge(a_ready[a % 2], a // 2 + 1)
                        uh = U[:, :, P * h:P * h + P]
                        V_.scalar_tensor_tensor(uh, a_bank(a).rearrange("p (t n) -> p t n", t=TT), PC[:, BS + h:BS + h + 1], uh,
                                                ALU.add, ALU.mult).then_inc(a_free[a % 2], 1)
                elif k == "ya":
                    for t in range(TT):
                        u = s["m"] + t
                        dve.wait_ge(mix_hi, t + 1)
                        cols = slice(t * P, t * P + P)
                        V_.tensor_tensor(HL[:, 0:4, cols], m_bank(u).rearrange("p (k n) -> p k n", k=4),
                                         HH[:, 0:4, cols].bitcast(f32), ALU.subtract).then_inc(m_free[u % 2], 1)
                    for j in range(4):
                        dve.wait_ge(mix_hi, TT + j + 1)
                        V_.tensor_tensor(HL[:, 4 + j, :], GT[:, j, :], HH[:, 4 + j, :].bitcast(f32), ALU.subtract).then_inc(mix_lo, 1)
                elif k == "softmax":
                    i, t, z = s["n"], s["t"], s["n"] % 2
                    nk = P * len(key_tiles(t))
                    m0 = mask_start(t)
                    if i == 0:
                        dve.wait_ge(l1_in[0], 16)
                        dve.wait_ge(const_in[9], 16)
                    if i >= 2:
                        upto(dve, pt_mm, pv_steps(i - 1) - 1)
                    for h in range(4):
                        dve.wait_ge(s_done, 4 * i + h + 1)
                        V_.tensor_tensor_reduce(out=Z[:, z, h, 0:nk], in0=PS[:, h, 0:nk], in1=MASK[:, m0:m0 + nk], scale=1.0,
                                                scalar=-3.0e38, op0=ALU.add, op1=ALU.max, accum_out=AST[:, z, 0, h:h + 1])\
                            .then_inc(z_ready, 1)
                    dve.wait_ge(z_ready, 4 * (i + 1))
                    snk = SINK[:, 4 * s["g"]:4 * s["g"] + 4]
                    link(V_.scalar_tensor_tensor(AST[:, z, 0, :], AST[:, z, 0, :], 0.125, snk, ALU.mult, ALU.max))
                    link(V_.tensor_scalar(AST[:, z, 1, :], AST[:, z, 0, :], -1.0, None, ALU.mult))
                    V_.tensor_tensor(AST[:, z, 4, :], snk, AST[:, z, 1, :], ALU.add).then_inc(nm_ready, 1)
                    if i:
                        normalise(i - 1, prev_t)
                    prev_t = t
                elif k == "PV":
                    i, g, t = s["n"], s["g"], s["t"]
                    if i == TT * NKV - 2:
                        normalise(TT * NKV - 1, prev_t)
                    u = s["m"]
                    dve.wait_ge(mix_hi, TT + 4 + i + 1)
                    cols = slice(t * P, t * P + P)
                    V_.tensor_tensor(HL[:, 2 * g:2 * g + 2, cols], m_bank(u)[:, 0:256].rearrange("p (k n) -> p k n", k=2),
                                     HH[:, 2 * g:2 * g + 2, cols].bitcast(f32), ALU.subtract).then_inc(m_free[u % 2], 1)

        @block.tensor
        def _(pe):
            MM = nc.tensor.matmul
            TR = nc.tensor.transpose

            def split3(out, w, x, first, last):
                (wh, wl), (xh, xl) = w, x
                MM(out, wh, xh, start=first, stop=False)
                MM(out, wh, xl, start=False, stop=False)
                return MM(out, wl, xh, start=False, stop=last)

            def a_acquire(a):
                if a >= 2:
                    pe.wait_ge(a_free[a % 2], a // 2)

            def b_acquire(b):
                if b >= 2:
                    pe.wait_ge(b_free[b % 2], b // 2)

            def m_acquire(u):
                if u >= 2:
                    pe.wait_ge(m_free[u % 2], u // 2)

            RANGE = ((0, 256), (256, TOK))
            ntiles = 0
            pe.wait_ge(const_in[5], 16)
            for s in STEPS:
                k = s["kind"]
                if k == "sheet":
                    pe.wait_ge(const_in[2], 16)
                    u = s["m"]
                    TR(m_bank(u)[:, 0:NCOL], SHEET[:, :], IDN[0:NCOL, 0:NCOL]).then_inc(m_ready[u % 2], 1)
                elif k == "mod":
                    u = s["m"]
                    m_acquire(u)
                    if s["n"] == 0:
                        pe.wait_ge(cl_ready, 1)
                    for kh in (0, 1):
                        ld = s["ld"] + kh
                        raw_arrived(pe, ld)
                        rv = RAW[:, ld % RAWN, :].rearrange("p (k n) -> p k n", k=4)
                        for kt in range(4):
                            ins = MM(PS[32 * kt:32 * kt + 32, 6 + u % 2, :], CL[:, 4 * kh + kt, :], rv[:, kt, :],
                                     start=(kh == 0), stop=(kh == 1))
                        if kh == 0:
                            ins.then_inc(mod_read, 1)
                    ins.then_inc(m_ready[u % 2], 1)
                elif k == "modfin":
                    pe.wait_ge(bmr_free, s["n"] + 1)
                    if s["c"] in (2, 5):
                        if s["c"] == 2 and s["layer"] == 0 and s["half"] == 0:
                            pe.wait_ge(const_in[6], 16)
                        for v in (0, 1):
                            u = s["m"] + v
                            m_acquire(u)
                            MM(m_bank(u), SEL[:, v, :], PART[:, :], start=True, stop=True).then_inc(m_ready[u % 2], 1)
                    else:
                        u = s["m"]
                        m_acquire(u)
                        for i in range(4):
                            ins = TR(m_bank(u)[:, P * i:P * i + P], PART[:, P * i:P * i + P], IDN[:, :])
                        ins.then_inc(m_ready[u % 2], 1)
                elif k == "T":
                    ntiles += 1
                    t = s["t"]
                    pe.wait_ge(xn_ready, s["n"] + 1)
                    for q in (0, 1):
                        u = s["m"] + q
                        m_acquire(u)
                        for i in range(4):
                            f = 4 * q + i
                            ins = TR(m_bank(u)[:, P * i:P * i + P], ACC[:, t, P * f:P * f + P], IDN[:, :])
                        ins.then_inc(m_ready[u % 2], 1)
                elif k == "A":
                    for part in s["parts"]:
                        if len(s["parts"]) == 1:
                            pe.wait_ge(h_lo, ntiles if part else TT * s["norm"] + 2)
                    if len(s["parts"]) == 2:
                        pe.wait_ge(h_lo, ntiles)
                    order = [(i, part) for i in (0, 1) for part in s["parts"]]
                    for i, part in order:
                        a, j = s["a"] + i, s["j"] + i
                        if part == s["parts"][0] and 0 in s["parts"]:
                            a_acquire(a)
                            pe.wait_ge(w_lo, j + 1)
                        c0, c1 = RANGE[part]
                        wh = WH[:, j % RING, :].rearrange("p (k n) -> p k n", k=KD)
                        wl = WL[:, j % RING, :].rearrange("p (k n) -> p k n", k=KD)
                        for kt in range(KD):
                            ins = split3(a_bank(a)[:, c0:c1], (wh[:, kt, :], wl[:, kt, :]), (HH[:, kt, c0:c1], HL[:, kt, c0:c1]),
                                         kt == 0, kt == KD - 1)
                        if part == 1:
                            ins.then_inc(a_ready[a % 2], 1)
                elif k == "rg":
                    j = s["tile"]
                    if j == 0:
                        pe.wait_ge(const_in[7], 16 * 8)
                    for d in (0, 1):
                        pe.wait_ge(xc_ready, 2 * j + d + 1)
                        for w in (0, 1):
                            a = s["a"] + 2 * d + w
                            a_acquire(a)
                            for c0, c1 in RANGE:
                                ins = MM(a_bank(a)[:, c0:c1], BD[:, w, d, j, :], XC[d][:, c0:c1], start=True, stop=True)
                            ins.then_inc(a_ready[a % 2], 1)
                elif k == "B":
                    b, t, nb, what = s["b"], s["t"], s["nb"], s["what"]
                    b_acquire(b)
                    if what == "wout":
                        pe.wait_ge(mix_lo, 4)
                        if s["ph"] == 3:
                            upto(pe, m_free, PV_M[-2])
                            upto(pe, m_free, PV_M[-1])
                    elif what == "qkv":
                        pe.wait_ge(h_lo, 2 * TT + (t + 1 if nb == 0 else TT))
                    for kt in range(KD):
                        j = s["j"] + kt // 2
                        if t == 0 and kt % 2 == 0:
                            pe.wait_ge(w_lo, j + 1)
                        cols = slice(512 * (kt % 2), 512 * (kt % 2) + 512)
                        hs = slice(t * P, t * P + P)
                        ins = split3(PS[:, 4 + b % 2, :], (HH[:, kt, hs], HL[:, kt, hs]), (WH[:, j % RING, cols], WL[:, j % RING, cols]),
                                     kt == 0, kt == KD - 1)
                    ins.then_inc(b_ready[b % 2], 1)
                elif k == "G2":
                    t = s["t"]
                    if t == 0:
                        pe.wait_ge(a_lo, 32 * s["layer"] + 4 * s["c"] + 4)
                        pe.wait_ge(w_lo, s["j"] + 4)
                    for nh in (0, 1):
                        b = s["b"] + nh
                        b_acquire(b)
                        for kt in range(4):
                            j, slot = s["j"] + kt, (32 * s["layer"] + 4 * s["c"] + kt) % AS
                            hs, cols = slice(t * P, t * P + P), slice(512 * nh, 512 * nh + 512)
                            ins = split3(PS[:, 4 + b % 2, :], (AH[:, slot, hs], AL[:, slot, hs]),
                                         (WH[:, j % RING, cols], WL[:, j % RING, cols]), kt == 0, kt == 3)
                        ins.then_inc(b_ready[b % 2], 1)
                elif k == "gmlp":
                    u = s["m"]
                    m_acquire(u)
                    pe.wait_ge(wst_in, 16)
                    for h in range(4):
                        ins = TR(m_bank(u)[:, P * h:P * h + P], WSR[:, h, :], IDN[:, :])
                    ins.then_inc(m_ready[u % 2], 1)
                    pe.wait_ge(m_free[u % 2], u // 2 + 1)
                    pe.wait_ge(vn_ready, TT)
                    for h in range(4):
                        a = s["a"] + h
                        a_acquire(a)
                        for (c0, c1), (t0, t1) in zip(RANGE, ((0, 2), (2, TT))):
                            ins = MM(a_bank(a)[:, c0:c1], WST[:, h, :], V[:, t0:t1, P * h:P * h + P], start=True, stop=True)
                        ins.then_inc(a_ready[a % 2], 1)
                    gmlp_a = s["a"]
                elif k == "ya":
                    for h in (2, 3):
                        a = gmlp_a + h
                        pe.wait_ge(a_free[a % 2], a // 2 + 1)
                    for t in range(TT):
                        u = s["m"] + t
                        m_acquire(u)
                        for h in range(4):
                            ins = TR(m_bank(u)[:, P * h:P * h + P], U[:, t, P * h:P * h + P], IDN[:, :])
                        ins.then_inc(m_ready[u % 2], 1)
                elif k == "kcache":
                    u = s["m"]
                    m_acquire(u)
                    pe.wait_ge(l1_in[2], 16)
                    pe.wait_ge(l1_in[3], 16)
                    for g in range(NKV):
                        ins = TR(m_bank(u)[:, P * g:P * g + P], KDUP[:, g, :, :].rearrange("p s d -> p (s d)"), IDN[:, :])
                    ins.then_inc(m_ready[u % 2], 1)
                elif k == "qkvT":
                    u, nb = s["m"], s["nb"]
                    m_acquire(u)
                    if s["t"]:
                        pe.wait_ge(qk_ready, LAT * nb + s["t"])
                    else:
                        upto(pe, b_free, s["group"])
                    for i in range(4):
                        src = QK1[:, P * i:P * i + P] if nb < 2 else KDUP[:, i, :, :].rearrange("p s d -> p (s d)")
                        ins = TR(m_bank(u)[:, P * i:P * i + P], src, IDN[:, :])
                    ins.then_inc(m_ready[u % 2], 1)
                elif k == "S":
                    i, g, t = s["n"], s["g"], s["t"]
                    keys = key_tiles(t)
                    if i == 0:
                        upto(pe, m_free, QKV_M - 1)
                        upto(pe, m_free, QKV_M)
                    for h in range(4):
                        if i:
                            pe.wait_ge(z_ready, 4 * (i - 1) + h + 1)
                        lo = 64 * (h % 2)
                        q = QT[lo:lo + 64, 2 * g + h // 2, t * P:t * P + P]
                        n = P * (len(keys) - 1) if t else P
                        ins = MM(PS[:, h, 0:n], q, KT[lo:lo + 64, g, P * keys[0]:P * keys[0] + n], start=True, stop=True)
                        if t:
                            ins = MM(PS[:, h, n:n + P], q, KT[lo:lo + 64, g, 5 * P:6 * P], start=True, stop=True)
                        ins.then_inc(s_done, 1)
                elif k == "PV":
                    i, g, t = s["n"], s["g"], s["t"]
                    keys = key_tiles(t)
                    base = pv_steps(i)
                    u = s["m"]
                    m_acquire(u)
                    pe.wait_ge(p_ready, 4 * (i + 1))
                    if i == 0:
                        pe.wait_ge(v_done, TT)
                        pe.wait_ge(l1_in[4], 16)

                    def transposed(kt):
                        q = base + kt
                        if q >= 2:
                            pe.wait_ge(pt_ready, q - 1)
                        for h in range(4):
                            ins = TR(PS[:, 4 + q % 2, P * h:P * h + P], Z[:, i % 2, h, P * kt:P * kt + P], IDN[:, :])
                        ins.then_inc(pt_mm[q % 2], 1)

                    def values(kt):
                        pe.wait_ge(pt_ready, base + kt + 1)
                        pt = PT[kt].rearrange("p (a s n) -> p s a n", a=2, s=2)
                        for par in (0, 1):
                            ins = MM(PS[64 * par:64 * par + 64, 6 + u % 2, 0:256], VV[:, keys[kt], HD * g:HD * g + HD],
                                     pt[:, par, :, :], start=(kt == 0), stop=(kt == len(keys) - 1))
                        return ins

                    transposed(0)
                    for kt in range(1, len(keys)):
                        transposed(kt)
                        values(kt - 1)
                    values(len(keys) - 1).then_inc(m_ready[u % 2], 1)


_W = ["x_prompt", "x_sample", "c", "cache_k", "cache_v", "c_ctx", "w_mod", "b_mod", "norm_mix_post", "norm_ffn_post",
      "w_ffn_in", "w_ffn_out", "w_in_even", "w_out_even", "gmlp_norm", "gmlp_ws", "rg_wa", "rg_wi", "w_qkv", "w_out_odd",
      "attn_sink"]


def shape_constants():
    i = np.arange(P)
    sel = np.zeros((P, 2, P), np.float32)
    for v in (0, 1):
        sel[v::32, v, :] = 1.0
    prev = np.where(i[None, :] >= i[:, None], 0.0, -1e30)
    nxt = np.where(i[None, :] <= i[:, None], 0.0, -1e30)
    zero = np.zeros((P, P))
    mask = np.concatenate([prev, zero, nxt, zero, prev, zero, zero], 1).astype(np.float32)
    nf, grid = HD // 4, 64
    inv = np.float32(10000.0) ** (-np.arange(nf, dtype=np.float32) / nf)
    pos = np.arange(LAT * P)
    row, col = (pos // grid).astype(np.float32)[:, None] * inv, (pos % grid).astype(np.float32)[:, None] * inv
    cos = np.concatenate([np.cos(row), np.cos(row), np.cos(col), np.cos(col)], 1)
    sin = np.concatenate([-np.sin(row), np.sin(row), -np.sin(col), np.sin(col)], 1)
    rope = np.stack([cos, sin]).reshape(2, LAT, P, HD).transpose(2, 0, 1, 3).reshape(P, -1).astype(np.float32)
    return dict(ident=np.eye(P, dtype=np.float32), sel=sel, mask=mask, rope=np.ascontiguousarray(rope))


def kernel(**inputs):
    import concourse.bacc as bacc
    from concourse.bass_utils import run_bass_kernel_spmd

    arrays = {n: np.ascontiguousarray(inputs[n]) for n in _W}
    arrays.update(shape_constants())
    rows = [inputs[n] for n in ("norm_mix_pre", "norm_ffn_pre", "rg_conv_w", "rg_conv_b", "rg_ba", "rg_bi", "rg_lambda",
                                "state_rglru", "gmlp_bs")]
    arrays["sheet"] = np.ascontiguousarray(np.concatenate([np.asarray(r).reshape(-1, P) for r in rows], 0))
    outs = dict(y_prompt=(1, P, D), y_sample=(1, LAT * P, D), new_state=(1, 1, 2, 512), new_k=(1, 1, P, NKV, HD),
                new_v=(1, 1, P, NKV, HD))
    nc = bacc.Bacc("TRN2", target_bir_lowering=False, num_devices=1)
    A = {n: nc.dram_tensor(f"in_{n}", a.shape, mybir.dt.from_np(a.dtype), kind="ExternalInput").ap() for n, a in arrays.items()}
    for n, shape in outs.items():
        A[n] = nc.dram_tensor(f"out_{n}", shape, mybir.dt.float32, kind="ExternalOutput").ap()
    A["new_state"] = A["new_state"].rearrange("a b d (j p) -> p (a b d j)", p=P)
    A["new_k"], A["new_v"] = A["new_k"][0, 0], A["new_v"][0, 0]
    hybrid_step(nc, A)
    r = run_bass_kernel_spmd(nc, [{f"in_{n}": a for n, a in arrays.items()}], core_ids=[0])
    return tuple(r.results[0][f"out_{n}"] for n in outs)
```

```python
from contextlib import ExitStack

import numpy as np

import concourse.bass as bass
from concourse import mybir

P = 128
D = 1024
KD = D // P
TT = 5
TOK = TT * P
LAT = 4
FF = 4 * D
FC = FF // 512
HD = 64
NKV = 4
N_MOD = 6
RAWN = 2
RING = 6
AS = 6
EPS = 1e-6
G_MIX, G_FFN, CW, CB, BA, BI, LAM, ST, BS, NCOL = 0, 16, 32, 64, 72, 80, 88, 96, 104, 108


def schedule():
    loads, steps = [], []
    n = dict(block=0, a=0, b=0, m=0)

    def load(kind, **spec):
        blocks = 0 if kind == "mod" else 2
        loads.append(dict(kind=kind, first=n["block"], blocks=blocks, m=n["m"], **spec))
        n["block"] += blocks
        return len(loads) - 1

    def step(kind, uses_a=0, uses_b=0, uses_m=0, frees=0, **spec):
        s = dict(kind=kind, a=n["a"], b=n["b"], m=n["m"], split=[], **spec)
        n["a"] += uses_a
        n["b"] += uses_b
        n["m"] += uses_m
        if frees:
            done = n.setdefault("freed", 0)
            s["split"] = list(range(done + RING, done + RING + frees))
            n["freed"] = done + frees
        s["frees"] = frees
        steps.append(s)
        return s

    pend = []

    def flush():
        if pend:
            layer, c, half, k = pend.pop()
            step("modfin", uses_m=1 if c not in (2, 5) else 2, layer=layer, c=c, half=half, n=k)

    cb = [0]

    def mod(layer, c, half):
        flush()
        ld = load("mod", layer=layer, c=c, half=half, kh=0, n=cb[0])
        load("mod", layer=layer, c=c, half=half, kh=1, n=cb[0])
        step("mod", uses_m=1, layer=layer, c=c, half=half, ld=ld, n=cb[0])
        pend.append((layer, c, half, cb[0]))
        cb[0] += 1

    def apair(what, tile, src, col, part=None, ld=None, norm=0):
        if ld is None:
            ld = load("acols", src=src, col=col)
        j = loads[ld]["first"]
        if part == 0:
            return step("A", uses_a=0, what=what, tile=tile, j=j, parts=(0,), fin=False, norm=norm), ld
        return step("A", uses_a=2, frees=2, what=what, tile=tile, j=j, parts=(1,) if part == 1 else (0, 1), fin=True, norm=norm), ld

    def bgroup(what, nb, t, j, ph=None):
        step("B", uses_b=1, frees=4 if t == TT - 1 else 0, what=what, nb=nb, t=t, j=j, ph=ph)

    def bload(src, nb):
        ld = load("bcols", src=src, col=512 * nb, kh=0)
        load("bcols", src=src, col=512 * nb, kh=1)
        return loads[ld]["first"]

    tcount = [0]

    def P_(ph, t, parts=("post", "pre")):
        for part in parts:
            if (part == "post" and ph) or (part == "pre" and ph < 4):
                step(part, ph=ph, t=t, yb=n["b"] - 1)

    def T_(ph, t):
        step("T", uses_m=2, ph=ph, t=t, n=tcount[0])
        tcount[0] += 1

    def ffn(layer, fillers):
        fill = list(fillers)
        ph = 1 if layer == 0 else 3

        def tiles(nt, part=None, ld=None):
            return apair("ffn", nt + 32 * layer, ("w1", layer), nt * P, part, ld, ph)[1]

        ld = tiles(0, 0)
        mod(*fill.pop(0))
        T_(ph, TT - 1)
        tiles(0, 1, ld)
        tiles(2)
        for c in range(FC):
            if c + 1 < FC:
                tiles(4 * c + 4)
            l0 = load("w2", layer=layer, c=c, kh=0)
            load("w2", layer=layer, c=c, kh=1)
            j = loads[l0]["first"]
            last = c == FC - 1
            for t in range(TT):
                step("G2", uses_b=2, frees=4 if t == TT - 1 else 0, layer=layer, c=c, t=t, j=j, ph=ph + 1)
                if t in (0, 2) and fill and not last:
                    mod(*fill.pop(0))
                if last:
                    if t == 0:
                        flush()
                    if t > 1 and ph + 1 < 4:
                        T_(ph + 1, t - 2)
                    P_(ph + 1, t)
            if c + 1 < FC:
                tiles(4 * c + 6)
        assert not fill and not pend

    step("sheet", uses_m=1)
    for t in range(TT):
        P_(0, t)
    for c in (0, 1):
        for half in (0, 1):
            mod(0, c, half)
    flush()
    for t in range(TT):
        T_(0, t)
        if t in (1, 2, 3):
            steps[-1]["split"] = [2 * t - 2, 2 * t - 1]
        if t == 2:
            ld = apair("xr", 0, ("w_in",), 1536, 0)[1]
    apair("xr", 0, ("w_in",), 1536, 1, ld)
    apair("xr", 2, ("w_in",), 1536 + 256)
    apair("gate", 0, ("w_in",), 1024)
    step("rg", uses_a=4, tile=0)
    step("root", tile=0)
    apair("gate", 2, ("w_in",), 1024 + 256)
    j = bload(("w_in",), 1)
    for t in range(TT):
        bgroup("v", 1, t, j)
        if t in (0, 2):
            mod(0, 3, t // 2)
        if t == 0:
            step("rg", uses_a=4, tile=1)
        if t == 1:
            step("root", tile=1)
        if t == 4:
            step("rg", uses_a=4, tile=2)
    j = bload(("w_in",), 0)
    for t in range(TT):
        bgroup("u", 0, t, j)
        if t == 0:
            step("root", tile=2)
            mod(0, 4, 0)
        if t == 2:
            mod(0, 4, 1)
            step("rg", uses_a=4, tile=3)
        if t == 3:
            step("root", tile=3)
            step("vnorm", uses_m=1)
    flush()
    step("gmlp", uses_a=4)
    step("ya", uses_m=TT)
    for nb in (0, 1):
        j = bload(("w_out_even",), nb)
        for t in range(TT):
            bgroup("wout", nb, t, j, ph=1)
            if nb == 0 and t in (0, 2):
                mod(0, 2, t // 2)
            if nb == 0 and t == 4:
                flush()
            if nb:
                if t > 1:
                    T_(1, t - 2)
                P_(1, t, ("post",))
                if t == TT - 1:
                    T_(1, TT - 2)
                P_(1, t, ("pre",))
    ffn(0, [(0, 5, 0), (0, 5, 1)] + [(1, c, h) for c in (0, 1, 3, 4) for h in (0, 1)])
    step("l1in")
    k_use = None
    for nb in (2, 0, 1):
        j = bload(("w_qkv",), nb)
        for t in range(TT):
            bgroup("qkv", nb, t, j)
            group = n["b"] - 1
            if nb == 2 and t < 2:
                T_(2, TT - 2 + t)
            if nb == 2 and t:
                k_use = n["m"]
                step("kT", uses_m=1, t=t - 1, group=group - 1)
            if nb == 0 and t == 0:
                step("kT", uses_m=1, t=TT - 1)
                step("kT", uses_m=1, t=TT)
            step("rope", nb=nb, t=t, group=group, pu=k_use - 1 if nb == 2 and t > 2 else None)
        if nb == 2:
            step("kvout", group=group - t)
    units = [(g, t) for t in range(TT) for g in range(NKV)]

    def unit(kind, i, **uses):
        step(kind, n=i, g=units[i][0], t=units[i][1], **uses)

    unit("Q", 0, uses_m=1)
    for i in range(len(units)):
        unit("S", i)
        if i + 1 < len(units):
            unit("Q", i + 1, uses_m=1)
        if i > 1:
            unit("PV", i - 2, uses_m=1)
        unit("softmax", i)
    for i in (len(units) - 2, len(units) - 1):
        unit("PV", i, uses_m=1)
    for nb in (0, 1):
        j = bload(("w_out_odd",), nb)
        for t in range(TT):
            bgroup("wout", nb, t, j, ph=3)
            if nb == 0 and t in (0, 2):
                mod(1, 2, t // 2)
            if nb == 0 and t == 4:
                flush()
            if nb:
                if t > 1:
                    T_(3, t - 2)
                P_(3, t, ("post",))
                if t == TT - 1:
                    T_(3, TT - 2)
                P_(3, t, ("pre",))
    ffn(1, [(1, 5, 0), (1, 5, 1)])
    mod_step = {ld: i for i, s in enumerate(steps) if s["kind"] == "mod" for ld in (s["ld"], s["ld"] + 1)}
    owner = [i for i, ld in enumerate(loads) for _ in range(ld["blocks"])]
    pending = [(i, j) for i, s in enumerate(steps) for j in s["split"] if j < n["block"]]
    for s in steps:
        s["split"] = []
    at = 0
    for i, j in pending:
        at = max([at, i] + [mod_step[ld] for ld in range(max(0, owner[j] - 9), owner[j] - 1) if ld in mod_step])
        steps[at]["split"].append((j, steps[i]))
    return loads, steps


def key_tiles(t):
    if t == 0:
        return [0]
    return [TT] + list(range(max(1, t - 1), min(LAT, t + 1) + 1))


def key_slot(k):
    return {0: 0, TT: 1}.get(k, k + 1)


def mask_start(t):
    return 0 if t < 2 else 3 * P


def pv_steps(n):
    return sum(len(key_tiles(t)) for t in range(TT) for _ in range(NKV) if t * NKV + _ < n)


def hybrid_step(nc, A):
    f32, f32r, bf16 = mybir.dt.float32, mybir.dt.float32r, mybir.dt.bfloat16
    ALU, ACT, AX = mybir.AluOpType, mybir.ActivationFunctionType, mybir.AxisListType
    LOADS, STEPS = schedule()

    ctx = ExitStack()
    with ctx:
        def sb(name, shape, dt=f32):
            return ctx.enter_context(nc.sbuf_tensor(name, shape, dt))

        def alias(name, shape, dt=f32):
            with nc.sbuf_tensor(name, shape, dt) as t:
                return t

        def sem(name):
            return ctx.enter_context(nc.semaphore(name))

        X = sb("X", [P, TT, D])
        EARLY_H = alias("EARLY_H", [P, 4, 2048])
        HH = sb("HH", [P, KD, TOK], f32r)
        HL = sb("HL", [P, KD, TOK], f32r)
        WH = sb("WH", [P, RING, 1024], f32r)
        WL = sb("WL", [P, RING, 1024], f32r)
        RAW = sb("RAW", [P, RAWN, 2048])
        MX = alias("MX", [P, 2 * AS * TOK])
        AH = sb("AH", [P, AS, TOK], f32r)
        AL = sb("AL", [P, AS, TOK], f32r)
        ACC = sb("ACC", [P, TT, D])
        GG = sb("GG", [P, 4, D])
        QS = alias("QS", [P, 2, 512], f32r)
        HF = sb("HF", [P, KD, P])
        PART = sb("PART", [P, 512])
        BMR = sb("BMR", [1, 512])
        IDN = sb("IDN", [P, P])
        SEL = sb("SEL", [P, 2, P])
        CC = sb("CC", [P, 2, KD])
        CSG = sb("CSG", [P, 2, KD])
        CL = sb("CL", [P, KD, 32])
        MODC = sb("MODC", [P, 2, 4, KD, 2])
        PC = sb("PC", [P, NCOL])
        BC = sb("BC", [P, 2, N_MOD * KD])
        STAT = sb("STAT", [P, TT, 6])
        EPSC = sb("EPSC", [P, 1])
        LG = sb("LG", [P, 4, 8])
        NCL = sb("NCL", [P, 8])
        NS = sb("NS", [P, 8])
        SV = sb("SV", [P, TT, 3])
        AST = sb("AST", [P, 2, 6, 4])
        SINK = sb("SINK", [P, 16])

        PS = ctx.enter_context(nc.psum_tensor("PS", [P, 8, 512], f32))
        PSF = PS[:, :, :].rearrange("p b n -> p (b n)")

        U = ACC[:, :, 0:512]
        V = ACC[:, :, 512:1024]
        XR = MX[:, 0:2560].rearrange("p (j n) -> p j n", j=4)
        GT = MX[:, 2560:5120].rearrange("p (j n) -> p j n", j=4)
        BD = MX[:, 5120:7168].rearrange("p (w d j n) -> p w d j n", w=2, d=2, j=4)
        GMN = MX[:, 7168:7680]
        GGF = GG[:, :, :].rearrange("p v n -> p (v n)")
        RG = [GGF[:, i * TOK:(i + 1) * TOK] for i in range(6)]
        RR, II, TH = RG[0:2], RG[2:4], RG[4:6]
        WST, WSR = HF[:, 0:4, :], HF[:, 4:8, :]
        SHEET, SHEET2 = HF[0:NCOL, 0, :], HF[0:2 * N_MOD * KD, 1, :]
        KH = AH[:, :, :].rearrange("p s n -> p (s n)")[:, 0:3072].rearrange("p (g n) -> p g n", g=NKV)
        KL = AL[:, :, :].rearrange("p s n -> p (s n)")[:, 0:3072].rearrange("p (g n) -> p g n", g=NKV)
        QK2 = GGF[:, 0:512]
        ROPE = GGF[:, 512:1024].rearrange("p (w t n) -> p w t n", w=2, t=LAT)
        KTOK = GGF[:, 1024:2048].rearrange("p (s n) -> p s n", s=4)
        Z = GGF.rearrange("p (u h n) -> p u h n", u=2, h=4)
        XCB = sb("XCB", [P, 2 * TOK])
        XC = [XCB[:, i * TOK:(i + 1) * TOK] for i in range(2)]
        JUNK = XCB[:, 0:D]
        MASK = XCB[:, 0:896]
        PT_LOAD = next(i for i, ld in enumerate(LOADS) if ld.get("src") == ("w_out_odd",)) + 1
        PT = [RAW[:, PT_LOAD % RAWN, 512 * i:512 * i + 512] for i in range(4)]

        def vv(t):
            c = AS * TOK * (t // 3) + 3072 + 256 * (t % 3)
            return MX[:, c:c + 256]

        def k_tok(t):
            return KTOK[:, {0: 0, TT: 1}.get(t, 2 + t % 2), :]

        EARLY = {i: EARLY_H[:, i - RAWN, :] for i in range(RAWN, RAWN + 4)}

        early_in = [sem(f"early_in{i}") for i in range(4)]
        raw_in = [sem(f"raw_in{i}") for i in range(RAWN)]
        const_in = [sem(f"const_in{i}") for i in range(14)]
        w_hi, w_lo, mod_read = sem("w_hi"), sem("w_lo"), sem("mod_read")
        a_ready = [sem(f"a_ready{i}") for i in range(2)]
        a_free = [sem(f"a_free{i}") for i in range(2)]
        b_ready = [sem(f"b_ready{i}") for i in range(2)]
        b_free = [sem(f"b_free{i}") for i in range(2)]
        m_ready = [sem(f"m_ready{i}") for i in range(2)]
        m_free = [sem(f"m_free{i}") for i in range(2)]
        bmr_in = sem("bmr_in")
        gg_in = [sem(f"gg_in{i}") for i in range(2)]
        dve_done, act_done = sem("dve_done"), sem("act_done")
        cl_ready, lam_e, lam_ready, csg = sem("cl_ready"), sem("lam_e"), sem("lam_ready"), sem("csg")
        consts_made = sem("consts_made")
        ysum, xsum, x_new, xn_ready = sem("ysum"), sem("xsum"), sem("x_new"), sem("xn_ready")
        h_hi = sem("h_hi")
        h_lo = [sem(f"h_lo{i}") for i in range(2)]
        sq_ready, a_hi, a_lo = sem("sq_ready"), sem("a_hi"), sem("a_lo")
        xc_ready, ea_ready, t_ready, root_ready, rg_done = (sem("xc_ready"), sem("ea_ready"), sem("t_ready"), sem("root_ready"),
                                                            sem("rg_done"))
        vs_ready, vn_ready, wst_in = sem("vs_ready"), sem("vn_ready"), sem("wst_in")
        mix_hi, mix_lo = sem("mix_hi"), sem("mix_lo")
        l1_in = [sem(f"l1_in{i}") for i in range(4)]
        mod_done = sem("mod_done")
        k_out, k_hi, q_hi = sem("k_out"), sem("k_hi"), sem("q_hi")
        qk_ready, v_done = sem("qk_ready"), sem("v_done")
        s_done, z_ready, e_ready, p_ready, nm_ready, es_ready = (sem("s_done"), sem("z_ready"), sem("e_ready"),
                                                                 sem("p_ready"), sem("nm_ready"), sem("es_ready"))
        pt_mm = [sem(f"pt_mm{i}") for i in range(2)]
        pt_ready = sem("pt_ready")
        stored = sem("stored")

        def upto(eng, pair, n):
            eng.wait_ge(pair[n % 2], n // 2 + 1)

        def input_ready(eng, n):
            for half in (0, 1):
                eng.wait_ge(h_lo[half], n)

        CHUNK_B = [s["b"] + 1 for s in STEPS if s["kind"] == "G2" and s["t"] == TT - 1]
        PV_M = [s["m"] for s in STEPS if s["kind"] == "PV"]
        KT_M = [s["m"] for s in STEPS if s["kind"] == "kT"][-1]
        GATE_M = [s["m"] for s in STEPS if s["kind"] == "modfin" and s["c"] in (2, 5)]
        PART_M = [s["m"] + (s["c"] in (2, 5)) for s in STEPS if s["kind"] == "modfin"]
        MOD_M = [s["m"] for s in STEPS if s["kind"] == "mod"]
        YA_M = [s["m"] for s in STEPS if s["kind"] == "ya"][0]
        Q_M = [s["m"] for s in STEPS if s["kind"] == "Q"]
        QKV_B = [s["b"] for s in STEPS if s["kind"] == "B" and s["what"] == "qkv"][-1]

        def step_done(eng, s):
            if s["kind"] == "A":
                upto(eng, a_ready, s["a"] + 1)
            elif s["kind"] == "B":
                upto(eng, b_ready, s["b"])
            elif s["kind"] == "G2":
                upto(eng, b_ready, s["b"] + 1)

        def w_view(ld, b):
            place = raw(ld)
            k = LOADS[ld]["kind"]
            if k == "acols":
                return place.rearrange("p (k n) -> p k n", k=KD)[:, :, P * b:P * b + P]
            return place[:, 1024 * b:1024 * b + 1024]

        def ring_view(buf, ld, j):
            k = LOADS[ld]["kind"]
            if k == "acols":
                return buf[:, j % RING, :].rearrange("p (k n) -> p k n", k=KD)
            return buf[:, j % RING, :]

        BLOCK_LOAD = {}
        for i, ld in enumerate(LOADS):
            for b in range(ld["blocks"]):
                BLOCK_LOAD[ld["first"] + b] = (i, b)

        def raw_arrived(eng, ld):
            if ld in EARLY:
                eng.wait_ge(early_in[ld - RAWN], 16)
            else:
                eng.wait_ge(raw_in[ld % RAWN], 16 * ((ld - (len(EARLY) if ld >= RAWN else 0)) // RAWN + 1))

        def dram_view(ld):
            k = ld["kind"]
            if k == "mod":
                w = A["w_mod"][ld["layer"]].rearrange("(p k) n -> p k n", k=KD)
                c0 = ld["c"] * D + ld["half"] * 512
                return w[:, 4 * ld["kh"]:4 * ld["kh"] + 4, c0:c0 + 512]
            if k == "w2":
                w = A["w_ffn_out"][ld["layer"]].rearrange("(k p) n -> p k n", p=P)
                k0 = 4 * ld["c"] + 2 * ld["kh"]
                return w[:, k0:k0 + 2, :]
            src = ld["src"]
            w = A["w_ffn_in"][src[1]] if src[0] == "w1" else {
                "w_in": A["w_in_even"], "w_out_even": A["w_out_even"], "w_qkv": A["w_qkv"],
                "w_out_odd": A["w_out_odd"]}[src[0]][0]
            w = w.rearrange("(k p) n -> p k n", p=P)
            if k == "acols":
                return w[:, :, ld["col"]:ld["col"] + 256]
            return w[:, 4 * ld["kh"]:4 * ld["kh"] + 4, ld["col"]:ld["col"] + 512]

        def raw(i):
            return EARLY[i] if i in EARLY else RAW[:, i % RAWN, :]

        def raw_dst(i, ld):
            k = {"mod": 4, "w2": 2, "acols": KD, "bcols": 4}[ld["kind"]]
            return raw(i).rearrange("p (k n) -> p k n", k=k)

        def a_bank(a):
            base = 1024 * (a % 2) + 256
            return PSF[:, base:base + TOK]

        def m_bank(u):
            return PS[:, 6 + u % 2, :]

        def modc(layer, c):
            return MODC[:, layer, {0: 0, 1: 1, 3: 2, 4: 3}[c], :, :]

        block = ctx.enter_context(nc.Block())

        @block.sync
        def _(sp):
            sp.dma_start(X[:, 0, :], A["x_prompt"][0]).then_inc(const_in[0], 16)
            for i, ld in enumerate(LOADS):
                if i in EARLY:
                    sp.dma_start(raw_dst(i, ld), dram_view(ld)).then_inc(early_in[i - RAWN], 16)
                    continue
                if i >= RAWN:
                    old = LOADS[i - RAWN - (len(EARLY) if i < 2 * RAWN + len(EARLY) else 0)]
                    if old["kind"] == "mod" and old["kh"] == 0:
                        sp.wait_ge(mod_read, old["n"] + 1)
                    elif old["kind"] == "mod":
                        upto(sp, m_ready, old["m"])
                    else:
                        sp.wait_ge(w_lo, old["first"] + 2)
                    if i == PT_LOAD + RAWN:
                        upto(sp, m_ready, PV_M[-1])
                sp.dma_start(raw_dst(i, ld), dram_view(ld)).then_inc(raw_in[i % RAWN], 16)
            for t in range(TT):
                sp.wait_ge(x_new, 3 * TT + t + 1)
                dst = A["y_prompt"][0] if t == 0 else A["y_sample"][0, (t - 1) * P:t * P, :]
                sp.dma_start(dst, X[:, t, :]).then_inc(stored, 16)
            sp.wait_ge(stored, 16 * (2 + TT))
            sp.wait_ge(k_out, 16)

        @block.scalar
        def _(act):
            own = [0]

            def link(ins):
                own[0] += 1
                ins.then_inc(act_done, 1)
                act.wait_ge(act_done, own[0])

            xs = A["x_sample"][0].rearrange("(t p) n -> p t n", p=P)
            act.dma_start(SHEET, A["sheet"]).then_inc(const_in[2], 16)
            act.dma_start(SHEET2, A["b_mod"].rearrange("l (k n) -> (l k) n", n=P)).then_inc(const_in[10], 16)
            act.dma_start(IDN[:, :], A["ident"]).then_inc(const_in[5], 16)
            act.dma_start(CC[:, 0, :], A["c_ctx"].rearrange("(p k) -> p k", k=KD)).then_inc(const_in[3], 16)
            act.dma_start(CC[:, 1, :], A["c"][0].rearrange("(p k) -> p k", k=KD)).then_inc(const_in[4], 16)
            act.dma_start(X[:, 1:TT, :], xs).then_inc(const_in[1], 16)
            act.dma_start(SEL[:, :, :], A["sel"]).then_inc(const_in[6], 16)
            act.dma_start(GMN, A["gmlp_norm"].broadcast_to([P, 512])).then_inc(const_in[8], 16)
            act.dma_start(SINK[:, :], A["attn_sink"].broadcast_to([P, 16])).then_inc(const_in[9], 16)
            act.wait_ge(consts_made, 3)
            for w, name in enumerate(("rg_wa", "rg_wi")):
                for d in (0, 1):
                    for odd in (0, 1):
                        act.dma_start(BD[64 * odd:64 * odd + 64, w, d, :, 64 * odd:64 * odd + 64],
                                      A[name][0, d].rearrange("(j o) i n -> o i j n", o=2)[odd]).then_inc(const_in[7], 16)
            act.wait_ge(const_in[3], 16)
            act.wait_ge(const_in[4], 16)
            nc.scalar.activation(CSG[:, :, :], CC[:, :, :], ACT.Sigmoid).then_inc(csg, 1)
            act.wait_ge(lam_e, 1)
            nc.scalar.activation(LG[:, 1, :], LG[:, 0, :], ACT.Exp).then_inc(lam_e, 1)

            def split(s):
                for j, freed_by in s["split"]:
                    ld, b = BLOCK_LOAD[j]
                    raw_arrived(act, ld)
                    step_done(act, freed_by)
                    nc.scalar.copy(ring_view(WH, ld, j), w_view(ld, b)).then_inc(w_hi, 1)

            ngate = 0
            for s in STEPS:
                k = s["kind"]
                if k == "mod":
                    if s["c"] in (2, 5):
                        if ngate:
                            upto(act, m_ready, GATE_M[ngate - 1] + 1)
                        ngate += 1
                        c0 = s["c"] * D + 512 * s["half"]
                        act.dma_start(BMR[:, :], A["b_mod"][s["layer"]:s["layer"] + 1, c0:c0 + 512]).then_inc(bmr_in, 16)
                        half, kind = s["half"], 0 if s["c"] == 2 else 2
                        if s["layer"] == 1:
                            for i in (18, 19):
                                upto(act, m_ready, PV_M[i])
                        elif kind:
                            act.wait_ge(x_new, TT)
                        else:
                            act.wait_ge(rg_done, 4)
                        g = A["norm_mix_post" if kind == 0 else "norm_ffn_post"][s["layer"]:s["layer"] + 1, 512 * half:512 * half + 512]
                        for v in (0, 1):
                            act.dma_start(GG[:, kind + v, 512 * half:512 * half + 512], g.broadcast_to([P, 512])).then_inc(gg_in[half], 16)
                if k == "post":
                    ph, t = s["ph"], s["t"]
                    b = s["yb"]
                    act.wait_ge(b_free[b % 2], b // 2 + 1)
                    if ph % 2 == 0:
                        act.wait_ge(a_lo, 16 * ph)
                    link(nc.scalar.activation(JUNK, ACC[:, t, :], ACT.Square, accum_out=STAT[:, t, 0:1]))
                    nc.scalar.activation(STAT[:, t, 1:2], STAT[:, t, 0:1], ACT.Sqrt, scale=1.0 / D, bias=EPSC[:, :])\
                        .then_inc(ysum, 1)
                elif k == "pre":
                    ph, t = s["ph"], s["t"]
                    if ph:
                        act.wait_ge(x_new, (ph - 1) * TT + t + 1)
                    else:
                        act.wait_ge(const_in[0] if t == 0 else const_in[1], 16)
                        act.wait_ge(consts_made, 3)
                    link(nc.scalar.activation(JUNK, X[:, t, :], ACT.Square, accum_out=STAT[:, t, 3:4]))
                    nc.scalar.activation(STAT[:, t, 4:5], STAT[:, t, 3:4], ACT.Sqrt, scale=1.0 / D, bias=EPSC[:, :])\
                        .then_inc(xsum, 1)
                elif k == "T":
                    ph, t, n_ = s["ph"], s["t"], s["n"]
                    u, v = s["m"] + 1, min(s["t"], 1)
                    layer, off = ph // 2, 0 if ph % 2 == 0 else 2
                    if n_:
                        act.wait_ge(h_lo[1], n_)
                    act.wait_ge(mod_done, 2 * ph + 2)
                    act.wait_ge(m_ready[u % 2], u // 2 + 1)
                    for i in range(4):
                        f = 4 + i
                        ins = nc.scalar.activation(HF[:, f, :], m_bank(u)[:, P * i:P * i + P], ACT.Identity,
                                                   scale=MODC[:, layer, off + 1, f, v:v + 1], bias=MODC[:, layer, off, f, v:v + 1])
                    ins.then_inc(m_free[u % 2], 1)
                    cols = slice(t * P, t * P + P)
                    act.wait_ge(m_free[(u - 1) % 2], (u - 1) // 2 + 1)
                    nc.scalar.copy(HH[:, 0:4, cols], HF[:, 0:4, :]).then_inc(h_hi, 1)
                    act.wait_ge(m_free[u % 2], u // 2 + 1)
                    nc.scalar.copy(HH[:, 4:8, cols], HF[:, 4:8, :]).then_inc(h_hi, 1)
                elif k == "A" and s["fin"]:
                    if s["what"] == "xr" and s["tile"] == 2:
                        input_ready(act, TT)
                        act.dma_start(WSR, A["gmlp_ws"][0].rearrange("h p q -> p h q")).then_inc(wst_in, 16)
                    for i in (0, 1):
                        a, tile = s["a"] + i, s["tile"] + i
                        act.wait_ge(a_ready[a % 2], a // 2 + 1)
                        if s["what"] == "xr":
                            nc.scalar.copy(XR[:, tile, :], a_bank(a)).then_inc(a_free[a % 2], 1)
                        elif s["what"] == "gate":
                            nc.scalar.activation(GT[:, tile, :], a_bank(a), ACT.Gelu_apprx_tanh).then_inc(a_free[a % 2], 1)
                        else:
                            if tile:
                                act.wait_ge(sq_ready, tile)
                            nc.scalar.activation(XC[0], a_bank(a), ACT.Relu).then_inc(a_free[a % 2], 1)
                            slot, c = tile % AS, (tile - AS) // 4
                            act.wait_ge(sq_ready, tile + 1)
                            if tile >= AS:
                                upto(act, b_ready, CHUNK_B[c])
                            nc.scalar.copy(AH[:, slot, :], XC[1]).then_inc(a_hi, 1)
                elif k == "rg":
                    j = s["tile"]
                    if j:
                        act.wait_ge(rg_done, j)
                    for d in (0, 1):
                        for w, dst, col in ((0, RR[d], BA), (1, II[d], BI)):
                            a = s["a"] + 2 * d + w
                            act.wait_ge(a_ready[a % 2], a // 2 + 1)
                            nc.scalar.activation(dst, a_bank(a), ACT.Sigmoid, bias=PC[:, col + 4 * d + j:col + 4 * d + j + 1])\
                                .then_inc(a_free[a % 2], 1)
                    act.wait_ge(a_free[0], (s["a"] + 3) // 2 + 1)
                    act.wait_ge(a_free[1], (s["a"] + 3) // 2 + 1)
                    act.wait_ge(lam_ready, 1)
                    for d in (0, 1):
                        c = 4 * d + j
                        nc.scalar.activation(TH[d], RR[d], ACT.Tanh, scale=NCL[:, c:c + 1]).then_inc(t_ready, 1)
                        act.wait_ge(t_ready, 2 * j + d + 1)
                        nc.scalar.activation(RR[d], RR[d], ACT.Exp, scale=LG[:, 3, c:c + 1]).then_inc(ea_ready, 1)
                    for d in (0, 1):
                        nc.scalar.activation(TH[d], TH[d], ACT.Sqrt).then_inc(root_ready, 1)
                elif k == "B":
                    b = s["b"]
                    bank = PS[:, 4 + b % 2, :]
                    if s["what"] == "v":
                        act.wait_ge(b_ready[b % 2], b // 2 + 1)
                        nc.scalar.activation(V[:, s["t"], :], bank, ACT.Gelu_apprx_tanh).then_inc(b_free[b % 2], 1)
                        act.wait_ge(b_free[b % 2], b // 2 + 1)
                        link(nc.scalar.activation(U[:, s["t"], :], V[:, s["t"], :], ACT.Square, accum_out=SV[:, s["t"], 0:1]))
                    elif s["what"] == "u":
                        act.wait_ge(b_ready[b % 2], b // 2 + 1)
                        nc.scalar.activation(U[:, s["t"], :], bank, ACT.Gelu_apprx_tanh).then_inc(b_free[b % 2], 1)
                    elif s["what"] == "qkv" and s["nb"] == 2:
                        act.wait_ge(b_ready[b % 2], b // 2 + 1)
                        nc.scalar.copy(vv(s["t"]), PS[:, 4 + b % 2, 256:512]).then_inc(v_done, 1)
                elif k == "l1in":
                    upto(act, b_ready, CHUNK_B[FC - 1])
                    act.dma_start(MASK, A["mask"]).then_inc(l1_in[0], 16)
                    act.dma_start(ROPE, A["rope"].rearrange("p (w t n) -> p w t n", w=2, t=LAT)).then_inc(l1_in[1], 16)
                    act.dma_start(k_tok(TT), A["cache_k"][0, 0].rearrange("p g d -> p (g d)")).then_inc(l1_in[2], 16)
                    act.dma_start(vv(TT), A["cache_v"][0, 0].rearrange("p g d -> p (g d)")).then_inc(l1_in[3], 16)
                elif k == "vnorm":
                    act.wait_ge(act_done, own[0])
                    nc.scalar.activation(SV[:, :, 1:2], SV[:, :, 0:1], ACT.Sqrt, scale=1.0 / 512, bias=EPSC[:, :]).then_inc(vs_ready, 1)
                elif k == "gmlp":
                    act.wait_ge(rg_done, 4)
                    with nc.allow_non_contiguous_dma(reason="1024 state values, features on the partitions"):
                        act.dma_start(A["new_state"], NS[:, :]).then_inc(stored, 16)
                    upto(act, b_ready, s["b"] - 1)
                    for j in range(4):
                        nc.scalar.copy(HH[:, 4 + j, :], GT[:, j, :]).then_inc(mix_hi, 1)
                elif k == "ya":
                    for t in range(TT):
                        u = s["m"] + t
                        act.wait_ge(m_ready[u % 2], u // 2 + 1)
                        nc.scalar.copy(HH[:, 0:4, t * P:t * P + P], m_bank(u).rearrange("p (k n) -> p k n", k=4)).then_inc(mix_hi, 1)
                elif k == "kT":
                    u, c = s["m"], P * key_slot(s["t"])
                    act.wait_ge(m_ready[u % 2], u // 2 + 1)
                    nc.scalar.copy(KH[:, :, c:c + P], m_bank(u).rearrange("p (g n) -> p g n", g=NKV)).then_inc(k_hi, 1)
                elif k == "Q":
                    u, i = s["m"], s["n"]
                    act.wait_ge(m_ready[u % 2], u // 2 + 1)
                    if i == 0:
                        input_ready(act, 3 * TT)
                    if i > 1:
                        act.wait_ge(s_done, 4 * (i - 1))
                    nc.scalar.copy(QS[:, i % 2, :], m_bank(u)).then_inc(q_hi, 1)
                elif k == "kvout":
                    upto(act, b_free, s["group"])
                    act.dma_start(A["new_k"].rearrange("p g d -> p (g d)"), k_tok(0)).then_inc(k_out, 16)
                    act.wait_ge(v_done, 1)
                    act.dma_start(A["new_v"].rearrange("p g d -> p (g d)"), vv(0)).then_inc(stored, 16)
                elif k == "softmax":
                    i, g, z = s["n"], s["g"], s["n"] % 2
                    nk = P * len(key_tiles(s["t"]))
                    act.wait_ge(nm_ready, i + 1)
                    for h in range(4):
                        nc.scalar.activation(Z[:, z, h, 0:nk], Z[:, z, h, 0:nk], ACT.Exp, scale=0.125,
                                             bias=AST[:, z, 1, h:h + 1], accum_out=AST[:, z, 2, h:h + 1]).then_inc(e_ready, 1)
                    nc.scalar.activation(AST[:, z, 3, :], AST[:, z, 4, :], ACT.Exp).then_inc(es_ready, 1)
                elif k == "PV":
                    i, g, t = s["n"], s["g"], s["t"]
                    nk = len(key_tiles(t))
                    base = pv_steps(i)
                    for kt in range(nk):
                        q = base + kt
                        act.wait_ge(pt_mm[q % 2], q // 2 + 1)
                        if i:
                            upto(act, m_ready, PV_M[i - 1])
                        elif kt == 0:
                            act.wait_ge(w_lo, LOADS[PT_LOAD]["first"] + 2)
                        nc.scalar.copy(PT[kt], PS[:, 4 + q % 2, :]).then_inc(pt_ready, 1)
                    u = s["m"]
                    act.wait_ge(m_ready[u % 2], u // 2 + 1)
                    nc.scalar.copy(HH[:, 2 * g:2 * g + 2, t * P:t * P + P], m_bank(u)[:, 0:256].rearrange("p (k n) -> p k n", k=2))\
                        .then_inc(mix_hi, 1)
                split(s)

        @block.gpsimd
        def _(pool):
            for s in STEPS:
                if s["kind"] == "T":
                    t = s["t"]
                    pool.wait_ge(h_hi, 2 * s["n"] + 2)
                    cols = slice(t * P, t * P + P)
                    nc.gpsimd.tensor_tensor(HL[:, 4:8, cols], HF[:, 4:8, :], HH[:, 4:8, cols].bitcast(f32), ALU.subtract)\
                        .then_inc(h_lo[1], 1)
                for j, _ in s["split"]:
                    ld, b = BLOCK_LOAD[j]
                    pool.wait_ge(w_hi, j + 1)
                    nc.gpsimd.tensor_tensor(ring_view(WL, ld, j), w_view(ld, b), ring_view(WH, ld, j).bitcast(f32),
                                            ALU.subtract).then_inc(w_lo, 1)

        @block.vector
        def _(dve):
            own = [0]
            V_ = nc.vector

            def link(ins):
                own[0] += 1
                ins.then_inc(dve_done, 1)
                dve.wait_ge(dve_done, own[0])

            V_.memset(EPSC[:, :], EPS).then_inc(consts_made, 1)
            V_.memset(BD, 0.0).then_inc(consts_made, 1)
            V_.memset(CL[:, :, :], 0.0).then_inc(consts_made, 1)
            dve.wait_ge(csg, 1)
            dve.wait_ge(consts_made, 3)
            V_.tensor_tensor(CL[:, :, 0:2].rearrange("p k v -> p v k"), CC[:, :, :], CSG[:, :, :], ALU.mult).then_inc(cl_ready, 1)

            def conv(j):
                if j == 0:
                    upto(dve, a_free, 2)
                    upto(dve, a_free, 3)
                for d in (0, 1):
                    w = lambda k: PC[:, CW + 16 * d + 4 * k + j:CW + 16 * d + 4 * k + j + 1]
                    link(V_.tensor_scalar(XC[d], XR[:, j, :], w(3 if d == 0 else 0),
                                          PC[:, CB + 4 * d + j:CB + 4 * d + j + 1], ALU.mult, ALU.add))
                    for sh in (1, 2, 3):
                        for lo, hi in ((0, P), (P, TOK)):
                            dst, src = (slice(lo + sh, hi), slice(lo, hi - sh)) if d == 0 else (slice(lo, hi - sh), slice(lo + sh, hi))
                            ins = V_.scalar_tensor_tensor(XC[d][:, dst], XR[:, j, src], w(3 - sh if d == 0 else sh),
                                                          XC[d][:, dst], ALU.mult, ALU.add)
                            if sh == 3 and lo:
                                ins.then_inc(xc_ready, 1)
                            else:
                                link(ins)

            def scans(d, j):
                seg = lambda lo, hi: slice(lo, hi) if d == 0 else slice(hi - 1, lo - 1 if lo else None, -1)
                link(V_.tensor_tensor_scan(TH[d][:, seg(0, P)], RR[d][:, seg(0, P)], II[d][:, seg(0, P)], 0.0, ALU.mult, ALU.add))
                link(V_.tensor_tensor_scan(TH[d][:, seg(P, TOK)], RR[d][:, seg(P, TOK)], II[d][:, seg(P, TOK)],
                                           PC[:, ST + 4 * d + j:ST + 4 * d + j + 1], ALU.mult, ALU.add))
                end = P - 1 if d == 0 else 0
                V_.tensor_copy(NS[:, 4 * d + j:4 * d + j + 1], TH[d][:, end:end + 1]).then_inc(dve_done, 1)
                own[0] += 1

            def normalise(i, t):
                z = i % 2
                nk = P * len(key_tiles(t))
                dve.wait_ge(e_ready, 4 * (i + 1))
                dve.wait_ge(es_ready, i + 1)
                link(V_.tensor_tensor(AST[:, z, 2, :], AST[:, z, 2, :], AST[:, z, 3, :], ALU.add))
                link(V_.reciprocal(AST[:, z, 5, :], AST[:, z, 2, :]))
                for h in range(4):
                    V_.tensor_scalar(Z[:, z, h, 0:nk], Z[:, z, h, 0:nk], AST[:, z, 5, h:h + 1], None, ALU.mult).then_inc(p_ready, 1)

            def remainder(i):
                u, g, t = PV_M[i], i % NKV, i // NKV
                dve.wait_ge(mix_hi, TT + 4 + i + 1)
                cols = slice(t * P, t * P + P)
                V_.tensor_tensor(HL[:, 2 * g:2 * g + 2, cols], m_bank(u)[:, 0:256].rearrange("p (k n) -> p k n", k=2),
                                 HH[:, 2 * g:2 * g + 2, cols].bitcast(f32), ALU.subtract).then_inc(m_free[u % 2], 1)

            nmod = nchain = nkt = nscale = 0
            fin_g = 0
            prev_t = None
            for s in STEPS:
                k = s["kind"]
                if k == "sheet":
                    u = s["m"]
                    dve.wait_ge(m_ready[u % 2], u // 2 + 1)
                    V_.tensor_copy(BC[:, :, :].rearrange("p l k -> p (l k)"), m_bank(u)[:, P:P + 2 * N_MOD * KD])
                    V_.tensor_copy(PC[:, :], m_bank(u)[:, 0:NCOL]).then_inc(m_free[u % 2], 1)
                    dve.wait_ge(m_free[u % 2], u // 2 + 1)
                    lam = PC[:, LAM:LAM + 8]
                    link(V_.tensor_scalar(LG[:, 1, :], lam, -1.0, None, ALU.mult))
                    V_.tensor_tensor(LG[:, 0, :], lam, LG[:, 1, :], ALU.min).then_inc(lam_e, 1)
                    dve.wait_ge(lam_e, 2)
                    e, v, w, acc = LG[:, 1, :], LG[:, 0, :], LG[:, 2, :], LG[:, 3, :]
                    link(V_.tensor_scalar(w, e, 2.0, None, ALU.add))
                    link(V_.reciprocal(w, w))
                    link(V_.tensor_tensor(v, e, w, ALU.mult))
                    link(V_.tensor_tensor(w, v, v, ALU.mult))
                    link(V_.memset(acc, 1.0 / 17))
                    for q in (15, 13, 11, 9, 7, 5, 3, 1):
                        link(V_.tensor_tensor(acc, acc, w, ALU.mult))
                        link(V_.tensor_scalar(acc, acc, 1.0 / q, None, ALU.add))
                    link(V_.tensor_tensor(acc, acc, v, ALU.mult))
                    link(V_.tensor_scalar(v, lam, 0.0, 8.0, ALU.min, ALU.mult))
                    link(V_.scalar_tensor_tensor(acc, acc, -16.0, v, ALU.mult, ALU.add))
                    V_.tensor_scalar(NCL[:, :], acc, -0.5, None, ALU.mult).then_inc(lam_ready, 1)
                elif k == "mod":
                    u = s["m"]
                    dve.wait_ge(m_ready[u % 2], u // 2 + 1)
                    if s["n"]:
                        upto(dve, m_ready, PART_M[s["n"] - 1])
                    V_.tensor_copy(PART[:, :], m_bank(u)).then_inc(m_free[u % 2], 1)
                elif k == "modfin":
                    layer, c, half = s["layer"], s["c"], s["half"]
                    if c in (2, 5):
                        fin_g += half == 0
                        for v in (0, 1):
                            u = s["m"] + v
                            dve.wait_ge(m_ready[u % 2], u // 2 + 1)
                            dve.wait_ge(gg_in[half], 32 * fin_g)
                            g = GG[:, (0 if c == 2 else 2) + v, 512 * half:512 * half + 512]
                            V_.tensor_tensor(g, m_bank(u), g, ALU.mult).then_inc(m_free[u % 2], 1)
                    else:
                        u = s["m"]
                        dve.wait_ge(m_ready[u % 2], u // 2 + 1)
                        src = m_bank(u).rearrange("p (i g w) -> p i w g", i=4, g=4)[:, :, 0:2, :]
                        dst = modc(layer, c)[:, 4 * half:4 * half + 4, :]
                        V_.tensor_reduce(dst, src, AX.X, ALU.add).then_inc(m_free[u % 2], 1)
                        dve.wait_ge(m_free[u % 2], u // 2 + 1)
                        k0 = KD * c + 4 * half
                        bias = BC[:, layer, k0:k0 + 4].unsqueeze(2).broadcast_to([P, 4, 2])
                        link(V_.tensor_tensor(dst, dst, bias, ALU.add))
                        if c in (1, 4):
                            g0 = (G_MIX if c == 1 else G_FFN) + 8 * layer + 4 * half
                            V_.scalar_tensor_tensor(dst[:, :, 0], dst[:, :, 0], 1.0, PC[:, g0:g0 + 4], ALU.add, ALU.mult)
                            V_.scalar_tensor_tensor(dst[:, :, 1], dst[:, :, 1], 1.0, PC[:, g0:g0 + 4], ALU.add, ALU.mult)\
                                .then_inc(mod_done, 1)
                            nscale += 1
                            dve.wait_ge(mod_done, nscale)
                elif k == "post":
                    ph, t = s["ph"], s["t"]
                    nchain += 1
                    dve.wait_ge(ysum, nchain)
                    link(V_.reciprocal(STAT[:, t, 2:3], STAT[:, t, 1:2]))
                    gain = GG[:, (0 if ph in (1, 3) else 2) + (t > 0), :]
                    link(V_.scalar_tensor_tensor(ACC[:, t, :], ACC[:, t, :], STAT[:, t, 2:3], gain, ALU.mult, ALU.mult))
                    V_.tensor_tensor(X[:, t, :], X[:, t, :], ACC[:, t, :], ALU.add).then_inc(x_new, 1)
                elif k == "pre":
                    ph, t = s["ph"], s["t"]
                    dve.wait_ge(xsum, ph * TT + t + 1)
                    link(V_.reciprocal(STAT[:, t, 5:6], STAT[:, t, 4:5]))
                    V_.tensor_scalar(ACC[:, t, :], X[:, t, :], STAT[:, t, 5:6], None, ALU.mult).then_inc(xn_ready, 1)
                elif k == "T":
                    ph, t, u0 = s["ph"], s["t"], s["m"]
                    layer, off = ph // 2, 0 if ph % 2 == 0 else 2
                    v = 0 if t == 0 else 1
                    if s["n"]:
                        dve.wait_ge(h_lo[0], s["n"])
                    dve.wait_ge(m_ready[u0 % 2], u0 // 2 + 1)
                    for f in range(4):
                        ins = V_.tensor_scalar(HF[:, f, :], m_bank(u0)[:, P * f:P * f + P], MODC[:, layer, off + 1, f, v:v + 1],
                                               MODC[:, layer, off, f, v:v + 1], ALU.mult, ALU.add)
                    ins.then_inc(m_free[u0 % 2], 1)
                    cols = slice(t * P, t * P + P)
                    dve.wait_ge(h_hi, 2 * s["n"] + 1)
                    V_.tensor_tensor(HL[:, 0:4, cols], HF[:, 0:4, :], HH[:, 0:4, cols].bitcast(f32), ALU.subtract).then_inc(h_lo[0], 1)
                elif k == "A":
                    if s["what"] == "xr" and s["fin"] and s["tile"] == 2:
                        conv(0)
                    if s["what"] == "ffn" and s["fin"]:
                        for tile in (s["tile"], s["tile"] + 1):
                            slot = tile % AS
                            a = s["a"] + tile - s["tile"]
                            dve.wait_ge(a_free[a % 2], a // 2 + 1)
                            if tile:
                                dve.wait_ge(a_hi, tile)
                                dve.wait_ge(a_lo, tile)
                            V_.tensor_tensor(XC[1], XC[0], XC[0], ALU.mult).then_inc(sq_ready, 1)
                            dve.wait_ge(a_hi, tile + 1)
                            V_.tensor_tensor(AL[:, slot, :], XC[1], AH[:, slot, :].bitcast(f32), ALU.subtract).then_inc(a_lo, 1)
                elif k == "rg":
                    j = s["tile"]
                    for d in (0, 1):
                        a = s["a"] + 2 * d + 1
                        upto(dve, a_free, a)
                        link(V_.tensor_tensor(II[d], II[d], XC[d], ALU.mult))
                    if j < 3:
                        conv(j + 1)
                elif k == "root":
                    j = s["tile"]
                    for d in (0, 1):
                        dve.wait_ge(root_ready, 2 * j + d + 1)
                        link(V_.scalar_tensor_tensor(TH[d], RR[d], 1.0, TH[d], ALU.add, ALU.mult))
                        link(V_.tensor_tensor(II[d], II[d], TH[d], ALU.mult))
                        scans(d, j)
                    link(V_.tensor_tensor(TH[0], TH[0], TH[1], ALU.add))
                    V_.tensor_tensor(GT[:, j, :], GT[:, j, :], TH[0], ALU.mult).then_inc(rg_done, 1)
                elif k == "B":
                    b, t, nb, what = s["b"], s["t"], s["nb"], s["what"]
                    bank = PS[:, 4 + b % 2, :]
                    if what == "wout":
                        dve.wait_ge(b_ready[b % 2], b // 2 + 1)
                        V_.tensor_copy(ACC[:, t, 512 * nb:512 * nb + 512], bank).then_inc(b_free[b % 2], 1)
                elif k == "rope":
                    t, nb, b = s["t"], s["nb"], s["group"]
                    bank = PS[:, 4 + b % 2, :]
                    heads = 8 if nb < 2 else NKV
                    n = heads * HD
                    dst = ACC[:, t, 512 * nb:512 * nb + 512] if nb < 2 else k_tok(t)
                    if nb == 2:
                        dve.wait_ge(v_done, t + 1)
                    upto(dve, b_ready, b)
                    if s["pu"] is not None:
                        upto(dve, m_ready, s["pu"])
                    if t == 0:
                        V_.tensor_copy(dst, bank[:, 0:n]).then_inc(b_free[b % 2], 1)
                    else:
                        if nb == 2 and t == 1:
                            dve.wait_ge(l1_in[1], 16)
                        hv = lambda x: x[:, 0:n].rearrange("p (h d) -> p h d", h=heads)
                        parts = lambda x, o: x.rearrange("p (h b o f) -> p h b o f", b=2, o=2, f=16)[:, :, :, o, :]
                        link(V_.tensor_tensor(hv(dst), hv(bank), ROPE[:, 0, t - 1, :].unsqueeze(1).broadcast_to([P, heads, HD]), ALU.mult))
                        for o in (0, 1):
                            sn = parts(ROPE[:, 1, t - 1, :], o).broadcast_to([P, heads, 2, 16])
                            ins = V_.tensor_tensor(parts(QK2[:, 0:n], o), parts(bank[:, 0:n], 1 - o), sn, ALU.mult)
                        ins.then_inc(b_free[b % 2], 1)
                        upto(dve, b_free, b)
                        V_.tensor_tensor(dst, dst, QK2[:, 0:n], ALU.add).then_inc(qk_ready, 1)
                elif k == "kT":
                    u, c = s["m"], P * key_slot(s["t"])
                    nkt += 1
                    dve.wait_ge(k_hi, nkt)
                    V_.tensor_tensor(KL[:, :, c:c + P], m_bank(u).rearrange("p (g n) -> p g n", g=NKV),
                                     KH[:, :, c:c + P].bitcast(f32), ALU.subtract).then_inc(m_free[u % 2], 1)
                elif k == "Q":
                    u, i = s["m"], s["n"]
                    dve.wait_ge(q_hi, i + 1)
                    V_.tensor_tensor(QS[64:128, i % 2, :], m_bank(u)[64:128, :], QS[64:128, i % 2, :].bitcast(f32),
                                     ALU.subtract).then_inc(m_free[u % 2], 1)
                elif k == "G2":
                    t, c = s["t"], s["c"]
                    for nh in (0, 1):
                        b = s["b"] + nh
                        bank = PS[:, 4 + b % 2, :]
                        acc = ACC[:, t, 512 * nh:512 * nh + 512]
                        dve.wait_ge(b_ready[b % 2], b // 2 + 1)
                        if c:
                            V_.tensor_tensor(acc, acc, bank, ALU.add).then_inc(b_free[b % 2], 1)
                        else:
                            V_.tensor_copy(acc, bank).then_inc(b_free[b % 2], 1)
                elif k == "vnorm":
                    u = s["m"]
                    dve.wait_ge(m_ready[u % 2], u // 2 + 1)
                    V_.tensor_copy(WST, m_bank(u).rearrange("p (h n) -> p h n", h=4)).then_inc(m_free[u % 2], 1)
                    dve.wait_ge(vs_ready, 1)
                    dve.wait_ge(const_in[8], 16)
                    link(V_.reciprocal(SV[:, :, 2:3], SV[:, :, 1:2]))
                    for t in range(TT):
                        V_.scalar_tensor_tensor(V[:, t, :], V[:, t, :], SV[:, t, 2:3], GMN, ALU.mult, ALU.mult).then_inc(vn_ready, 1)
                elif k == "gmlp":
                    upto(dve, b_free, s["b"] - 1)
                    for h in range(4):
                        a = s["a"] + h
                        dve.wait_ge(a_ready[a % 2], a // 2 + 1)
                        uh = U[:, :, P * h:P * h + P]
                        V_.scalar_tensor_tensor(uh, a_bank(a).rearrange("p (t n) -> p t n", t=TT), PC[:, BS + h:BS + h + 1], uh,
                                                ALU.add, ALU.mult).then_inc(a_free[a % 2], 1)
                        dve.wait_ge(mix_hi, h + 1)
                        V_.tensor_tensor(HL[:, 4 + h, :], GT[:, h, :], HH[:, 4 + h, :].bitcast(f32), ALU.subtract).then_inc(mix_lo, 1)
                elif k == "ya":
                    for t in range(TT):
                        u = s["m"] + t
                        dve.wait_ge(mix_hi, 4 + t + 1)
                        cols = slice(t * P, t * P + P)
                        V_.tensor_tensor(HL[:, 0:4, cols], m_bank(u).rearrange("p (k n) -> p k n", k=4),
                                         HH[:, 0:4, cols].bitcast(f32), ALU.subtract).then_inc(m_free[u % 2], 1)
                elif k == "softmax":
                    i, t, z = s["n"], s["t"], s["n"] % 2
                    nk = P * len(key_tiles(t))
                    m0 = mask_start(t)
                    if i == 0:
                        dve.wait_ge(k_out, 16)
                        dve.wait_ge(l1_in[0], 16)
                        dve.wait_ge(const_in[9], 16)
                    if i >= 2:
                        upto(dve, pt_mm, pv_steps(i - 1) - 1)
                    for h in range(4):
                        dve.wait_ge(s_done, 4 * i + h + 1)
                        V_.tensor_tensor_reduce(out=Z[:, z, h, 0:nk], in0=PS[:, h, 0:nk], in1=MASK[:, m0:m0 + nk], scale=1.0,
                                                scalar=-3.0e38, op0=ALU.add, op1=ALU.max, accum_out=AST[:, z, 0, h:h + 1])\
                            .then_inc(z_ready, 1)
                    dve.wait_ge(z_ready, 4 * (i + 1))
                    snk = SINK[:, 4 * s["g"]:4 * s["g"] + 4]
                    link(V_.scalar_tensor_tensor(AST[:, z, 0, :], AST[:, z, 0, :], 0.125, snk, ALU.mult, ALU.max))
                    link(V_.tensor_scalar(AST[:, z, 1, :], AST[:, z, 0, :], -1.0, None, ALU.mult))
                    V_.tensor_tensor(AST[:, z, 4, :], snk, AST[:, z, 1, :], ALU.add).then_inc(nm_ready, 1)
                    if i:
                        normalise(i - 1, prev_t)
                    if i > 1:
                        remainder(i - 2)
                    prev_t = t
                elif k == "PV":
                    i = s["n"]
                    if i == TT * NKV - 2:
                        normalise(TT * NKV - 1, prev_t)
                    if i >= TT * NKV - 2:
                        remainder(i)

        @block.tensor
        def _(pe):
            MM = nc.tensor.matmul
            TR = nc.tensor.transpose

            def split3(out, w, x, first, last):
                (wh, wl), (xh, xl) = w, x
                MM(out, wh, xh, start=first, stop=False)
                MM(out, wh, xl, start=False, stop=False)
                return MM(out, wl, xh, start=False, stop=last)

            def a_acquire(a):
                if a >= 2:
                    pe.wait_ge(a_free[a % 2], a // 2)

            def b_acquire(b):
                if b >= 2:
                    pe.wait_ge(b_free[b % 2], b // 2)

            def m_acquire(u):
                if u >= 2:
                    pe.wait_ge(m_free[u % 2], u // 2)

            RANGE = ((0, 256), (256, TOK))
            ntiles = ngate = 0
            pe.wait_ge(const_in[5], 16)
            for s in STEPS:
                k = s["kind"]
                if k == "sheet":
                    pe.wait_ge(const_in[2], 16)
                    u = s["m"]
                    pe.wait_ge(const_in[10], 16)
                    TR(m_bank(u)[:, 0:NCOL], SHEET, IDN[0:NCOL, 0:NCOL])
                    nb = 2 * N_MOD * KD
                    TR(m_bank(u)[:, P:P + nb], SHEET2, IDN[0:nb, 0:nb]).then_inc(m_ready[u % 2], 1)
                elif k == "mod":
                    u = s["m"]
                    m_acquire(u)
                    if s["n"] == 0:
                        pe.wait_ge(cl_ready, 1)
                    for kh in (0, 1):
                        ld = s["ld"] + kh
                        raw_arrived(pe, ld)
                        rv = raw(ld).rearrange("p (k n) -> p k n", k=4)
                        for kt in range(4):
                            ins = MM(PS[32 * kt:32 * kt + 32, 6 + u % 2, :], CL[:, 4 * kh + kt, :], rv[:, kt, :],
                                     start=(kh == 0), stop=(kh == 1))
                        if kh == 0:
                            ins.then_inc(mod_read, 1)
                    ins.then_inc(m_ready[u % 2], 1)
                elif k == "modfin":
                    upto(pe, m_free, MOD_M[s["n"]])
                    if s["c"] in (2, 5):
                        ngate += 1
                        pe.wait_ge(bmr_in, 16 * ngate)
                        if s["c"] == 2 and s["layer"] == 0 and s["half"] == 0:
                            pe.wait_ge(const_in[6], 16)
                        for v in (0, 1):
                            u = s["m"] + v
                            m_acquire(u)
                            MM(m_bank(u), SEL[:, v, :], PART[:, :], start=True, stop=False)
                            MM(m_bank(u), SEL[0:1, 0, :], BMR[:, :], start=False, stop=True).then_inc(m_ready[u % 2], 1)
                    else:
                        u = s["m"]
                        m_acquire(u)
                        for i in range(4):
                            ins = TR(m_bank(u)[:, P * i:P * i + P], PART[:, P * i:P * i + P], IDN[:, :])
                        ins.then_inc(m_ready[u % 2], 1)
                elif k == "T":
                    ntiles += 1
                    t = s["t"]
                    pe.wait_ge(xn_ready, s["n"] + 1)
                    for q in (0, 1):
                        u = s["m"] + q
                        m_acquire(u)
                        for i in range(4):
                            f = 4 * q + i
                            ins = TR(m_bank(u)[:, P * i:P * i + P], ACC[:, t, P * f:P * f + P], IDN[:, :])
                        ins.then_inc(m_ready[u % 2], 1)
                elif k == "A":
                    for part in s["parts"]:
                        if len(s["parts"]) == 1:
                            input_ready(pe, ntiles if part else TT * s["norm"] + 2)
                    if len(s["parts"]) == 2:
                        input_ready(pe, ntiles)
                    order = [(i, part) for i in (0, 1) for part in s["parts"]]
                    for i, part in order:
                        a, j = s["a"] + i, s["j"] + i
                        if part == s["parts"][0] and 0 in s["parts"]:
                            a_acquire(a)
                            pe.wait_ge(w_lo, j + 1)
                        c0, c1 = RANGE[part]
                        wh = WH[:, j % RING, :].rearrange("p (k n) -> p k n", k=KD)
                        wl = WL[:, j % RING, :].rearrange("p (k n) -> p k n", k=KD)
                        for kt in range(KD):
                            ins = split3(a_bank(a)[:, c0:c1], (wh[:, kt, :], wl[:, kt, :]), (HH[:, kt, c0:c1], HL[:, kt, c0:c1]),
                                         kt == 0, kt == KD - 1)
                        if part == 1:
                            ins.then_inc(a_ready[a % 2], 1)
                elif k == "rg":
                    j = s["tile"]
                    if j == 0:
                        pe.wait_ge(const_in[7], 16 * 8)
                    for d in (0, 1):
                        pe.wait_ge(xc_ready, 2 * j + d + 1)
                        for w in (0, 1):
                            a = s["a"] + 2 * d + w
                            a_acquire(a)
                            for c0, c1 in RANGE:
                                ins = MM(a_bank(a)[:, c0:c1], BD[:, w, d, j, :], XC[d][:, c0:c1], start=True, stop=True)
                            ins.then_inc(a_ready[a % 2], 1)
                elif k == "B":
                    b, t, nb, what = s["b"], s["t"], s["nb"], s["what"]
                    b_acquire(b)
                    if what == "wout":
                        if s["ph"] == 1 and nb == 0:
                            pe.wait_ge(mix_lo, 4)
                            upto(pe, m_free, YA_M + t)
                        if s["ph"] == 3:
                            upto(pe, m_free, PV_M[-2])
                            upto(pe, m_free, PV_M[-1])
                    elif what == "qkv":
                        input_ready(pe, 2 * TT + (t + 1 if nb == 2 else TT))
                    for kt in range(KD):
                        j = s["j"] + kt // 2
                        if t == 0 and kt % 2 == 0:
                            pe.wait_ge(w_lo, j + 1)
                        cols = slice(512 * (kt % 2), 512 * (kt % 2) + 512)
                        hs = slice(t * P, t * P + P)
                        ins = split3(PS[:, 4 + b % 2, :], (HH[:, kt, hs], HL[:, kt, hs]), (WH[:, j % RING, cols], WL[:, j % RING, cols]),
                                     kt == 0, kt == KD - 1)
                    ins.then_inc(b_ready[b % 2], 1)
                elif k == "G2":
                    t = s["t"]
                    if t == 0:
                        pe.wait_ge(a_lo, 32 * s["layer"] + 4 * s["c"] + 4)
                        pe.wait_ge(w_lo, s["j"] + 4)
                    for nh in (0, 1):
                        b = s["b"] + nh
                        b_acquire(b)
                        for kt in range(4):
                            j, slot = s["j"] + kt, (32 * s["layer"] + 4 * s["c"] + kt) % AS
                            hs, cols = slice(t * P, t * P + P), slice(512 * nh, 512 * nh + 512)
                            ins = split3(PS[:, 4 + b % 2, :], (AH[:, slot, hs], AL[:, slot, hs]),
                                         (WH[:, j % RING, cols], WL[:, j % RING, cols]), kt == 0, kt == 3)
                        ins.then_inc(b_ready[b % 2], 1)
                elif k == "vnorm":
                    u = s["m"]
                    m_acquire(u)
                    pe.wait_ge(wst_in, 16)
                    for h in range(4):
                        ins = TR(m_bank(u)[:, P * h:P * h + P], WSR[:, h, :], IDN[:, :])
                    ins.then_inc(m_ready[u % 2], 1)
                    vnorm_m = u
                elif k == "gmlp":
                    upto(pe, m_free, vnorm_m)
                    pe.wait_ge(vn_ready, TT)
                    for h in range(4):
                        a = s["a"] + h
                        a_acquire(a)
                        for (c0, c1), (t0, t1) in zip(RANGE, ((0, 2), (2, TT))):
                            ins = MM(a_bank(a)[:, c0:c1], WST[:, h, :], V[:, t0:t1, P * h:P * h + P], start=True, stop=True)
                        ins.then_inc(a_ready[a % 2], 1)
                    gmlp_a = s["a"]
                elif k == "ya":
                    for h in (2, 3):
                        a = gmlp_a + h
                        pe.wait_ge(a_free[a % 2], a // 2 + 1)
                    for t in range(TT):
                        u = s["m"] + t
                        m_acquire(u)
                        for h in range(4):
                            ins = TR(m_bank(u)[:, P * h:P * h + P], U[:, t, P * h:P * h + P], IDN[:, :])
                        ins.then_inc(m_ready[u % 2], 1)
                elif k == "kT":
                    u, t = s["m"], s["t"]
                    m_acquire(u)
                    if t == 0:
                        upto(pe, b_free, s["group"])
                    elif t < TT:
                        pe.wait_ge(qk_ready, t)
                    else:
                        pe.wait_ge(l1_in[2], 16)
                    for g in range(NKV):
                        for half in (0, 64):
                            ins = MM(m_bank(u)[half:half + 64, P * g:P * g + P], k_tok(t)[:, HD * g:HD * g + HD], IDN[:, :], start=True, stop=True)
                    ins.then_inc(m_ready[u % 2], 1)
                elif k == "Q":
                    u, g, t = s["m"], s["g"], s["t"]
                    m_acquire(u)
                    if s["n"] == 0:
                        upto(pe, b_free, QKV_B - LAT)
                    if s["n"] == NKV:
                        pe.wait_ge(qk_ready, 3 * LAT)
                    for h in range(4):
                        c = HD * (4 * g + h)
                        for half in (0, 64):
                            ins = MM(m_bank(u)[half:half + 64, P * h:P * h + P], ACC[:, t, c:c + HD], IDN[:, :], start=True, stop=True)
                    ins.then_inc(m_ready[u % 2], 1)
                elif k == "S":
                    i, g, t = s["n"], s["g"], s["t"]
                    if i == 0:
                        upto(pe, m_free, KT_M - 1)
                        upto(pe, m_free, KT_M)
                    upto(pe, m_free, Q_M[i])
                    pieces = {0: [(0, 0, 2)], 1: [(0, 1, 3)], 2: [(0, 1, 4)], 3: [(0, 1, 2), (P, 3, 3)], 4: [(0, 1, 2), (P, 4, 2)]}[t]
                    for h in range(4):
                        if i:
                            pe.wait_ge(z_ready, 4 * (i - 1) + h + 1)
                        q = QS[:, i % 2, P * h:P * h + P]
                        for c, slot, nt in pieces:
                            out, keys = PS[:, h, c:c + P * nt], slice(P * slot, P * (slot + nt))
                            MM(out, q, KH[:, g, keys], start=True, stop=False)
                            ins = MM(out, q, KL[:, g, keys], start=False, stop=True)
                        ins.then_inc(s_done, 1)
                elif k == "PV":
                    i, g, t = s["n"], s["g"], s["t"]
                    keys = key_tiles(t)
                    base = pv_steps(i)
                    u = s["m"]
                    m_acquire(u)
                    pe.wait_ge(p_ready, 4 * (i + 1))
                    if i == 0:
                        upto(pe, b_free, QKV_B - 1)
                        upto(pe, b_free, QKV_B)
                        pe.wait_ge(v_done, TT)
                        pe.wait_ge(l1_in[3], 16)

                    def transposed(kt):
                        q = base + kt
                        if q >= 2:
                            pe.wait_ge(pt_ready, q - 1)
                        for h in range(4):
                            ins = TR(PS[:, 4 + q % 2, P * h:P * h + P], Z[:, i % 2, h, P * kt:P * kt + P], IDN[:, :])
                        ins.then_inc(pt_mm[q % 2], 1)

                    def values(kt):
                        pe.wait_ge(pt_ready, base + kt + 1)
                        pt = PT[kt].rearrange("p (a s n) -> p s a n", a=2, s=2)
                        for par in (0, 1):
                            ins = MM(PS[64 * par:64 * par + 64, 6 + u % 2, 0:256], vv(keys[kt])[:, HD * g:HD * g + HD],
                                     pt[:, par, :, :], start=(kt == 0), stop=(kt == len(keys) - 1))
                        return ins

                    transposed(0)
                    for kt in range(1, len(keys)):
                        transposed(kt)
                        values(kt - 1)
                    values(len(keys) - 1).then_inc(m_ready[u % 2], 1)


_W = ["x_prompt", "x_sample", "c", "cache_k", "cache_v", "c_ctx", "w_mod", "b_mod", "norm_mix_post", "norm_ffn_post",
      "w_ffn_in", "w_ffn_out", "w_in_even", "w_out_even", "gmlp_norm", "gmlp_ws", "rg_wa", "rg_wi", "w_qkv", "w_out_odd",
      "attn_sink"]


def shape_constants():
    i = np.arange(P)
    sel = np.zeros((P, 2, P), np.float32)
    for v in (0, 1):
        sel[v::32, v, :] = 1.0
    prev = np.where(i[None, :] >= i[:, None], 0.0, -1e30)
    nxt = np.where(i[None, :] <= i[:, None], 0.0, -1e30)
    zero = np.zeros((P, P))
    mask = np.concatenate([zero, zero, nxt, zero, prev, zero, nxt], 1).astype(np.float32)
    nf, grid = HD // 4, 64
    inv = np.float32(10000.0) ** (-np.arange(nf, dtype=np.float32) / nf)
    pos = np.arange(LAT * P)
    row, col = (pos // grid).astype(np.float32)[:, None] * inv, (pos % grid).astype(np.float32)[:, None] * inv
    cos = np.concatenate([np.cos(row), np.cos(row), np.cos(col), np.cos(col)], 1)
    sin = np.concatenate([-np.sin(row), np.sin(row), -np.sin(col), np.sin(col)], 1)
    rope = np.stack([cos, sin]).reshape(2, LAT, P, HD).transpose(2, 0, 1, 3).reshape(P, -1).astype(np.float32)
    return dict(ident=np.eye(P, dtype=np.float32), sel=sel, mask=mask, rope=np.ascontiguousarray(rope))


def kernel(**inputs):
    import concourse.bacc as bacc
    from concourse.bass_utils import run_bass_kernel_spmd

    arrays = {n: np.ascontiguousarray(inputs[n]) for n in _W}
    arrays.update(shape_constants())
    rows = [inputs[n] for n in ("norm_mix_pre", "norm_ffn_pre", "rg_conv_w", "rg_conv_b", "rg_ba", "rg_bi", "rg_lambda",
                                "state_rglru", "gmlp_bs")]
    arrays["sheet"] = np.ascontiguousarray(np.concatenate([np.asarray(r).reshape(-1, P) for r in rows], 0))
    outs = dict(y_prompt=(1, P, D), y_sample=(1, LAT * P, D), new_state=(1, 1, 2, 512), new_k=(1, 1, P, NKV, HD),
                new_v=(1, 1, P, NKV, HD))
    nc = bacc.Bacc("TRN2", target_bir_lowering=False, num_devices=1)
    A = {n: nc.dram_tensor(f"in_{n}", a.shape, mybir.dt.from_np(a.dtype), kind="ExternalInput").ap() for n, a in arrays.items()}
    for n, shape in outs.items():
        A[n] = nc.dram_tensor(f"out_{n}", shape, mybir.dt.float32, kind="ExternalOutput").ap()
    A["new_state"] = A["new_state"].rearrange("a b d (j p) -> p (a b d j)", p=P)
    A["new_k"], A["new_v"] = A["new_k"][0, 0], A["new_v"][0, 0]
    hybrid_step(nc, A)
    r = run_bass_kernel_spmd(nc, [{f"in_{n}": a for n, a in arrays.items()}], core_ids=[0])
    return tuple(r.results[0][f"out_{n}"] for n in outs)
```

```python
from contextlib import ExitStack

import numpy as np

import concourse.bass as bass
from concourse import mybir

P = 128
D = 1024
KD = D // P
TT = 5
TOK = TT * P
LAT = 4
FF = 4 * D
FC = FF // 512
HD = 64
NKV = 4
N_MOD = 6
RAWN = 2
RING = 6
AS = 6
EPS = 1e-6
G_MIX, G_FFN, CW, CB, BA, BI, LAM, ST, BS, NCOL = 0, 16, 32, 64, 72, 80, 88, 96, 104, 108


def schedule():
    loads, steps = [], []
    n = dict(block=0, a=0, b=0, m=0)

    def load(kind, **spec):
        blocks = 0 if kind == "mod" else 2
        loads.append(dict(kind=kind, first=n["block"], blocks=blocks, m=n["m"], **spec))
        n["block"] += blocks
        return len(loads) - 1

    def step(kind, uses_a=0, uses_b=0, uses_m=0, frees=0, **spec):
        s = dict(kind=kind, a=n["a"], b=n["b"], m=n["m"], split=[], **spec)
        n["a"] += uses_a
        n["b"] += uses_b
        n["m"] += uses_m
        if frees:
            done = n.setdefault("freed", 0)
            s["split"] = list(range(done + RING, done + RING + frees))
            n["freed"] = done + frees
        s["frees"] = frees
        steps.append(s)
        return s

    pend = []

    def flush():
        if pend:
            layer, c, half, k = pend.pop()
            step("modfin", uses_m=1 if c not in (2, 5) else 2, layer=layer, c=c, half=half, n=k)

    cb = [0]

    def mod(layer, c, half):
        flush()
        ld = load("mod", layer=layer, c=c, half=half, kh=0, n=cb[0])
        load("mod", layer=layer, c=c, half=half, kh=1, n=cb[0])
        step("mod", uses_m=1, layer=layer, c=c, half=half, ld=ld, n=cb[0])
        pend.append((layer, c, half, cb[0]))
        cb[0] += 1

    def apair(what, tile, src, col, part=None, ld=None, norm=0):
        if ld is None:
            ld = load("acols", src=src, col=col)
        j = loads[ld]["first"]
        if part == 0:
            return step("A", uses_a=0, what=what, tile=tile, j=j, parts=(0,), fin=False, norm=norm), ld
        return step("A", uses_a=2, frees=2, what=what, tile=tile, j=j, parts=(1,) if part == 1 else (0, 1), fin=True, norm=norm), ld

    def bgroup(what, nb, t, j, ph=None):
        step("B", uses_b=1, frees=4 if t == TT - 1 else 0, what=what, nb=nb, t=t, j=j, ph=ph)

    def bload(src, nb):
        ld = load("bcols", src=src, col=512 * nb, kh=0)
        load("bcols", src=src, col=512 * nb, kh=1)
        return loads[ld]["first"]

    tcount = [0]

    def P_(ph, t, parts=("post", "pre")):
        for part in parts:
            if (part == "post" and ph) or (part == "pre" and ph < 4):
                step(part, ph=ph, t=t, yb=n["b"] - 1)

    def T_(ph, t, cut=True):
        step("T", uses_m=2, ph=ph, t=t, n=tcount[0])
        if cut:
            cut_()

    def cut_():
        of = next(s for s in reversed(steps) if s["kind"] == "T")
        step("cut", ph=of["ph"], t=of["t"], tm=of["m"], n=tcount[0])
        tcount[0] += 1

    def normed(ph, t):
        if t > 1:
            T_(ph, t - 2, cut=False)
        P_(ph, t, ("post",))
        if t > 1:
            cut_()
        P_(ph, t, ("pre",))

    def ffn(layer, fillers):
        fill = list(fillers)
        ph = 1 if layer == 0 else 3

        def tiles(nt, part=None, ld=None):
            return apair("ffn", nt + 32 * layer, ("w1", layer), nt * P, part, ld, ph)[1]

        T_(ph, TT - 2)
        ld = tiles(0, 0)
        T_(ph, TT - 1)
        mod(*fill.pop(0))
        tiles(0, 1, ld)
        tiles(2)
        for c in range(FC):
            if c + 1 < FC:
                tiles(4 * c + 4)
            l0 = load("w2", layer=layer, c=c, kh=0)
            load("w2", layer=layer, c=c, kh=1)
            j = loads[l0]["first"]
            last = c == FC - 1
            for t in range(TT):
                step("G2", uses_b=2, frees=4 if t == TT - 1 else 0, layer=layer, c=c, t=t, j=j, ph=ph + 1)
                if t in (0, 2) and fill and not last:
                    mod(*fill.pop(0))
                if last:
                    if t == 0:
                        flush()
                    if ph + 1 < 4:
                        normed(ph + 1, t)
                    else:
                        P_(ph + 1, t)
            if c + 1 < FC:
                tiles(4 * c + 6)
        assert not fill and not pend

    mod(0, 0, 0)
    step("sheet", uses_m=1)
    mod(0, 0, 1)
    P_(0, 0)
    mod(0, 1, 0)
    P_(0, 1)
    P_(0, 2)
    mod(0, 1, 1)
    P_(0, 3)
    P_(0, 4)
    flush()
    steps[-1]["split"] = [0, 1]
    for t in range(TT):
        T_(0, t)
        if t == 4:
            steps[-1]["split"] = [2, 3, 4, 5]
        if t == 3:
            ld = apair("xr", 0, ("w_in",), 1536, 0)[1]
    step("lambda")
    apair("xr", 0, ("w_in",), 1536, 1, ld)
    apair("xr", 2, ("w_in",), 1536 + 256)
    apair("gate", 0, ("w_in",), 1024)
    for d in (0, 1):
        step("rg", uses_a=2, tile=0, d=d)
    step("root", tile=0)
    apair("gate", 2, ("w_in",), 1024 + 256)
    halves = [(1, 0), (1, 1), None, (2, 0), (2, 1), None, (3, 0), (3, 1)]
    fill = [(0, 3, 0), (0, 3, 1), (0, 4, 0), (0, 4, 1)]
    for what, nb in (("v", 1), ("u", 0)):
        j = bload(("w_in",), nb)
        for t in range(TT):
            bgroup(what, nb, t, j)
            if what == "u" and t == 2:
                step("vnorm", uses_m=1)
            half = halves.pop(0) if halves else None
            if half:
                tile, d = half
                step("rg", uses_a=2, tile=tile, d=d)
                if d:
                    step("root", tile=tile)
            if t in (0, 2):
                mod(*fill.pop(0))
    flush()
    step("gmlp", uses_a=4)
    step("ya", uses_m=1, t=0)
    step("ya", uses_m=1, t=1)
    for nb in (0, 1):
        j = bload(("w_out_even",), nb)
        for t in range(TT):
            bgroup("wout", nb, t, j, ph=1)
            if nb == 0 and t + 2 < TT:
                step("ya", uses_m=1, t=t + 2)
            if nb == 0 and t in (0, 2):
                mod(0, 2, t // 2)
            if nb == 0 and t == 4:
                flush()
            if nb:
                normed(1, t)
    ffn(0, [(0, 5, 0), (0, 5, 1)] + [(1, c, h) for c in (0, 1, 3, 4) for h in (0, 1)])
    step("l1in")
    k_use = None
    for nb in (2, 0, 1):
        j = bload(("w_qkv",), nb)
        for t in range(TT):
            bgroup("qkv", nb, t, j)
            group = n["b"] - 1
            if nb == 2 and t < 2:
                T_(2, TT - 2 + t)
            if nb == 2 and t:
                k_use = n["m"]
                step("kT", uses_m=1, t=t - 1, group=group - 1)
            if nb == 0 and t == 0:
                step("kT", uses_m=1, t=TT - 1)
                step("kT", uses_m=1, t=TT)
            step("rope", nb=nb, t=t, group=group, pu=k_use - 1 if nb == 2 and t > 2 else None)
        if nb == 2:
            step("kvout", group=group - t)
    units = [(g, t) for t in range(TT) for g in range(NKV)]

    def unit(kind, i, **uses):
        step(kind, n=i, g=units[i][0], t=units[i][1], **uses)

    unit("Q", 0, uses_m=1)
    for i in range(len(units)):
        unit("S", i)
        if i + 1 < len(units):
            unit("Q", i + 1, uses_m=1)
        if i > 1:
            unit("PV", i - 2, uses_m=1)
        if i:
            unit("sums", i - 1)
        unit("softmax", i)
    unit("sums", len(units) - 1)
    for i in (len(units) - 2, len(units) - 1):
        unit("PV", i, uses_m=1)
    for nb in (0, 1):
        j = bload(("w_out_odd",), nb)
        for t in range(TT):
            bgroup("wout", nb, t, j, ph=3)
            if nb == 0 and t in (0, 2):
                mod(1, 2, t // 2)
            if nb == 0 and t == 4:
                flush()
            if nb:
                normed(3, t)
    ffn(1, [(1, 5, 0), (1, 5, 1)])
    mod_step = {ld: i for i, s in enumerate(steps) if s["kind"] == "mod" for ld in (s["ld"], s["ld"] + 1)}
    owner = [i for i, ld in enumerate(loads) for _ in range(ld["blocks"])]
    pending = [(i, j) for i, s in enumerate(steps) for j in s["split"] if j < n["block"]]
    for s in steps:
        s["split"] = []
    at = 0
    for i, j in pending:
        at = max([at, i] + [mod_step[ld] for ld in range(max(0, owner[j] - 9), owner[j] - 1) if ld in mod_step])
        steps[at]["split"].append((j, steps[i]))
    return loads, steps


def key_tiles(t):
    if t == 0:
        return [0]
    return [TT] + list(range(max(1, t - 1), min(LAT, t + 1) + 1))


def key_slot(k):
    return {0: 0, TT: 1}.get(k, k + 1)


def mask_start(t):
    return 0 if t < 2 else 3 * P


def pv_steps(n):
    return sum(len(key_tiles(t)) for t in range(TT) for _ in range(NKV) if t * NKV + _ < n)


def hybrid_step(nc, A):
    f32, f32r, bf16 = mybir.dt.float32, mybir.dt.float32r, mybir.dt.bfloat16
    ALU, ACT, AX = mybir.AluOpType, mybir.ActivationFunctionType, mybir.AxisListType
    LOADS, STEPS = schedule()

    ctx = ExitStack()
    with ctx:
        def sb(name, shape, dt=f32):
            return ctx.enter_context(nc.sbuf_tensor(name, shape, dt))

        def alias(name, shape, dt=f32):
            with nc.sbuf_tensor(name, shape, dt) as t:
                return t

        def sem(name):
            return ctx.enter_context(nc.semaphore(name))

        X = sb("X", [P, TT, D])
        EARLY_H = alias("EARLY_H", [P, 4, 2048])
        HH = sb("HH", [P, KD, TOK], f32r)
        HL = sb("HL", [P, KD, TOK], f32r)
        WH = sb("WH", [P, RING, 1024], f32r)
        WL = sb("WL", [P, RING, 1024], f32r)
        RAW = sb("RAW", [P, RAWN, 2048])
        MX = alias("MX", [P, 2 * AS * TOK])
        AH = sb("AH", [P, AS, TOK], f32r)
        AL = sb("AL", [P, AS, TOK], f32r)
        ACC = sb("ACC", [P, TT, D])
        GG = sb("GG", [P, 4, D])
        QS = alias("QS", [P, 2, 512], f32r)
        HF = sb("HF", [P, KD, P])
        PART = sb("PART", [P, 512])
        BMR = sb("BMR", [1, 512])
        IDN = sb("IDN", [P, P])
        SEL = sb("SEL", [P, 2, P])
        CC = sb("CC", [P, 2, KD])
        CSG = sb("CSG", [P, 2, KD])
        CL = sb("CL", [P, KD, 32])
        MODC = sb("MODC", [P, 2, 4, KD, 2])
        PC = sb("PC", [P, NCOL])
        BC = sb("BC", [P, 2, N_MOD * KD])
        STAT = sb("STAT", [P, TT, 6])
        EPSC = sb("EPSC", [P, 1])
        LG = sb("LG", [P, 4, 8])
        NCL = sb("NCL", [P, 8])
        NS = sb("NS", [P, 8])
        SV = sb("SV", [P, TT, 3])
        AST = sb("AST", [P, 2, 6, 4])
        SINK = sb("SINK", [P, 16])

        PS = ctx.enter_context(nc.psum_tensor("PS", [P, 8, 512], f32))
        PSF = PS[:, :, :].rearrange("p b n -> p (b n)")

        U = ACC[:, :, 0:512]
        V = ACC[:, :, 512:1024]
        XR = MX[:, 0:2560].rearrange("p (j n) -> p j n", j=4)
        GT = MX[:, 2560:5120].rearrange("p (j n) -> p j n", j=4)
        BD = MX[:, 5120:7168].rearrange("p (w d j n) -> p w d j n", w=2, d=2, j=4)
        GMN = MX[:, 7168:7680]
        GGF = GG[:, :, :].rearrange("p v n -> p (v n)")
        RG = [GGF[:, i * TOK:(i + 1) * TOK] for i in range(6)]
        RR, II, TH = RG[0:2], RG[2:4], RG[4:6]
        WST, WSR = HF[:, 0:4, :], HF[:, 4:8, :]
        SHEET, SHEET2 = HF[0:NCOL, 0, :], HF[0:2 * N_MOD * KD, 1, :]
        KH = AH[:, :, :].rearrange("p s n -> p (s n)")[:, 0:3072].rearrange("p (g n) -> p g n", g=NKV)
        KL = AL[:, :, :].rearrange("p s n -> p (s n)")[:, 0:3072].rearrange("p (g n) -> p g n", g=NKV)
        QK2 = GGF[:, 0:512]
        ROPE = GGF[:, 512:1024].rearrange("p (w t n) -> p w t n", w=2, t=LAT)
        KTOK = GGF[:, 1024:2048].rearrange("p (s n) -> p s n", s=4)
        Z = GGF.rearrange("p (u h n) -> p u h n", u=2, h=4)
        XCB = sb("XCB", [P, 2 * TOK])
        XC = [XCB[:, i * TOK:(i + 1) * TOK] for i in range(2)]
        JUNK = XCB[:, 0:D]
        MASK = XCB[:, 0:896]
        PT_LOAD = next(i for i, ld in enumerate(LOADS) if ld.get("src") == ("w_out_odd",)) + 1
        PT = [RAW[:, PT_LOAD % RAWN, 512 * i:512 * i + 512] for i in range(4)]

        def vv(t):
            c = AS * TOK * (t // 3) + 3072 + 256 * (t % 3)
            return MX[:, c:c + 256]

        def k_tok(t):
            return KTOK[:, {0: 0, TT: 1}.get(t, 2 + t % 2), :]

        EARLY = {i: EARLY_H[:, i - RAWN, :] if i < RAWN + 4 else MX[:, 2048 * (i % 2):2048 * (i % 2) + 2048]
                 for i in range(RAWN, RAWN + 6)}

        early_in = [sem(f"early_in{i}") for i in range(6)]
        raw_in = [sem(f"raw_in{i}") for i in range(RAWN)]
        const_in = [sem(f"const_in{i}") for i in range(14)]
        w_hi, w_lo, mod_read = sem("w_hi"), sem("w_lo"), sem("mod_read")
        a_ready = [sem(f"a_ready{i}") for i in range(2)]
        a_free = [sem(f"a_free{i}") for i in range(2)]
        b_ready = [sem(f"b_ready{i}") for i in range(2)]
        b_free = [sem(f"b_free{i}") for i in range(2)]
        m_ready = [sem(f"m_ready{i}") for i in range(2)]
        m_free = [sem(f"m_free{i}") for i in range(2)]
        bmr_in = sem("bmr_in")
        gg_in = [sem(f"gg_in{i}") for i in range(2)]
        dve_done, act_done = sem("dve_done"), sem("act_done")
        cl_ready, lam_e, lam_ready, csg = sem("cl_ready"), sem("lam_e"), sem("lam_ready"), sem("csg")
        consts_made = sem("consts_made")
        ysum, xsum, x_new, xn_ready = sem("ysum"), sem("xsum"), sem("x_new"), sem("xn_ready")
        h_hi = sem("h_hi")
        h_lo = [sem(f"h_lo{i}") for i in range(2)]
        sq_ready, a_hi, a_lo = sem("sq_ready"), sem("a_hi"), sem("a_lo")
        xc_ready = [sem(f"xc_ready{i}") for i in range(2)]
        h_ready, h_sum = sem("h_ready"), sem("h_sum")
        xc_used, ea_ready, t_ready, root_ready, rg_done = (sem("xc_used"), sem("ea_ready"), sem("t_ready"), sem("root_ready"),
                                                            sem("rg_done"))
        vs_ready, vn_ready, wst_in = sem("vs_ready"), sem("vn_ready"), sem("wst_in")
        mix_hi, mix_lo = sem("mix_hi"), sem("mix_lo")
        l1_in = [sem(f"l1_in{i}") for i in range(4)]
        mod_done = sem("mod_done")
        sum_ready = sem("sum_ready")
        k_out, k_hi, q_hi = sem("k_out"), sem("k_hi"), sem("q_hi")
        qk_ready, v_done = sem("qk_ready"), sem("v_done")
        s_done, z_ready, e_ready, p_ready, nm_ready, es_ready = (sem("s_done"), sem("z_ready"), sem("e_ready"),
                                                                 sem("p_ready"), sem("nm_ready"), sem("es_ready"))
        pt_mm = [sem(f"pt_mm{i}") for i in range(2)]
        pt_ready = [sem("pt_ready_dve"), sem("pt_ready_act")]
        PT_TILES, done = [], [0, 0]
        for t in range(TT):
            for g in range(NKV):
                nk = len(key_tiles(t))
                for kt in range(nk):
                    who = 0 if kt < nk // 2 else 1
                    done[who] += 1
                    PT_TILES.append((NKV * t + g, kt, who, done[who]))
        stored = sem("stored")

        def upto(eng, pair, n):
            eng.wait_ge(pair[n % 2], n // 2 + 1)

        def input_ready(eng, n):
            for half in (0, 1):
                eng.wait_ge(h_lo[half], n)

        CHUNK_B = [s["b"] + 1 for s in STEPS if s["kind"] == "G2" and s["t"] == TT - 1]
        PV_M = [s["m"] for s in STEPS if s["kind"] == "PV"]
        KT_M = [s["m"] for s in STEPS if s["kind"] == "kT"][-1]
        GATE_A = [s["a"] + i for s in STEPS if s["kind"] == "A" and s["what"] == "gate" for i in (0, 1)]
        SHEET_M = [s["m"] for s in STEPS if s["kind"] == "sheet"][0]
        GATE_M = [s["m"] for s in STEPS if s["kind"] == "mod" and s["c"] in (2, 5)]
        PART_M = [s["m"] + (s["c"] in (2, 5)) for s in STEPS if s["kind"] == "modfin"]
        MOD_M = [s["m"] for s in STEPS if s["kind"] == "mod"]
        YA_M = [s["m"] for s in STEPS if s["kind"] == "ya"]
        Q_M = [s["m"] for s in STEPS if s["kind"] == "Q"]
        QKV_B = [s["b"] for s in STEPS if s["kind"] == "B" and s["what"] == "qkv"][-1]

        def step_done(eng, s):
            if s["kind"] == "A":
                upto(eng, a_ready, s["a"] + 1)
            elif s["kind"] == "B":
                upto(eng, b_ready, s["b"])
            elif s["kind"] == "G2":
                upto(eng, b_ready, s["b"] + 1)

        def conv(eng, V_, link, d, j):
            if j == 0:
                upto(eng, m_free, SHEET_M)
                upto(eng, a_free, 2)
                upto(eng, a_free, 3)
            w = lambda k: PC[:, CW + 16 * d + 4 * k + j:CW + 16 * d + 4 * k + j + 1]
            link(V_.tensor_scalar(XC[d], XR[:, j, :], w(3 if d == 0 else 0),
                                  PC[:, CB + 4 * d + j:CB + 4 * d + j + 1], ALU.mult, ALU.add))
            for sh in (1, 2, 3):
                for lo, hi in ((0, P), (P, TOK)):
                    dst, src = (slice(lo + sh, hi), slice(lo, hi - sh)) if d == 0 else (slice(lo, hi - sh), slice(lo + sh, hi))
                    ins = V_.scalar_tensor_tensor(XC[d][:, dst], XR[:, j, src], w(3 - sh if d == 0 else sh),
                                                  XC[d][:, dst], ALU.mult, ALU.add)
                    if sh == 3 and lo:
                        ins.then_inc(xc_ready[d], 1)
                    else:
                        link(ins)

        def pt_copies(eng, copy, i, who):
            for q, (unit, kt, by, _) in enumerate(PT_TILES):
                if unit == i and by == who:
                    upto(eng, pt_mm, q)
                    if i:
                        upto(eng, m_ready, PV_M[i - 1])
                    copy(PT[kt], PS[:, 4 + q % 2, :]).then_inc(pt_ready[who], 1)

        def w_view(ld, b):
            place = raw(ld)
            k = LOADS[ld]["kind"]
            if k == "acols":
                return place.rearrange("p (k n) -> p k n", k=KD)[:, :, P * b:P * b + P]
            return place[:, 1024 * b:1024 * b + 1024]

        def ring_view(buf, ld, j):
            k = LOADS[ld]["kind"]
            if k == "acols":
                return buf[:, j % RING, :].rearrange("p (k n) -> p k n", k=KD)
            return buf[:, j % RING, :]

        BLOCK_LOAD = {}
        for i, ld in enumerate(LOADS):
            for b in range(ld["blocks"]):
                BLOCK_LOAD[ld["first"] + b] = (i, b)

        def raw_arrived(eng, ld):
            if ld in EARLY:
                eng.wait_ge(early_in[ld - RAWN], 16)
            else:
                eng.wait_ge(raw_in[ld % RAWN], 16 * ((ld - (len(EARLY) if ld >= RAWN else 0)) // RAWN + 1))

        def dram_view(ld):
            k = ld["kind"]
            if k == "mod":
                w = A["w_mod"][ld["layer"]].rearrange("(p k) n -> p k n", k=KD)
                c0 = ld["c"] * D + ld["half"] * 512
                return w[:, 4 * ld["kh"]:4 * ld["kh"] + 4, c0:c0 + 512]
            if k == "w2":
                w = A["w_ffn_out"][ld["layer"]].rearrange("(k p) n -> p k n", p=P)
                k0 = 4 * ld["c"] + 2 * ld["kh"]
                return w[:, k0:k0 + 2, :]
            src = ld["src"]
            w = A["w_ffn_in"][src[1]] if src[0] == "w1" else {
                "w_in": A["w_in_even"], "w_out_even": A["w_out_even"], "w_qkv": A["w_qkv"],
                "w_out_odd": A["w_out_odd"]}[src[0]][0]
            w = w.rearrange("(k p) n -> p k n", p=P)
            if k == "acols":
                return w[:, :, ld["col"]:ld["col"] + 256]
            return w[:, 4 * ld["kh"]:4 * ld["kh"] + 4, ld["col"]:ld["col"] + 512]

        def raw(i):
            return EARLY[i] if i in EARLY else RAW[:, i % RAWN, :]

        def raw_dst(i, ld):
            k = {"mod": 4, "w2": 2, "acols": KD, "bcols": 4}[ld["kind"]]
            return raw(i).rearrange("p (k n) -> p k n", k=k)

        def a_bank(a):
            base = 1024 * (a % 2) + 256
            return PSF[:, base:base + TOK]

        def m_bank(u):
            return PS[:, 6 + u % 2, :]

        def modc(layer, c):
            return MODC[:, layer, {0: 0, 1: 1, 3: 2, 4: 3}[c], :, :]

        block = ctx.enter_context(nc.Block())

        @block.sync
        def _(sp):
            for i, ld in enumerate(LOADS):
                if i in EARLY:
                    sp.dma_start(raw_dst(i, ld), dram_view(ld)).then_inc(early_in[i - RAWN], 16)
                    continue
                if i >= RAWN:
                    old = LOADS[i - RAWN - (len(EARLY) if i < 2 * RAWN + len(EARLY) else 0)]
                    if old["kind"] == "mod" and old["kh"] == 0:
                        sp.wait_ge(mod_read, old["n"] + 1)
                    elif old["kind"] == "mod":
                        upto(sp, m_ready, old["m"])
                    else:
                        sp.wait_ge(w_lo, old["first"] + 2)
                    if i == PT_LOAD + RAWN:
                        upto(sp, m_ready, PV_M[-1])
                sp.dma_start(raw_dst(i, ld), dram_view(ld)).then_inc(raw_in[i % RAWN], 16)
            for t in range(TT):
                sp.wait_ge(x_new, 3 * TT + t + 1)
                dst = A["y_prompt"][0] if t == 0 else A["y_sample"][0, (t - 1) * P:t * P, :]
                sp.dma_start(dst, X[:, t, :]).then_inc(stored, 16)
            sp.wait_ge(stored, 16 * (2 + TT))
            sp.wait_ge(k_out, 16)

        @block.scalar
        def _(act):
            own = [0]

            def link(ins):
                own[0] += 1
                ins.then_inc(act_done, 1)
                act.wait_ge(act_done, own[0])

            xs = A["x_sample"][0].rearrange("(t p) n -> p t n", p=P)
            act.dma_start(CC[:, 0, :], A["c_ctx"].rearrange("(p k) -> p k", k=KD)).then_inc(const_in[3], 16)
            act.dma_start(CC[:, 1, :], A["c"][0].rearrange("(p k) -> p k", k=KD)).then_inc(const_in[4], 16)
            act.dma_start(SHEET, A["sheet"]).then_inc(const_in[2], 16)
            act.dma_start(SHEET2, A["b_mod"].rearrange("l (k n) -> (l k) n", n=P)).then_inc(const_in[10], 16)
            act.dma_start(IDN[:, :], A["ident"]).then_inc(const_in[5], 16)
            act.dma_start(X[:, 0, :], A["x_prompt"][0]).then_inc(const_in[0], 16)
            act.dma_start(X[:, 1:TT, :], xs).then_inc(const_in[1], 16)
            act.wait_ge(const_in[3], 16)
            act.wait_ge(const_in[4], 16)
            nc.scalar.activation(CSG[:, :, :], CC[:, :, :], ACT.Sigmoid).then_inc(csg, 1)
            act.dma_start(SEL[:, :, :], A["sel"]).then_inc(const_in[6], 16)
            act.dma_start(GMN, A["gmlp_norm"].broadcast_to([P, 512])).then_inc(const_in[8], 16)
            act.dma_start(SINK[:, :], A["attn_sink"].broadcast_to([P, 16])).then_inc(const_in[9], 16)

            def split(s):
                for j, freed_by in s["split"]:
                    ld, b = BLOCK_LOAD[j]
                    raw_arrived(act, ld)
                    step_done(act, freed_by)
                    nc.scalar.copy(ring_view(WH, ld, j), w_view(ld, b)).then_inc(w_hi, 1)

            ngate = 0
            for s in STEPS:
                k = s["kind"]
                if k == "mod":
                    if s["c"] in (2, 5):
                        if ngate:
                            upto(act, m_ready, GATE_M[ngate - 1])
                        ngate += 1
                        c0 = s["c"] * D + 512 * s["half"]
                        act.dma_start(BMR[:, :], A["b_mod"][s["layer"]:s["layer"] + 1, c0:c0 + 512]).then_inc(bmr_in, 16)
                        half, kind = s["half"], 0 if s["c"] == 2 else 2
                        if s["layer"] == 1:
                            for i in (18, 19):
                                upto(act, m_ready, PV_M[i])
                        elif kind:
                            act.wait_ge(x_new, TT)
                        else:
                            act.wait_ge(rg_done, 4)
                        g = A["norm_mix_post" if kind == 0 else "norm_ffn_post"][s["layer"]:s["layer"] + 1, 512 * half:512 * half + 512]
                        for v in (0, 1):
                            act.dma_start(GG[:, kind + v, 512 * half:512 * half + 512], g.broadcast_to([P, 512])).then_inc(gg_in[half], 16)
                if k == "lambda":
                    act.wait_ge(lam_e, 1)
                    nc.scalar.activation(LG[:, 1, :], LG[:, 0, :], ACT.Exp).then_inc(lam_e, 1)
                    act.wait_ge(consts_made, 3)
                    for w, name in enumerate(("rg_wa", "rg_wi")):
                        for d in (0, 1):
                            for odd in (0, 1):
                                act.dma_start(BD[64 * odd:64 * odd + 64, w, d, :, 64 * odd:64 * odd + 64],
                                              A[name][0, d].rearrange("(j o) i n -> o i j n", o=2)[odd]).then_inc(const_in[7], 16)
                elif k == "post":
                    ph, t = s["ph"], s["t"]
                    b = s["yb"]
                    act.wait_ge(b_free[b % 2], b // 2 + 1)
                    if ph % 2 == 0:
                        act.wait_ge(a_lo, 16 * ph)
                    link(nc.scalar.activation(JUNK, ACC[:, t, :], ACT.Square, accum_out=STAT[:, t, 0:1]))
                    nc.scalar.activation(STAT[:, t, 1:2], STAT[:, t, 0:1], ACT.Sqrt, scale=1.0 / D, bias=EPSC[:, :])\
                        .then_inc(ysum, 1)
                elif k == "pre":
                    ph, t = s["ph"], s["t"]
                    if ph:
                        act.wait_ge(x_new, (ph - 1) * TT + t + 1)
                    else:
                        act.wait_ge(const_in[0] if t == 0 else const_in[1], 16)
                        act.wait_ge(consts_made, 3)
                    link(nc.scalar.activation(JUNK, X[:, t, :], ACT.Square, accum_out=STAT[:, t, 3:4]))
                    nc.scalar.activation(STAT[:, t, 4:5], STAT[:, t, 3:4], ACT.Sqrt, scale=1.0 / D, bias=EPSC[:, :])\
                        .then_inc(xsum, 1)
                elif k == "cut":
                    ph, t, n_ = s["ph"], s["t"], s["n"]
                    u, v = s["tm"] + 1, min(s["t"], 1)
                    layer, off = ph // 2, 0 if ph % 2 == 0 else 2
                    if n_:
                        act.wait_ge(h_lo[1], n_)
                    act.wait_ge(mod_done, 2 * ph + 2)
                    act.wait_ge(m_ready[u % 2], u // 2 + 1)
                    for i in range(4):
                        f = 4 + i
                        ins = nc.scalar.activation(HF[:, f, :], m_bank(u)[:, P * i:P * i + P], ACT.Identity,
                                                   scale=MODC[:, layer, off + 1, f, v:v + 1], bias=MODC[:, layer, off, f, v:v + 1])
                    ins.then_inc(m_free[u % 2], 1)
                    cols = slice(t * P, t * P + P)
                    upto(act, m_free, u - 1)
                    nc.scalar.copy(HH[:, 0:4, cols], HF[:, 0:4, :]).then_inc(h_hi, 1)
                    upto(act, m_free, u)
                    nc.scalar.copy(HH[:, 4:8, cols], HF[:, 4:8, :]).then_inc(h_hi, 1)
                elif k == "A" and s["fin"]:
                    if s["what"] == "xr" and s["tile"] == 2:
                        input_ready(act, TT)
                        act.dma_start(WSR, A["gmlp_ws"][0].rearrange("h p q -> p h q")).then_inc(wst_in, 16)
                    for i in (0, 1):
                        a, tile = s["a"] + i, s["tile"] + i
                        act.wait_ge(a_ready[a % 2], a // 2 + 1)
                        if s["what"] == "xr":
                            nc.scalar.copy(XR[:, tile, :], a_bank(a)).then_inc(a_free[a % 2], 1)
                        elif s["what"] == "gate":
                            nc.scalar.activation(GT[:, tile, :], a_bank(a), ACT.Gelu_apprx_tanh).then_inc(a_free[a % 2], 1)
                        else:
                            if tile:
                                act.wait_ge(sq_ready, tile)
                            nc.scalar.activation(XC[0], a_bank(a), ACT.Relu).then_inc(a_free[a % 2], 1)
                            slot, c = tile % AS, (tile - AS) // 4
                            act.wait_ge(sq_ready, tile + 1)
                            if tile >= AS:
                                upto(act, b_ready, CHUNK_B[c])
                            nc.scalar.copy(AH[:, slot, :], XC[1]).then_inc(a_hi, 1)
                elif k == "rg":
                    j, d = s["tile"], s["d"]
                    if j and d == 0:
                        act.wait_ge(rg_done, j)
                    for w, dst, col in ((0, RR[d], BA), (1, II[d], BI)):
                        a = s["a"] + w
                        act.wait_ge(a_ready[a % 2], a // 2 + 1)
                        nc.scalar.activation(dst, a_bank(a), ACT.Sigmoid, bias=PC[:, col + 4 * d + j:col + 4 * d + j + 1])\
                            .then_inc(a_free[a % 2], 1)
                    if d == 0:
                        split(s)
                        continue
                    upto(act, a_free, s["a"])
                    upto(act, a_free, s["a"] + 1)
                    act.wait_ge(lam_ready, 1)
                    for d in (0, 1):
                        c = 4 * d + j
                        nc.scalar.activation(TH[d], RR[d], ACT.Tanh, scale=NCL[:, c:c + 1]).then_inc(t_ready, 1)
                        act.wait_ge(t_ready, 2 * j + d + 1)
                        nc.scalar.activation(RR[d], RR[d], ACT.Exp, scale=LG[:, 3, c:c + 1]).then_inc(ea_ready, 1)
                    for d in (0, 1):
                        nc.scalar.activation(TH[d], TH[d], ACT.Sqrt).then_inc(root_ready, 1)
                elif k == "B":
                    b = s["b"]
                    bank = PS[:, 4 + b % 2, :]
                    if s["what"] == "v":
                        act.wait_ge(b_ready[b % 2], b // 2 + 1)
                        nc.scalar.activation(V[:, s["t"], :], bank, ACT.Gelu_apprx_tanh).then_inc(b_free[b % 2], 1)
                        act.wait_ge(b_free[b % 2], b // 2 + 1)
                        link(nc.scalar.activation(U[:, s["t"], :], V[:, s["t"], :], ACT.Square, accum_out=SV[:, s["t"], 0:1]))
                    elif s["what"] == "wout" and s["nb"]:
                        act.wait_ge(b_ready[b % 2], b // 2 + 1)
                        nc.scalar.copy(ACC[:, s["t"], 512:1024], bank).then_inc(b_free[b % 2], 1)
                    elif s["what"] == "u":
                        act.wait_ge(b_ready[b % 2], b // 2 + 1)
                        nc.scalar.activation(U[:, s["t"], :], bank, ACT.Gelu_apprx_tanh).then_inc(b_free[b % 2], 1)
                    elif s["what"] == "qkv" and s["nb"] == 2:
                        act.wait_ge(b_ready[b % 2], b // 2 + 1)
                        nc.scalar.copy(vv(s["t"]), PS[:, 4 + b % 2, 256:512]).then_inc(v_done, 1)
                elif k == "l1in":
                    upto(act, b_ready, CHUNK_B[FC - 1])
                    act.dma_start(MASK, A["mask"]).then_inc(l1_in[0], 16)
                    act.dma_start(ROPE, A["rope"].rearrange("p (w t n) -> p w t n", w=2, t=LAT)).then_inc(l1_in[1], 16)
                    act.dma_start(k_tok(TT), A["cache_k"][0, 0].rearrange("p g d -> p (g d)")).then_inc(l1_in[2], 16)
                    act.dma_start(vv(TT), A["cache_v"][0, 0].rearrange("p g d -> p (g d)")).then_inc(l1_in[3], 16)
                elif k == "vnorm":
                    act.wait_ge(act_done, own[0])
                    nc.scalar.activation(SV[:, :, 1:2], SV[:, :, 0:1], ACT.Sqrt, scale=1.0 / 512, bias=EPSC[:, :]).then_inc(vs_ready, 1)
                elif k == "gmlp":
                    act.wait_ge(rg_done, 4)
                    with nc.allow_non_contiguous_dma(reason="1024 state values, features on the partitions"):
                        act.dma_start(A["new_state"], NS[:, :]).then_inc(stored, 16)
                    upto(act, b_ready, s["b"] - 1)
                    for j in range(4):
                        nc.scalar.copy(HH[:, 4 + j, :], GT[:, j, :]).then_inc(mix_hi, 1)
                elif k == "ya":
                    u, t = s["m"], s["t"]
                    act.wait_ge(m_ready[u % 2], u // 2 + 1)
                    nc.scalar.copy(HH[:, 0:4, t * P:t * P + P], m_bank(u).rearrange("p (k n) -> p k n", k=4)).then_inc(mix_hi, 1)
                elif k == "kT":
                    u, c = s["m"], P * key_slot(s["t"])
                    act.wait_ge(m_ready[u % 2], u // 2 + 1)
                    nc.scalar.copy(KH[:, :, c:c + P], m_bank(u).rearrange("p (g n) -> p g n", g=NKV)).then_inc(k_hi, 1)
                elif k == "Q":
                    u, i = s["m"], s["n"]
                    act.wait_ge(m_ready[u % 2], u // 2 + 1)
                    if i == 0:
                        input_ready(act, 3 * TT)
                    if i > 1:
                        act.wait_ge(s_done, 4 * (i - 1))
                    nc.scalar.copy(QS[:, i % 2, :], m_bank(u)).then_inc(q_hi, 1)
                elif k == "kvout":
                    upto(act, b_free, s["group"])
                    act.dma_start(A["new_k"].rearrange("p g d -> p (g d)"), k_tok(0)).then_inc(k_out, 16)
                    act.wait_ge(v_done, 1)
                    act.dma_start(A["new_v"].rearrange("p g d -> p (g d)"), vv(0)).then_inc(stored, 16)
                elif k == "softmax":
                    i, g, z = s["n"], s["g"], s["n"] % 2
                    nk = P * len(key_tiles(s["t"]))
                    act.wait_ge(nm_ready, i + 1)
                    for h in range(4):
                        nc.scalar.activation(Z[:, z, h, 0:nk], Z[:, z, h, 0:nk], ACT.Exp, scale=0.125,
                                             bias=AST[:, z, 1, h:h + 1], accum_out=AST[:, z, 2, h:h + 1]).then_inc(e_ready, 1)
                    nc.scalar.activation(AST[:, z, 3, :], AST[:, z, 4, :], ACT.Exp).then_inc(es_ready, 1)
                elif k == "PV":
                    i, g, t = s["n"], s["g"], s["t"]
                    if i == 0:
                        act.wait_ge(w_lo, LOADS[PT_LOAD]["first"] + 2)
                    pt_copies(act, nc.scalar.copy, i, 1)
                    u = s["m"]
                    act.wait_ge(m_ready[u % 2], u // 2 + 1)
                    nc.scalar.copy(HH[:, 2 * g:2 * g + 2, t * P:t * P + P], m_bank(u)[:, 0:256].rearrange("p (k n) -> p k n", k=2))\
                        .then_inc(mix_hi, 1)
                split(s)

        @block.gpsimd
        def _(pool):
            for s in STEPS:
                k = s["kind"]
                if k == "root":
                    j = s["tile"]
                    pool.wait_ge(h_ready, 2 * j + 2)
                    upto(pool, a_free, GATE_A[j])
                    nc.gpsimd.tensor_tensor(TH[0], TH[0], TH[1], ALU.add).then_inc(h_sum, 1)
                    pool.wait_ge(h_sum, j + 1)
                    nc.gpsimd.tensor_tensor(GT[:, j, :], GT[:, j, :], TH[0], ALU.mult).then_inc(rg_done, 1)
                elif k == "sums":
                    i, z = s["n"], s["n"] % 2
                    nk = P * len(key_tiles(s["t"]))
                    pool.wait_ge(sum_ready, i + 1)
                    inv = AST[:, z, 5, :].unsqueeze(2).broadcast_to([P, 4, nk])
                    nc.gpsimd.tensor_tensor(Z[:, z, :, 0:nk], Z[:, z, :, 0:nk], inv, ALU.mult).then_inc(p_ready, 1)
                if s["kind"] == "cut":
                    t = s["t"]
                    pool.wait_ge(h_hi, 2 * s["n"] + 2)
                    cols = slice(t * P, t * P + P)
                    nc.gpsimd.tensor_tensor(HL[:, 4:8, cols], HF[:, 4:8, :], HH[:, 4:8, cols].bitcast(f32), ALU.subtract)\
                        .then_inc(h_lo[1], 1)
                for j, _ in s["split"]:
                    ld, b = BLOCK_LOAD[j]
                    pool.wait_ge(w_hi, j + 1)
                    nc.gpsimd.tensor_tensor(ring_view(WL, ld, j), w_view(ld, b), ring_view(WH, ld, j).bitcast(f32),
                                            ALU.subtract).then_inc(w_lo, 1)

        @block.vector
        def _(dve):
            own = [0]
            V_ = nc.vector

            def link(ins):
                own[0] += 1
                ins.then_inc(dve_done, 1)
                dve.wait_ge(dve_done, own[0])

            V_.memset(EPSC[:, :], EPS).then_inc(consts_made, 1)
            V_.memset(BD, 0.0).then_inc(consts_made, 1)
            V_.memset(CL[:, :, :], 0.0).then_inc(consts_made, 1)
            dve.wait_ge(csg, 1)
            dve.wait_ge(consts_made, 3)
            V_.tensor_tensor(CL[:, :, 0:2].rearrange("p k v -> p v k"), CC[:, :, :], CSG[:, :, :], ALU.mult).then_inc(cl_ready, 1)

            def scans(d, j):
                seg = lambda lo, hi: slice(lo, hi) if d == 0 else slice(hi - 1, lo - 1 if lo else None, -1)
                link(V_.tensor_tensor_scan(TH[d][:, seg(0, P)], RR[d][:, seg(0, P)], II[d][:, seg(0, P)], 0.0, ALU.mult, ALU.add))
                link(V_.tensor_tensor_scan(TH[d][:, seg(P, TOK)], RR[d][:, seg(P, TOK)], II[d][:, seg(P, TOK)],
                                           PC[:, ST + 4 * d + j:ST + 4 * d + j + 1], ALU.mult, ALU.add))
                end = P - 1 if d == 0 else 0
                V_.tensor_copy(NS[:, 4 * d + j:4 * d + j + 1], TH[d][:, end:end + 1]).then_inc(h_ready, 1)

            def query_remainder(i):
                u = Q_M[i]
                dve.wait_ge(q_hi, i + 1)
                V_.tensor_tensor(QS[64:128, i % 2, :], m_bank(u)[64:128, :], QS[64:128, i % 2, :].bitcast(f32),
                                 ALU.subtract).then_inc(m_free[u % 2], 1)

            def remainder(i):
                u, g, t = PV_M[i], i % NKV, i // NKV
                dve.wait_ge(mix_hi, TT + 4 + i + 1)
                cols = slice(t * P, t * P + P)
                V_.tensor_tensor(HL[:, 2 * g:2 * g + 2, cols], m_bank(u)[:, 0:256].rearrange("p (k n) -> p k n", k=2),
                                 HH[:, 2 * g:2 * g + 2, cols].bitcast(f32), ALU.subtract).then_inc(m_free[u % 2], 1)

            nmod = nchain = nkt = nscale = 0
            fin_g = 0
            for s in STEPS:
                k = s["kind"]
                if k == "sheet":
                    u = s["m"]
                    dve.wait_ge(m_ready[u % 2], u // 2 + 1)
                    V_.tensor_copy(BC[:, :, :].rearrange("p l k -> p (l k)"), m_bank(u)[:, P:P + 2 * N_MOD * KD])
                    V_.tensor_copy(PC[:, :], m_bank(u)[:, 0:NCOL]).then_inc(m_free[u % 2], 1)
                elif k == "lambda":
                    lam = PC[:, LAM:LAM + 8]
                    upto(dve, m_free, SHEET_M)
                    link(V_.tensor_scalar(LG[:, 1, :], lam, -1.0, None, ALU.mult))
                    V_.tensor_tensor(LG[:, 0, :], lam, LG[:, 1, :], ALU.min).then_inc(lam_e, 1)
                    dve.wait_ge(lam_e, 2)
                    e, v, w, acc = LG[:, 1, :], LG[:, 0, :], LG[:, 2, :], LG[:, 3, :]
                    link(V_.tensor_scalar(w, e, 2.0, None, ALU.add))
                    link(V_.reciprocal(w, w))
                    link(V_.tensor_tensor(v, e, w, ALU.mult))
                    link(V_.tensor_tensor(w, v, v, ALU.mult))
                    link(V_.memset(acc, 1.0 / 17))
                    for q in (15, 13, 11, 9, 7, 5, 3, 1):
                        link(V_.tensor_tensor(acc, acc, w, ALU.mult))
                        link(V_.tensor_scalar(acc, acc, 1.0 / q, None, ALU.add))
                    link(V_.tensor_tensor(acc, acc, v, ALU.mult))
                    link(V_.tensor_scalar(v, lam, 0.0, 8.0, ALU.min, ALU.mult))
                    link(V_.scalar_tensor_tensor(acc, acc, -16.0, v, ALU.mult, ALU.add))
                    V_.tensor_scalar(NCL[:, :], acc, -0.5, None, ALU.mult).then_inc(lam_ready, 1)
                elif k == "mod":
                    u = s["m"]
                    dve.wait_ge(m_ready[u % 2], u // 2 + 1)
                    if s["n"]:
                        upto(dve, m_ready, PART_M[s["n"] - 1])
                    V_.tensor_copy(PART[:, :], m_bank(u)).then_inc(m_free[u % 2], 1)
                elif k == "modfin":
                    layer, c, half = s["layer"], s["c"], s["half"]
                    if c in (2, 5):
                        fin_g += half == 0
                        for v in (0, 1):
                            u = s["m"] + v
                            dve.wait_ge(m_ready[u % 2], u // 2 + 1)
                            dve.wait_ge(gg_in[half], 32 * fin_g)
                            g = GG[:, (0 if c == 2 else 2) + v, 512 * half:512 * half + 512]
                            V_.tensor_tensor(g, m_bank(u), g, ALU.mult).then_inc(m_free[u % 2], 1)
                    else:
                        u = s["m"]
                        dve.wait_ge(m_ready[u % 2], u // 2 + 1)
                        src = m_bank(u).rearrange("p (i g w) -> p i w g", i=4, g=4)[:, :, 0:2, :]
                        dst = modc(layer, c)[:, 4 * half:4 * half + 4, :]
                        V_.tensor_reduce(dst, src, AX.X, ALU.add).then_inc(m_free[u % 2], 1)
                        dve.wait_ge(m_free[u % 2], u // 2 + 1)
                        k0 = KD * c + 4 * half
                        bias = BC[:, layer, k0:k0 + 4].unsqueeze(2).broadcast_to([P, 4, 2])
                        link(V_.tensor_tensor(dst, dst, bias, ALU.add))
                        if c in (1, 4):
                            g0 = (G_MIX if c == 1 else G_FFN) + 8 * layer + 4 * half
                            V_.scalar_tensor_tensor(dst[:, :, 0], dst[:, :, 0], 1.0, PC[:, g0:g0 + 4], ALU.add, ALU.mult)
                            V_.scalar_tensor_tensor(dst[:, :, 1], dst[:, :, 1], 1.0, PC[:, g0:g0 + 4], ALU.add, ALU.mult)\
                                .then_inc(mod_done, 1)
                            nscale += 1
                            dve.wait_ge(mod_done, nscale)
                elif k == "post":
                    ph, t = s["ph"], s["t"]
                    nchain += 1
                    dve.wait_ge(ysum, nchain)
                    link(V_.reciprocal(STAT[:, t, 2:3], STAT[:, t, 1:2]))
                    gain = GG[:, (0 if ph in (1, 3) else 2) + (t > 0), :]
                    link(V_.scalar_tensor_tensor(ACC[:, t, :], ACC[:, t, :], STAT[:, t, 2:3], gain, ALU.mult, ALU.mult))
                    V_.tensor_tensor(X[:, t, :], X[:, t, :], ACC[:, t, :], ALU.add).then_inc(x_new, 1)
                elif k == "pre":
                    ph, t = s["ph"], s["t"]
                    dve.wait_ge(xsum, ph * TT + t + 1)
                    link(V_.reciprocal(STAT[:, t, 5:6], STAT[:, t, 4:5]))
                    V_.tensor_scalar(ACC[:, t, :], X[:, t, :], STAT[:, t, 5:6], None, ALU.mult).then_inc(xn_ready, 1)
                elif k == "T":
                    ph, t, u0 = s["ph"], s["t"], s["m"]
                    layer, off = ph // 2, 0 if ph % 2 == 0 else 2
                    v = 0 if t == 0 else 1
                    if s["n"]:
                        dve.wait_ge(h_lo[0], s["n"])
                    dve.wait_ge(m_ready[u0 % 2], u0 // 2 + 1)
                    for f in range(4):
                        ins = V_.tensor_scalar(HF[:, f, :], m_bank(u0)[:, P * f:P * f + P], MODC[:, layer, off + 1, f, v:v + 1],
                                               MODC[:, layer, off, f, v:v + 1], ALU.mult, ALU.add)
                    ins.then_inc(m_free[u0 % 2], 1)
                elif k == "cut":
                    cols = slice(s["t"] * P, s["t"] * P + P)
                    dve.wait_ge(h_hi, 2 * s["n"] + 1)
                    V_.tensor_tensor(HL[:, 0:4, cols], HF[:, 0:4, :], HH[:, 0:4, cols].bitcast(f32), ALU.subtract).then_inc(h_lo[0], 1)
                elif k == "A":
                    if s["what"] == "xr" and s["fin"] and s["tile"] == 2:
                        conv(dve, V_, link, 0, 0)
                        conv(dve, V_, link, 1, 0)
                    if s["what"] == "ffn" and s["fin"]:
                        for tile in (s["tile"], s["tile"] + 1):
                            slot = tile % AS
                            a = s["a"] + tile - s["tile"]
                            dve.wait_ge(a_free[a % 2], a // 2 + 1)
                            if tile:
                                dve.wait_ge(a_hi, tile)
                                dve.wait_ge(a_lo, tile)
                            V_.tensor_tensor(XC[1], XC[0], XC[0], ALU.mult).then_inc(sq_ready, 1)
                            dve.wait_ge(a_hi, tile + 1)
                            V_.tensor_tensor(AL[:, slot, :], XC[1], AH[:, slot, :].bitcast(f32), ALU.subtract).then_inc(a_lo, 1)
                elif k == "rg":
                    j, d = s["tile"], s["d"]
                    upto(dve, a_free, s["a"] + 1)
                    V_.tensor_tensor(II[d], II[d], XC[d], ALU.mult).then_inc(xc_used, 1)
                    dve.wait_ge(xc_used, 2 * j + d + 1)
                    if j < 3 and d:
                        conv(dve, V_, link, 0, j + 1)
                        conv(dve, V_, link, 1, j + 1)
                elif k == "root":
                    j = s["tile"]
                    for d in (0, 1):
                        dve.wait_ge(root_ready, 2 * j + d + 1)
                        link(V_.scalar_tensor_tensor(TH[d], RR[d], 1.0, TH[d], ALU.add, ALU.mult))
                        link(V_.tensor_tensor(II[d], II[d], TH[d], ALU.mult))
                        scans(d, j)
                elif k == "B":
                    b, t, nb, what = s["b"], s["t"], s["nb"], s["what"]
                    bank = PS[:, 4 + b % 2, :]
                    if what == "wout" and nb == 0:
                        dve.wait_ge(b_ready[b % 2], b // 2 + 1)
                        V_.tensor_copy(ACC[:, t, 512 * nb:512 * nb + 512], bank).then_inc(b_free[b % 2], 1)
                elif k == "rope":
                    t, nb, b = s["t"], s["nb"], s["group"]
                    bank = PS[:, 4 + b % 2, :]
                    heads = 8 if nb < 2 else NKV
                    n = heads * HD
                    dst = ACC[:, t, 512 * nb:512 * nb + 512] if nb < 2 else k_tok(t)
                    if nb == 2:
                        dve.wait_ge(v_done, t + 1)
                    upto(dve, b_ready, b)
                    if s["pu"] is not None:
                        upto(dve, m_ready, s["pu"])
                    if t == 0:
                        V_.tensor_copy(dst, bank[:, 0:n]).then_inc(b_free[b % 2], 1)
                    else:
                        if nb == 2 and t == 1:
                            dve.wait_ge(l1_in[1], 16)
                        hv = lambda x: x[:, 0:n].rearrange("p (h d) -> p h d", h=heads)
                        parts = lambda x, o: x.rearrange("p (h b o f) -> p h b o f", b=2, o=2, f=16)[:, :, :, o, :]
                        link(V_.tensor_tensor(hv(dst), hv(bank), ROPE[:, 0, t - 1, :].unsqueeze(1).broadcast_to([P, heads, HD]), ALU.mult))
                        for o in (0, 1):
                            sn = parts(ROPE[:, 1, t - 1, :], o).broadcast_to([P, heads, 2, 16])
                            ins = V_.tensor_tensor(parts(QK2[:, 0:n], o), parts(bank[:, 0:n], 1 - o), sn, ALU.mult)
                        ins.then_inc(b_free[b % 2], 1)
                        upto(dve, b_free, b)
                        V_.tensor_tensor(dst, dst, QK2[:, 0:n], ALU.add).then_inc(qk_ready, 1)
                elif k == "kT":
                    u, c = s["m"], P * key_slot(s["t"])
                    nkt += 1
                    dve.wait_ge(k_hi, nkt)
                    V_.tensor_tensor(KL[:, :, c:c + P], m_bank(u).rearrange("p (g n) -> p g n", g=NKV),
                                     KH[:, :, c:c + P].bitcast(f32), ALU.subtract).then_inc(m_free[u % 2], 1)
                elif k == "Q":
                    if s["n"] == 0:
                        query_remainder(0)
                elif k == "G2":
                    t, c = s["t"], s["c"]
                    for nh in (0, 1):
                        b = s["b"] + nh
                        bank = PS[:, 4 + b % 2, :]
                        acc = ACC[:, t, 512 * nh:512 * nh + 512]
                        dve.wait_ge(b_ready[b % 2], b // 2 + 1)
                        if c:
                            V_.tensor_tensor(acc, acc, bank, ALU.add).then_inc(b_free[b % 2], 1)
                        else:
                            V_.tensor_copy(acc, bank).then_inc(b_free[b % 2], 1)
                elif k == "vnorm":
                    u = s["m"]
                    dve.wait_ge(m_ready[u % 2], u // 2 + 1)
                    V_.tensor_copy(WST, m_bank(u).rearrange("p (h n) -> p h n", h=4)).then_inc(m_free[u % 2], 1)
                    dve.wait_ge(vs_ready, 1)
                    dve.wait_ge(const_in[8], 16)
                    link(V_.reciprocal(SV[:, :, 2:3], SV[:, :, 1:2]))
                    for t in range(TT):
                        V_.scalar_tensor_tensor(V[:, t, :], V[:, t, :], SV[:, t, 2:3], GMN, ALU.mult, ALU.mult).then_inc(vn_ready, 1)
                elif k == "gmlp":
                    upto(dve, b_free, s["b"] - 1)
                    for h in range(4):
                        a = s["a"] + h
                        dve.wait_ge(a_ready[a % 2], a // 2 + 1)
                        uh = U[:, :, P * h:P * h + P]
                        V_.scalar_tensor_tensor(uh, a_bank(a).rearrange("p (t n) -> p t n", t=TT), PC[:, BS + h:BS + h + 1], uh,
                                                ALU.add, ALU.mult).then_inc(a_free[a % 2], 1)
                        dve.wait_ge(mix_hi, h + 1)
                        V_.tensor_tensor(HL[:, 4 + h, :], GT[:, h, :], HH[:, 4 + h, :].bitcast(f32), ALU.subtract).then_inc(mix_lo, 1)
                elif k == "ya":
                    u, t = s["m"], s["t"]
                    dve.wait_ge(mix_hi, 4 + t + 1)
                    cols = slice(t * P, t * P + P)
                    V_.tensor_tensor(HL[:, 0:4, cols], m_bank(u).rearrange("p (k n) -> p k n", k=4),
                                     HH[:, 0:4, cols].bitcast(f32), ALU.subtract).then_inc(m_free[u % 2], 1)
                elif k == "softmax":
                    i, t, z = s["n"], s["t"], s["n"] % 2
                    nk = P * len(key_tiles(t))
                    m0 = mask_start(t)
                    if i == 0:
                        dve.wait_ge(k_out, 16)
                        dve.wait_ge(l1_in[0], 16)
                        dve.wait_ge(const_in[9], 16)
                    if i + 1 < TT * NKV:
                        query_remainder(i + 1)
                    if i >= 2:
                        upto(dve, pt_mm, pv_steps(i - 1) - 1)
                    for h in range(4):
                        dve.wait_ge(s_done, 4 * i + h + 1)
                        V_.tensor_tensor_reduce(out=Z[:, z, h, 0:nk], in0=PS[:, h, 0:nk], in1=MASK[:, m0:m0 + nk], scale=1.0,
                                                scalar=-3.0e38, op0=ALU.add, op1=ALU.max, accum_out=AST[:, z, 0, h:h + 1])\
                            .then_inc(z_ready, 1)
                    dve.wait_ge(z_ready, 4 * (i + 1))
                    snk = SINK[:, 4 * s["g"]:4 * s["g"] + 4]
                    link(V_.scalar_tensor_tensor(AST[:, z, 0, :], AST[:, z, 0, :], 0.125, snk, ALU.mult, ALU.max))
                    link(V_.tensor_scalar(AST[:, z, 1, :], AST[:, z, 0, :], -1.0, None, ALU.mult))
                    V_.tensor_tensor(AST[:, z, 4, :], snk, AST[:, z, 1, :], ALU.add).then_inc(nm_ready, 1)
                    if i > 1:
                        remainder(i - 2)
                elif k == "sums":
                    i, z = s["n"], s["n"] % 2
                    dve.wait_ge(e_ready, 4 * (i + 1))
                    dve.wait_ge(es_ready, i + 1)
                    link(V_.tensor_tensor(AST[:, z, 2, :], AST[:, z, 2, :], AST[:, z, 3, :], ALU.add))
                    V_.reciprocal(AST[:, z, 5, :], AST[:, z, 2, :]).then_inc(sum_ready, 1)
                elif k == "PV":
                    i = s["n"]
                    if i == 0:
                        dve.wait_ge(w_lo, LOADS[PT_LOAD]["first"] + 2)
                    pt_copies(dve, V_.tensor_copy, i, 0)
                    if i >= TT * NKV - 2:
                        remainder(i)

        @block.tensor
        def _(pe):
            MM = nc.tensor.matmul
            TR = nc.tensor.transpose

            def split3(out, w, x, first, last):
                (wh, wl), (xh, xl) = w, x
                MM(out, wh, xh, start=first, stop=False)
                MM(out, wh, xl, start=False, stop=False)
                return MM(out, wl, xh, start=False, stop=last)

            def a_acquire(a):
                if a >= 2:
                    pe.wait_ge(a_free[a % 2], a // 2)

            def b_acquire(b):
                if b >= 2:
                    pe.wait_ge(b_free[b % 2], b // 2)

            def m_acquire(u):
                if u >= 2:
                    pe.wait_ge(m_free[u % 2], u // 2)

            RANGE = ((0, 256), (256, TOK))
            ntiles = ngate = 0
            for s in STEPS:
                k = s["kind"]
                if k == "sheet":
                    pe.wait_ge(const_in[2], 16)
                    pe.wait_ge(const_in[5], 16)
                    u = s["m"]
                    pe.wait_ge(const_in[10], 16)
                    TR(m_bank(u)[:, 0:NCOL], SHEET, IDN[0:NCOL, 0:NCOL])
                    nb = 2 * N_MOD * KD
                    TR(m_bank(u)[:, P:P + nb], SHEET2, IDN[0:nb, 0:nb]).then_inc(m_ready[u % 2], 1)
                elif k == "mod":
                    u = s["m"]
                    m_acquire(u)
                    if s["n"] == 0:
                        pe.wait_ge(cl_ready, 1)
                    for kh in (0, 1):
                        ld = s["ld"] + kh
                        raw_arrived(pe, ld)
                        rv = raw(ld).rearrange("p (k n) -> p k n", k=4)
                        for kt in range(4):
                            gate = s["c"] in (2, 5) and kh == 1 and kt == 0
                            ins = MM(PS[32 * kt:32 * kt + 32, 6 + u % 2, :], CL[:, 4 * kh + kt, :], rv[:, kt, :],
                                     start=(kh == 0), stop=(kh == 1 and not gate))
                            if gate:
                                ngate += 1
                                pe.wait_ge(const_in[6], 16)
                                pe.wait_ge(bmr_in, 16 * ngate)
                                MM(PS[0:32, 6 + u % 2, :], SEL[0:1, 0, 0:32], BMR[:, :], start=False, stop=True)
                        if kh == 0:
                            ins.then_inc(mod_read, 1)
                    ins.then_inc(m_ready[u % 2], 1)
                elif k == "modfin":
                    upto(pe, m_free, MOD_M[s["n"]])
                    if s["c"] in (2, 5):
                        for v in (0, 1):
                            u = s["m"] + v
                            m_acquire(u)
                            MM(m_bank(u), SEL[:, v, :], PART[:, :], start=True, stop=True).then_inc(m_ready[u % 2], 1)
                    else:
                        u = s["m"]
                        m_acquire(u)
                        for i in range(4):
                            ins = TR(m_bank(u)[:, P * i:P * i + P], PART[:, P * i:P * i + P], IDN[:, :])
                        ins.then_inc(m_ready[u % 2], 1)
                elif k == "T":
                    ntiles += 1
                    t = s["t"]
                    pe.wait_ge(xn_ready, s["n"] + 1)
                    for q in (0, 1):
                        u = s["m"] + q
                        m_acquire(u)
                        for i in range(4):
                            f = 4 * q + i
                            ins = TR(m_bank(u)[:, P * i:P * i + P], ACC[:, t, P * f:P * f + P], IDN[:, :])
                        ins.then_inc(m_ready[u % 2], 1)
                elif k == "A":
                    for part in s["parts"]:
                        if len(s["parts"]) == 1:
                            input_ready(pe, ntiles if part else TT * s["norm"] + 2)
                    if len(s["parts"]) == 2:
                        input_ready(pe, ntiles)
                    order = [(i, part) for i in (0, 1) for part in s["parts"]]
                    for i, part in order:
                        a, j = s["a"] + i, s["j"] + i
                        if part == s["parts"][0] and 0 in s["parts"]:
                            a_acquire(a)
                            pe.wait_ge(w_lo, j + 1)
                        c0, c1 = RANGE[part]
                        wh = WH[:, j % RING, :].rearrange("p (k n) -> p k n", k=KD)
                        wl = WL[:, j % RING, :].rearrange("p (k n) -> p k n", k=KD)
                        for kt in range(KD):
                            ins = split3(a_bank(a)[:, c0:c1], (wh[:, kt, :], wl[:, kt, :]), (HH[:, kt, c0:c1], HL[:, kt, c0:c1]),
                                         kt == 0, kt == KD - 1)
                        if part == 1:
                            ins.then_inc(a_ready[a % 2], 1)
                elif k == "rg":
                    j, d = s["tile"], s["d"]
                    if j == 0 and d == 0:
                        pe.wait_ge(const_in[7], 16 * 8)
                    pe.wait_ge(xc_ready[d], j + 1)
                    for w in (0, 1):
                        a = s["a"] + w
                        a_acquire(a)
                        for c0, c1 in RANGE:
                            ins = MM(a_bank(a)[:, c0:c1], BD[:, w, d, j, :], XC[d][:, c0:c1], start=True, stop=True)
                        ins.then_inc(a_ready[a % 2], 1)
                elif k == "B":
                    b, t, nb, what = s["b"], s["t"], s["nb"], s["what"]
                    b_acquire(b)
                    if what == "wout":
                        if s["ph"] == 1 and nb == 0:
                            pe.wait_ge(mix_lo, 4)
                            upto(pe, m_free, YA_M[t])
                        if s["ph"] == 3:
                            upto(pe, m_free, PV_M[-2])
                            upto(pe, m_free, PV_M[-1])
                    elif what == "qkv":
                        input_ready(pe, 2 * TT + (t + 1 if nb == 2 else TT))
                    for kt in range(KD):
                        j = s["j"] + kt // 2
                        if t == 0 and kt % 2 == 0:
                            pe.wait_ge(w_lo, j + 1)
                        cols = slice(512 * (kt % 2), 512 * (kt % 2) + 512)
                        hs = slice(t * P, t * P + P)
                        ins = split3(PS[:, 4 + b % 2, :], (HH[:, kt, hs], HL[:, kt, hs]), (WH[:, j % RING, cols], WL[:, j % RING, cols]),
                                     kt == 0, kt == KD - 1)
                    ins.then_inc(b_ready[b % 2], 1)
                elif k == "G2":
                    t = s["t"]
                    if t == 0:
                        pe.wait_ge(a_lo, 32 * s["layer"] + 4 * s["c"] + 4)
                        pe.wait_ge(w_lo, s["j"] + 4)
                    for nh in (0, 1):
                        b = s["b"] + nh
                        b_acquire(b)
                        for kt in range(4):
                            j, slot = s["j"] + kt, (32 * s["layer"] + 4 * s["c"] + kt) % AS
                            hs, cols = slice(t * P, t * P + P), slice(512 * nh, 512 * nh + 512)
                            ins = split3(PS[:, 4 + b % 2, :], (AH[:, slot, hs], AL[:, slot, hs]),
                                         (WH[:, j % RING, cols], WL[:, j % RING, cols]), kt == 0, kt == 3)
                        ins.then_inc(b_ready[b % 2], 1)
                elif k == "vnorm":
                    u = s["m"]
                    m_acquire(u)
                    pe.wait_ge(wst_in, 16)
                    for h in range(4):
                        ins = TR(m_bank(u)[:, P * h:P * h + P], WSR[:, h, :], IDN[:, :])
                    ins.then_inc(m_ready[u % 2], 1)
                    vnorm_m = u
                elif k == "gmlp":
                    upto(pe, m_free, vnorm_m)
                    pe.wait_ge(vn_ready, TT)
                    for h in range(4):
                        a = s["a"] + h
                        a_acquire(a)
                        for (c0, c1), (t0, t1) in zip(RANGE, ((0, 2), (2, TT))):
                            ins = MM(a_bank(a)[:, c0:c1], WST[:, h, :], V[:, t0:t1, P * h:P * h + P], start=True, stop=True)
                        ins.then_inc(a_ready[a % 2], 1)
                    gmlp_a = s["a"]
                elif k == "ya":
                    u, t = s["m"], s["t"]
                    for h in (2, 3):
                        upto(pe, a_free, gmlp_a + h)
                    m_acquire(u)
                    for h in range(4):
                        ins = TR(m_bank(u)[:, P * h:P * h + P], U[:, t, P * h:P * h + P], IDN[:, :])
                    ins.then_inc(m_ready[u % 2], 1)
                elif k == "kT":
                    u, t = s["m"], s["t"]
                    m_acquire(u)
                    if t == 0:
                        upto(pe, b_free, s["group"])
                    elif t < TT:
                        pe.wait_ge(qk_ready, t)
                    else:
                        pe.wait_ge(l1_in[2], 16)
                    for g in range(NKV):
                        for half in (0, 64):
                            ins = MM(m_bank(u)[half:half + 64, P * g:P * g + P], k_tok(t)[:, HD * g:HD * g + HD], IDN[:, :], start=True, stop=True)
                    ins.then_inc(m_ready[u % 2], 1)
                elif k == "Q":
                    u, g, t = s["m"], s["g"], s["t"]
                    m_acquire(u)
                    if s["n"] == 0:
                        upto(pe, b_free, QKV_B - LAT)
                    if s["n"] == NKV:
                        pe.wait_ge(qk_ready, 3 * LAT)
                    for h in range(4):
                        c = HD * (4 * g + h)
                        for half in (0, 64):
                            ins = MM(m_bank(u)[half:half + 64, P * h:P * h + P], ACC[:, t, c:c + HD], IDN[:, :], start=True, stop=True)
                    ins.then_inc(m_ready[u % 2], 1)
                elif k == "S":
                    i, g, t = s["n"], s["g"], s["t"]
                    if i == 0:
                        upto(pe, m_free, KT_M - 1)
                        upto(pe, m_free, KT_M)
                    upto(pe, m_free, Q_M[i])
                    pieces = {0: [(0, 0, 2)], 1: [(0, 1, 3)], 2: [(0, 1, 4)], 3: [(0, 1, 2), (P, 3, 3)], 4: [(0, 1, 2), (P, 4, 2)]}[t]
                    for h in range(4):
                        if i:
                            pe.wait_ge(z_ready, 4 * (i - 1) + h + 1)
                        q = QS[:, i % 2, P * h:P * h + P]
                        for c, slot, nt in pieces:
                            out, keys = PS[:, h, c:c + P * nt], slice(P * slot, P * (slot + nt))
                            MM(out, q, KH[:, g, keys], start=True, stop=False)
                            ins = MM(out, q, KL[:, g, keys], start=False, stop=True)
                        ins.then_inc(s_done, 1)
                elif k == "PV":
                    i, g, t = s["n"], s["g"], s["t"]
                    keys = key_tiles(t)
                    base = pv_steps(i)
                    u = s["m"]
                    m_acquire(u)
                    pe.wait_ge(p_ready, i + 1)
                    if i == 0:
                        upto(pe, b_free, QKV_B - 1)
                        upto(pe, b_free, QKV_B)
                        pe.wait_ge(v_done, TT)
                        pe.wait_ge(l1_in[3], 16)

                    def transposed(kt):
                        q = base + kt
                        if q >= 2:
                            _, _, by, count = PT_TILES[q - 2]
                            pe.wait_ge(pt_ready[by], count)
                        for h in range(4):
                            ins = TR(PS[:, 4 + q % 2, P * h:P * h + P], Z[:, i % 2, h, P * kt:P * kt + P], IDN[:, :])
                        ins.then_inc(pt_mm[q % 2], 1)

                    def values(kt):
                        _, _, by, count = PT_TILES[base + kt]
                        pe.wait_ge(pt_ready[by], count)
                        pt = PT[kt].rearrange("p (a s n) -> p s a n", a=2, s=2)
                        for par in (0, 1):
                            ins = MM(PS[64 * par:64 * par + 64, 6 + u % 2, 0:256], vv(keys[kt])[:, HD * g:HD * g + HD],
                                     pt[:, par, :, :], start=(kt == 0), stop=(kt == len(keys) - 1))
                        return ins

                    transposed(0)
                    for kt in range(1, len(keys)):
                        transposed(kt)
                        values(kt - 1)
                    values(len(keys) - 1).then_inc(m_ready[u % 2], 1)


_W = ["x_prompt", "x_sample", "c", "cache_k", "cache_v", "c_ctx", "w_mod", "b_mod", "norm_mix_post", "norm_ffn_post",
      "w_ffn_in", "w_ffn_out", "w_in_even", "w_out_even", "gmlp_norm", "gmlp_ws", "rg_wa", "rg_wi", "w_qkv", "w_out_odd",
      "attn_sink"]


def shape_constants():
    i = np.arange(P)
    sel = np.zeros((P, 2, P), np.float32)
    for v in (0, 1):
        sel[v::32, v, :] = 1.0
    prev = np.where(i[None, :] >= i[:, None], 0.0, -1e30)
    nxt = np.where(i[None, :] <= i[:, None], 0.0, -1e30)
    zero = np.zeros((P, P))
    mask = np.concatenate([zero, zero, nxt, zero, prev, zero, nxt], 1).astype(np.float32)
    nf, grid = HD // 4, 64
    inv = np.float32(10000.0) ** (-np.arange(nf, dtype=np.float32) / nf)
    pos = np.arange(LAT * P)
    row, col = (pos // grid).astype(np.float32)[:, None] * inv, (pos % grid).astype(np.float32)[:, None] * inv
    cos = np.concatenate([np.cos(row), np.cos(row), np.cos(col), np.cos(col)], 1)
    sin = np.concatenate([-np.sin(row), np.sin(row), -np.sin(col), np.sin(col)], 1)
    rope = np.stack([cos, sin]).reshape(2, LAT, P, HD).transpose(2, 0, 1, 3).reshape(P, -1).astype(np.float32)
    return dict(ident=np.eye(P, dtype=np.float32), sel=sel, mask=mask, rope=np.ascontiguousarray(rope))


def kernel(**inputs):
    import concourse.bacc as bacc
    from concourse.bass_utils import run_bass_kernel_spmd

    arrays = {n: np.ascontiguousarray(inputs[n]) for n in _W}
    arrays.update(shape_constants())
    rows = [inputs[n] for n in ("norm_mix_pre", "norm_ffn_pre", "rg_conv_w", "rg_conv_b", "rg_ba", "rg_bi", "rg_lambda",
                                "state_rglru", "gmlp_bs")]
    arrays["sheet"] = np.ascontiguousarray(np.concatenate([np.asarray(r).reshape(-1, P) for r in rows], 0))
    outs = dict(y_prompt=(1, P, D), y_sample=(1, LAT * P, D), new_state=(1, 1, 2, 512), new_k=(1, 1, P, NKV, HD),
                new_v=(1, 1, P, NKV, HD))
    nc = bacc.Bacc("TRN2", target_bir_lowering=False, num_devices=1)
    A = {n: nc.dram_tensor(f"in_{n}", a.shape, mybir.dt.from_np(a.dtype), kind="ExternalInput").ap() for n, a in arrays.items()}
    for n, shape in outs.items():
        A[n] = nc.dram_tensor(f"out_{n}", shape, mybir.dt.float32, kind="ExternalOutput").ap()
    A["new_state"] = A["new_state"].rearrange("a b d (j p) -> p (a b d j)", p=P)
    A["new_k"], A["new_v"] = A["new_k"][0, 0], A["new_v"][0, 0]
    hybrid_step(nc, A)
    r = run_bass_kernel_spmd(nc, [{f"in_{n}": a for n, a in arrays.items()}], core_ids=[0])
    return tuple(r.results[0][f"out_{n}"] for n in outs)
```
